# Optimizing a Trainium2 kernel written in Bass

```python
import jax, jax.numpy as jnp
from jax import lax
import numpy as np
import math

D_MODEL = 1024
BATCH = 1
SEQ = 256
DEPTH = 2

GRID_W = 64
ROPE_THETA = 10000.0
EPS = 1e-6
Q_BLOCK = 128

MLA_HEADS = 8
MLA_Q_LORA = 256
MLA_KV_LORA = 128
MLA_NOPE = 64
MLA_ROPE = 32
MLA_V = 64
MLA_QK = MLA_NOPE + MLA_ROPE

GQA_HEADS = 8
GQA_KV_HEADS = 2
GQA_HEAD_DIM = 64

POOL_WINDOWS = (2, 4, 8, 16)
POOL_GROUPS = 4
POOL_GROUP = 128
POOL_WIDTH = POOL_GROUPS * POOL_GROUP

N_BRANCH = 3
MLA_OUT = MLA_HEADS * MLA_V
GQA_OUT = GQA_HEADS * GQA_HEAD_DIM

D_FF = 2816
CONV_W = 3

IN_SIZES = (MLA_Q_LORA, MLA_KV_LORA, MLA_ROPE,
            GQA_HEADS * GQA_HEAD_DIM, GQA_KV_HEADS * GQA_HEAD_DIM, GQA_KV_HEADS * GQA_HEAD_DIM,
            POOL_WIDTH, N_BRANCH * D_MODEL)
IN_WIDTH = (MLA_Q_LORA + MLA_KV_LORA + MLA_ROPE
            + (GQA_HEADS + 2 * GQA_KV_HEADS) * GQA_HEAD_DIM
            + POOL_WIDTH + N_BRANCH * D_MODEL)


def rms_norm(x, g):
    xf = x.astype(jnp.float32)
    y = xf * lax.rsqrt(jnp.mean(xf * xf, axis=-1, keepdims=True) + EPS)
    return (y * g.astype(jnp.float32)).astype(x.dtype)

def split_columns(y, sizes):
    out, start = [], 0
    for n in sizes:
        out.append(y[..., start:start + n])
        start += n
    return out

def axial_rope_tables(seq_len, rot_dim):
    rows = seq_len // GRID_W
    row_idx = jnp.repeat(jnp.arange(rows, dtype=jnp.float32), GRID_W)
    col_idx = jnp.tile(jnp.arange(GRID_W, dtype=jnp.float32), rows)
    n_axis = rot_dim // 4
    inv_freq = ROPE_THETA ** (-jnp.arange(n_axis, dtype=jnp.float32) / n_axis)
    ang = jnp.concatenate([row_idx[:, None] * inv_freq, col_idx[:, None] * inv_freq], axis=-1)
    return jnp.cos(ang), jnp.sin(ang)

def apply_rope(x, cos, sin):
    half = x.shape[-1] // 2
    x1, x2 = x[..., :half], x[..., half:]
    c = cos[None, :, None, :].astype(x.dtype)
    s = sin[None, :, None, :].astype(x.dtype)
    return jnp.concatenate([x1 * c - x2 * s, x1 * s + x2 * c], axis=-1)

def block_attention(q, k, v):
    b, s, h, dk = q.shape
    g = k.shape[2]
    rep = h // g
    dv = v.shape[-1]
    scale = dk ** -0.5
    nb = s // Q_BLOCK
    qb = q.reshape(b, nb, Q_BLOCK, g, rep, dk).transpose(1, 0, 2, 3, 4, 5)

    def one_block(qi):
        sc = jnp.einsum('bqgrd,bkgd->bgrqk', qi, k, preferred_element_type=jnp.float32) * scale
        p = jax.nn.softmax(sc, axis=-1).astype(v.dtype)
        return jnp.einsum('bgrqk,bkgv->bqgrv', p, v)

    out = lax.map(one_block, qb)
    return out.transpose(1, 0, 2, 3, 4, 5).reshape(b, s, h, dv)

def mla_branch(c_q, c_kv, k_rope_raw, q_norm_g, w_uq, kv_norm_g, w_ukv, qh_g, kh_g, cos, sin):
    b, s, _ = c_q.shape
    q = (rms_norm(c_q, q_norm_g) @ w_uq).reshape(b, s, MLA_HEADS, MLA_QK)
    kv = (rms_norm(c_kv, kv_norm_g) @ w_ukv).reshape(b, s, MLA_HEADS, MLA_NOPE + MLA_V)
    k_nope, v = kv[..., :MLA_NOPE], kv[..., MLA_NOPE:]
    k_rope = jnp.broadcast_to(k_rope_raw[:, :, None, :], (b, s, MLA_HEADS, MLA_ROPE))
    k = jnp.concatenate([k_nope, k_rope], axis=-1)
    q = rms_norm(q, qh_g)
    k = rms_norm(k, kh_g)
    q = jnp.concatenate([q[..., :MLA_NOPE], apply_rope(q[..., MLA_NOPE:], cos, sin)], axis=-1)
    k = jnp.concatenate([k[..., :MLA_NOPE], apply_rope(k[..., MLA_NOPE:], cos, sin)], axis=-1)
    o = block_attention(q, k, v)
    return o.reshape(b, s, MLA_OUT)

def gqa_branch(q_raw, k_raw, v_raw, qn_g, kn_g, cos, sin):
    b, s, _ = q_raw.shape
    q = q_raw.reshape(b, s, GQA_HEADS, GQA_HEAD_DIM)
    k = k_raw.reshape(b, s, GQA_KV_HEADS, GQA_HEAD_DIM)
    v = v_raw.reshape(b, s, GQA_KV_HEADS, GQA_HEAD_DIM)
    q = apply_rope(rms_norm(q, qn_g), cos, sin)
    k = apply_rope(rms_norm(k, kn_g), cos, sin)
    o = block_attention(q, k, v)
    return o.reshape(b, s, GQA_OUT)

def pool_branch(p, w_pool, pool_scale):
    b, s, _ = p.shape
    pg = p.reshape(b, s, POOL_GROUPS, POOL_GROUP)
    pf = pg.astype(jnp.float32)
    csum = jnp.concatenate([jnp.zeros((b, 1, POOL_GROUPS, POOL_GROUP), jnp.float32),
                            jnp.cumsum(pf, axis=1)], axis=1)
    t = jnp.arange(s)
    means = []
    for gi, w in enumerate(POOL_WINDOWS):
        lo = jnp.clip(t - w // 2, 0, s)
        hi = jnp.clip(t + w - w // 2, 0, s)
        cg = csum[:, :, gi]
        total = jnp.take(cg, hi, axis=1) - jnp.take(cg, lo, axis=1)
        means.append(total / (hi - lo).astype(jnp.float32)[None, :, None])
    pooled = jnp.stack(means, axis=2)
    mixed = (pooled - pf).astype(p.dtype)
    y = jnp.einsum('bsgc,gcd->bsgd', mixed, w_pool).reshape(b, s, POOL_WIDTH)
    return y * pool_scale

def depthwise_conv(u, w, bias):
    c = u.shape[-1]
    y = lax.conv_general_dilated(u, w[:, None, :], window_strides=(1,),
                                 padding=[(CONV_W // 2, CONV_W // 2)],
                                 dimension_numbers=('NWC', 'WIO', 'NWC'),
                                 feature_group_count=c)
    return y + bias

def first_inputs(seed: int = 0) -> dict:
    key = jax.random.key(seed)
    ks = jax.random.split(key, 24)
    f32 = jnp.float32

    def dense(k, shape, fan_in):
        return jax.random.normal(k, shape, f32) * (fan_in ** -0.5)

    def gain(k, shape):
        return 1.0 + 0.1 * jax.random.normal(k, shape, f32)

    L = DEPTH
    conv_center = jnp.zeros((CONV_W, 1), f32).at[CONV_W // 2].set(1.0)
    return {
        'x': jax.random.normal(ks[0], (BATCH, SEQ, D_MODEL), f32),
        'attn_norm_g': gain(ks[1], (L, D_MODEL)),
        'w_in': dense(ks[2], (L, D_MODEL, IN_WIDTH), D_MODEL),
        'mla_q_norm_g': gain(ks[3], (L, MLA_Q_LORA)),
        'mla_w_uq': dense(ks[4], (L, MLA_Q_LORA, MLA_HEADS * MLA_QK), MLA_Q_LORA),
        'mla_kv_norm_g': gain(ks[5], (L, MLA_KV_LORA)),
        'mla_w_ukv': dense(ks[6], (L, MLA_KV_LORA, MLA_HEADS * (MLA_NOPE + MLA_V)), MLA_KV_LORA),
        'mla_q_head_g': gain(ks[7], (L, MLA_QK)),
        'mla_k_head_g': gain(ks[8], (L, MLA_QK)),
        'gqa_q_head_g': gain(ks[9], (L, GQA_HEAD_DIM)),
        'gqa_k_head_g': gain(ks[10], (L, GQA_HEAD_DIM)),
        'pool_w': dense(ks[11], (L, POOL_GROUPS, POOL_GROUP, POOL_GROUP), POOL_GROUP),
        'pool_scale': gain(ks[12], (L, POOL_WIDTH)),
        'w_branch_mla': dense(ks[13], (L, MLA_OUT, D_MODEL), MLA_OUT),
        'w_branch_gqa': dense(ks[14], (L, GQA_OUT, D_MODEL), GQA_OUT),
        'w_branch_pool': dense(ks[15], (L, POOL_WIDTH, D_MODEL), POOL_WIDTH),
        'w_out': dense(ks[16], (L, D_MODEL, D_MODEL), D_MODEL),
        'ffn_norm_g': gain(ks[17], (L, D_MODEL)),
        'ffn_w_up': dense(ks[18], (L, D_MODEL, 2 * D_FF), D_MODEL),
        'ffn_conv_w': conv_center[None] + 0.3 * jax.random.normal(ks[19], (L, CONV_W, 2 * D_FF), f32),
        'ffn_conv_b': 0.01 * jax.random.normal(ks[20], (L, 2 * D_FF), f32),
        'ffn_w_down': dense(ks[21], (L, D_FF, D_MODEL), D_FF),
    }

def first_block(x, attn_norm_g, w_in, mla_q_norm_g, mla_w_uq, mla_kv_norm_g, mla_w_ukv,
              mla_q_head_g, mla_k_head_g, gqa_q_head_g, gqa_k_head_g, pool_w, pool_scale,
              w_branch_mla, w_branch_gqa, w_branch_pool, w_out, ffn_norm_g, ffn_w_up,
              ffn_conv_w, ffn_conv_b, ffn_w_down):
    b, s, d = x.shape
    cos_m, sin_m = axial_rope_tables(s, MLA_ROPE)
    cos_g, sin_g = axial_rope_tables(s, GQA_HEAD_DIM)
    for l in range(DEPTH):
        h = rms_norm(x, attn_norm_g[l])
        proj = h @ w_in[l]
        c_q, c_kv, k_rope, gq, gk, gv, pool_in, gate_logits = split_columns(proj, IN_SIZES)
        o_mla = mla_branch(c_q, c_kv, k_rope, mla_q_norm_g[l], mla_w_uq[l], mla_kv_norm_g[l],
                           mla_w_ukv[l], mla_q_head_g[l], mla_k_head_g[l], cos_m, sin_m)
        o_gqa = gqa_branch(gq, gk, gv, gqa_q_head_g[l], gqa_k_head_g[l], cos_g, sin_g)
        o_pool = pool_branch(pool_in, pool_w[l], pool_scale[l])
        gates = jax.nn.sigmoid(gate_logits.astype(jnp.float32)).astype(x.dtype).reshape(b, s, N_BRANCH, d)
        merged = (gates[:, :, 0] * (o_mla @ w_branch_mla[l])
                  + gates[:, :, 1] * (o_gqa @ w_branch_gqa[l])
                  + gates[:, :, 2] * (o_pool @ w_branch_pool[l]))
        x = x + merged @ w_out[l]
        hf = rms_norm(x, ffn_norm_g[l])
        u = depthwise_conv(hf @ ffn_w_up[l], ffn_conv_w[l], ffn_conv_b[l])
        u_gate, u_val = u[..., :D_FF], u[..., D_FF:]
        x = x + (jax.nn.silu(u_gate) * u_val) @ ffn_w_down[l]
    return x


PLE_DIM = 256
HEAD_DIM = 64
DIFF_HEADS = 4
DSA_HEADS = 8
IDX_HEADS = 8
IDX_DIM = 64
TOPK_MAX = 256
N_GROUPS = 4
EXPERTS_PER_GROUP = 8
TOP_K_IN_GROUP = 2
D_EXPERT = 256
ROPE_THETA_2 = 500000.0
ROT_DIM = HEAD_DIM // 4
LN_EPS = 1e-5
NEG_INF = -1e30
ALPHA = (2 * DEPTH) ** 0.25
BETA = (8 * DEPTH) ** -0.25
DIFF_WIDTH = DIFF_HEADS * 2 * HEAD_DIM
DSA_WIDTH = DSA_HEADS * HEAD_DIM
SPLIT_SIZES = (DIFF_WIDTH, DIFF_WIDTH, DIFF_WIDTH, DSA_WIDTH, DSA_WIDTH, DSA_WIDTH,
               IDX_HEADS * IDX_DIM, IDX_DIM, IDX_HEADS, D_MODEL, D_MODEL)
W_IN_COLS = sum(SPLIT_SIZES)


def layer_norm(x, g, b):
    xf = x.astype(jnp.float32)
    mu = jnp.mean(xf, axis=-1, keepdims=True)
    var = jnp.mean(jnp.square(xf - mu), axis=-1, keepdims=True)
    y = (xf - mu) * lax.rsqrt(var + LN_EPS)
    return (y * g.astype(jnp.float32) + b.astype(jnp.float32)).astype(x.dtype)

def rms_norm_2(x, g):
    xf = x.astype(jnp.float32)
    y = xf * lax.rsqrt(jnp.mean(jnp.square(xf), axis=-1, keepdims=True) + LN_EPS)
    return (y * g.astype(jnp.float32)).astype(x.dtype)

def rope_tables(positions):
    inv_freq = 1.0 / (ROPE_THETA_2 ** (jnp.arange(0, ROT_DIM, 2, dtype=jnp.float32) / ROT_DIM))
    ang = positions.astype(jnp.float32)[..., None] * inv_freq
    return jnp.cos(ang), jnp.sin(ang)

def partial_rope(t, cos, sin):
    half = ROT_DIM // 2
    shp = cos.shape[:2] + (1,) * (t.ndim - 3) + (half,)
    c = cos.reshape(shp).astype(t.dtype)
    s = sin.reshape(shp).astype(t.dtype)
    x1 = t[..., :half]
    x2 = t[..., half:ROT_DIM]
    return jnp.concatenate([x1 * c - x2 * s, x2 * c + x1 * s, t[..., ROT_DIM:]], axis=-1)

def diff_attention(q, k, v, lam):
    B, S, H, _, dk = q.shape
    nb = S // Q_BLOCK
    scale = dk ** -0.5
    qb = q.reshape(B, nb, Q_BLOCK, H, 2, dk).swapaxes(0, 1)
    key_pos = jnp.arange(S)

    def one_block(args):
        q_i, b_i = args
        q_pos = b_i * Q_BLOCK + jnp.arange(Q_BLOCK)
        s = jnp.einsum('bqhcd,bkhcd->bhcqk', q_i, k).astype(jnp.float32) * scale
        s = jnp.where(key_pos[None, :] <= q_pos[:, None], s, NEG_INF)
        pr = jax.nn.softmax(s, axis=-1)
        a = pr[:, :, 0] - lam * pr[:, :, 1]
        return jnp.einsum('bhqk,bkhe->bqhe', a.astype(v.dtype), v)

    o = lax.map(one_block, (qb, jnp.arange(nb)))
    return o.swapaxes(0, 1).reshape(B, S, H, v.shape[-1])

def dsa_attention(q, k, v, q_idx, k_idx, w_idx, topk):
    B, S, H, dh = q.shape
    nb = S // Q_BLOCK
    scale = dh ** -0.5
    to_blocks = lambda t: t.reshape((B, nb, Q_BLOCK) + t.shape[2:]).swapaxes(0, 1)
    key_pos = jnp.arange(S)

    def one_block(args):
        q_b, qi_b, wi_b, b_i = args
        q_pos = b_i * Q_BLOCK + jnp.arange(Q_BLOCK)
        dots = jnp.einsum('bqhd,bsd->bqhs', qi_b, k_idx).astype(jnp.float32) * (IDX_DIM ** -0.5)
        score = jnp.einsum('bqhs,bqh->bqs', jax.nn.relu(dots), wi_b.astype(jnp.float32))
        score = jnp.where(key_pos[None, None, :] <= q_pos[None, :, None], score, NEG_INF)
        _, sel = lax.top_k(score, topk)
        valid = sel <= q_pos[None, :, None]
        kg = jax.vmap(lambda kb, ib: kb[ib])(k, sel)
        vg = jax.vmap(lambda vb, ib: vb[ib])(v, sel)
        s = jnp.einsum('bqhd,bqkhd->bhqk', q_b, kg).astype(jnp.float32) * scale
        s = jnp.where(valid[:, None], s, NEG_INF)
        pr = jax.nn.softmax(s, axis=-1)
        return jnp.einsum('bhqk,bqkhd->bqhd', pr.astype(v.dtype), vg)

    o = lax.map(one_block, (to_blocks(q), to_blocks(q_idx), to_blocks(w_idx), jnp.arange(nb)))
    return o.swapaxes(0, 1).reshape(B, S, H * dh)

def token_mixers(x, cos, sin, w_in, lam_params, subln_g, w_bd, w_bs, w_o, lam_init):
    B, S, _ = x.shape
    h = x @ w_in
    points = [int(c) for c in np.cumsum(SPLIT_SIZES)[:-1]]
    dq, dkk, dv, sq, sk, sv, iq, ik, iw, ga, gb = jnp.split(h, points, axis=-1)

    dq = partial_rope(dq.reshape(B, S, DIFF_HEADS, 2, HEAD_DIM), cos, sin)
    dkk = partial_rope(dkk.reshape(B, S, DIFF_HEADS, 2, HEAD_DIM), cos, sin)
    dv = dv.reshape(B, S, DIFF_HEADS, 2 * HEAD_DIM)
    lp = lam_params.astype(jnp.float32)
    lam = jnp.exp(jnp.sum(lp[0] * lp[1])) - jnp.exp(jnp.sum(lp[2] * lp[3])) + lam_init
    ya = diff_attention(dq, dkk, dv, lam)
    ya = (rms_norm_2(ya, subln_g) * (1.0 - lam_init)).reshape(B, S, DIFF_WIDTH)

    sq = partial_rope(sq.reshape(B, S, DSA_HEADS, HEAD_DIM), cos, sin)
    sk = partial_rope(sk.reshape(B, S, DSA_HEADS, HEAD_DIM), cos, sin)
    sv = sv.reshape(B, S, DSA_HEADS, HEAD_DIM)
    iq = partial_rope(iq.reshape(B, S, IDX_HEADS, IDX_DIM), cos, sin)
    ik = partial_rope(ik, cos, sin)
    iw = iw * (IDX_HEADS ** -0.5)
    topk = min(TOPK_MAX, S // 4)
    yb = dsa_attention(sq, sk, sv, iq, ik, iw, topk)

    merged = jax.nn.sigmoid(ga) * (ya @ w_bd) + jax.nn.sigmoid(gb) * (yb @ w_bs)
    return merged @ w_o

def hierarchical_moe(x, w_rg, b_rg, w_re, b_re, w_g, w_u, w_d):
    B, S, D = x.shape
    xt = x.reshape(-1, D)
    n = xt.shape[0]
    g_prob = jax.nn.softmax((xt @ w_rg).astype(jnp.float32) + b_rg.astype(jnp.float32), axis=-1)
    g_val, g_idx = lax.top_k(g_prob, 1)
    e_logit = ((xt @ w_re).astype(jnp.float32) + b_re.astype(jnp.float32)).reshape(n, N_GROUPS, EXPERTS_PER_GROUP)
    e_logit = jnp.take_along_axis(e_logit, g_idx[:, :, None], axis=1)[:, 0]
    e_prob = jax.nn.softmax(e_logit, axis=-1)
    e_val, e_idx = lax.top_k(e_prob, TOP_K_IN_GROUP)
    e_val = e_val / jnp.sum(e_val, axis=-1, keepdims=True)
    within = jnp.sum(jax.nn.one_hot(e_idx, EXPERTS_PER_GROUP, dtype=jnp.float32) * e_val[..., None], axis=1)
    comb = jax.nn.one_hot(g_idx[:, 0], N_GROUPS, dtype=jnp.float32)[:, :, None] * (g_val * within)[:, None, :]
    y = jnp.zeros_like(xt)
    for g in range(N_GROUPS):
        hg = jax.nn.silu(jnp.einsum('nd,edf->nef', xt, w_g[g])) * jnp.einsum('nd,edf->nef', xt, w_u[g])
        y = y + jnp.einsum('nef,efd->nd', hg * comb[:, g, :, None].astype(hg.dtype), w_d[g])
    return y.reshape(B, S, D)

def second_inputs(seed: int = 0) -> dict:
    key = jax.random.key(seed)
    ks = jax.random.split(key, 24)
    L, D = DEPTH, D_MODEL
    G, E, F = N_GROUPS, EXPERTS_PER_GROUP, D_EXPERT
    nrm = lambda k, shape, scale: jax.random.normal(k, shape, jnp.float32) * scale
    return {
        'x': nrm(ks[0], (BATCH, SEQ, D), 1.0),
        'p': nrm(ks[1], (L, BATCH, SEQ, PLE_DIM), 1.0),
        'positions': jnp.broadcast_to(jnp.arange(SEQ, dtype=jnp.int32), (BATCH, SEQ)),
        'w_in': nrm(ks[2], (L, D, W_IN_COLS), D ** -0.5),
        'diff_lambda': nrm(ks[3], (L, 4, HEAD_DIM), 0.1),
        'diff_subln_g': 1.0 + nrm(ks[4], (L, 2 * HEAD_DIM), 0.01),
        'w_branch_diff': nrm(ks[5], (L, DIFF_WIDTH, D), DIFF_WIDTH ** -0.5),
        'w_branch_dsa': nrm(ks[6], (L, DSA_WIDTH, D), DSA_WIDTH ** -0.5),
        'w_out': nrm(ks[7], (L, D, D), BETA * D ** -0.5),
        'ln1_g': 1.0 + nrm(ks[8], (L, D), 0.01),
        'ln1_b': nrm(ks[9], (L, D), 0.01),
        'w_route_group': nrm(ks[10], (L, D, G), D ** -0.5),
        'b_route_group': nrm(ks[11], (L, G), 0.01),
        'w_route_expert': nrm(ks[12], (L, D, G * E), D ** -0.5),
        'b_route_expert': nrm(ks[13], (L, G * E), 0.01),
        'w_exp_gate': nrm(ks[14], (L, G, E, D, F), D ** -0.5),
        'w_exp_up': nrm(ks[15], (L, G, E, D, F), D ** -0.5),
        'w_exp_down': nrm(ks[16], (L, G, E, F, D), BETA * F ** -0.5),
        'w_ple': nrm(ks[17], (L, PLE_DIM, D), BETA * PLE_DIM ** -0.5),
        'w_ple_gate': nrm(ks[18], (L, D, D), D ** -0.5),
        'ln2_g': 1.0 + nrm(ks[19], (L, D), 0.01),
        'ln2_b': nrm(ks[20], (L, D), 0.01),
    }

def second_block(x, p, positions, w_in, diff_lambda, diff_subln_g, w_branch_diff, w_branch_dsa,
              w_out, ln1_g, ln1_b, w_route_group, b_route_group, w_route_expert, b_route_expert,
              w_exp_gate, w_exp_up, w_exp_down, w_ple, w_ple_gate, ln2_g, ln2_b):
    cos, sin = rope_tables(positions)
    for i in range(DEPTH):
        lam_init = 0.8 - 0.6 * math.exp(-0.3 * i)
        mix = token_mixers(x, cos, sin, w_in[i], diff_lambda[i], diff_subln_g[i],
                           w_branch_diff[i], w_branch_dsa[i], w_out[i], lam_init)
        x = layer_norm(ALPHA * x + mix, ln1_g[i], ln1_b[i])
        ffn = hierarchical_moe(x, w_route_group[i], b_route_group[i], w_route_expert[i],
                               b_route_expert[i], w_exp_gate[i], w_exp_up[i], w_exp_down[i])
        ple = jax.nn.sigmoid(x @ w_ple_gate[i]) * (p[i] @ w_ple[i])
        x = layer_norm(ALPHA * x + ffn + ple, ln2_g[i], ln2_b[i])
    return x


def setup_inputs(seed=0):
    out = dict(first_inputs(seed))
    for name, value in second_inputs(seed + 1).items():
        if name != "x":
            out[name + "_2"] = value
    return out


def reference(
    x, attn_norm_g, w_in, mla_q_norm_g, mla_w_uq, mla_kv_norm_g, mla_w_ukv, mla_q_head_g,
    mla_k_head_g, gqa_q_head_g, gqa_k_head_g, pool_w, pool_scale, w_branch_mla, w_branch_gqa,
    w_branch_pool, w_out, ffn_norm_g, ffn_w_up, ffn_conv_w, ffn_conv_b, ffn_w_down, p_2,
    positions_2, w_in_2, diff_lambda_2, diff_subln_g_2, w_branch_diff_2, w_branch_dsa_2,
    w_out_2, ln1_g_2, ln1_b_2, w_route_group_2, b_route_group_2, w_route_expert_2,
    b_route_expert_2, w_exp_gate_2, w_exp_up_2, w_exp_down_2, w_ple_2, w_ple_gate_2, ln2_g_2,
    ln2_b_2,
):
    x = first_block(
        x, attn_norm_g, w_in, mla_q_norm_g, mla_w_uq, mla_kv_norm_g, mla_w_ukv, mla_q_head_g,
        mla_k_head_g, gqa_q_head_g, gqa_k_head_g, pool_w, pool_scale, w_branch_mla,
        w_branch_gqa, w_branch_pool, w_out, ffn_norm_g, ffn_w_up, ffn_conv_w, ffn_conv_b,
        ffn_w_down,
    )
    return second_block(
        x, p_2, positions_2, w_in_2, diff_lambda_2, diff_subln_g_2, w_branch_diff_2,
        w_branch_dsa_2, w_out_2, ln1_g_2, ln1_b_2, w_route_group_2, b_route_group_2,
        w_route_expert_2, b_route_expert_2, w_exp_gate_2, w_exp_up_2, w_exp_down_2, w_ple_2,
        w_ple_gate_2, ln2_g_2, ln2_b_2,
    )


_drawn_inputs = setup_inputs


def setup_inputs(seed=0):
    import zlib

    import numpy as np

    out = dict(_drawn_inputs(seed))
    spreads = {}
    factors = {'mla_q_norm_g': 2.944,
     'mla_q_head_g': 2.921,
     'mla_k_head_g': 2.713,
     'gqa_q_head_g': 3.018,
     'gqa_k_head_g': 2.96,
     'ffn_conv_b': 2.801,
     'diff_subln_g_2': 8.0,
     'ln1_g_2': 2.866,
     'ln1_b_2': 2.937,
     'b_route_group_2': 8.0,
     'b_route_expert_2': 8.0,
     'ln2_g_2': 3.539,
     'ln2_b_2': 3.038}
    for name, (base, spread) in spreads.items():
        noise = np.random.default_rng([zlib.crc32(name.encode()), seed]).standard_normal(out[name].shape)
        drawn = base * np.exp(spread * noise) if base else spread * noise
        out[name] = __import__('jax').numpy.asarray(drawn.astype(out[name].dtype))
    for name, factor in factors.items():
        out[name] = (out[name] * factor).astype(out[name].dtype)
    return out
```

```python
from contextlib import ExitStack

import numpy as np

import concourse.bass as bass
from concourse import mybir

F32 = mybir.dt.float32
F32R = mybir.dt.float32r
I32 = mybir.dt.int32
ACT = mybir.ActivationFunctionType
ALU = mybir.AluOpType
AX_X = mybir.AxisListType.X

P = 128
S = 256
T = S // P
D = 1024
KD = D // P
DEPTH = 2
EPS = 1e-6
LN_EPS = 1e-5

MLA_H, MLA_QL, MLA_KVL, NOPE, ROPE, MLA_V = 8, 256, 128, 64, 32, 64
MLA_QK = NOPE + ROPE
GQA_H, GQA_KV, HD = 8, 2, 64
POOL_WINDOWS = (2, 4, 8, 16)
POOL_G = 4
D_FF = 2816
FF_STEPS = D_FF // S
LATENT = MLA_QL + MLA_KVL + ROPE
C_GQ = LATENT
C_GK = C_GQ + GQA_H * HD
C_GV = C_GK + GQA_KV * HD
C_POOL = C_GV + GQA_KV * HD
C_GATE = C_POOL + POOL_G * P

DIFF_H, DSA_H, IDX_H = 4, 8, 8
TOPK = 64
ROT = HD // 4
N_G, E_G, D_E = 4, 8, 256
N_E = N_G * E_G
ALPHA = (2 * DEPTH) ** 0.25
NEG = -1e30
PICKED = -3e38
C_DQ, C_DK, C_DV, C_SQ, C_SK, C_SV, C_IQ, C_IK = 0, 512, 1024, 1536, 2048, 2560, 3072, 3584
C_IW = C_IK + HD
C_GA = C_IW + IDX_H
C_ATT = C_GA

RING = 3
CHUNK = 2048
PER_TURN = (1, 1, 2, 2)


def later(value, i, per):
    return value if i is None else i * per + value


class Signals:

    def __init__(self, nc, ctx):
        self.nc, self.ctx, self.made = nc, ctx, {}

    def __getitem__(self, name):
        if name not in self.made:
            self.made[name] = self.ctx.enter_context(self.nc.semaphore(name))
        return self.made[name]

    def span(self):
        nums = [s.num for s in self.made.values()]
        return range(min(nums), max(nums) + 1)


class Chain:

    def __init__(self, eng, done):
        self.eng, self.done, self.n, self.i, self.per = eng, done, 0, None, 0

    def __call__(self, ins):
        self.n += 1
        ins.then_inc(self.done, 1)
        self.eng.wait_ge(self.done, later(self.n, self.i, self.per))

    def enter(self, i, per):
        self.i, self.per, self.n0 = i, per, self.n

    def leave(self, turns):
        assert self.n - self.n0 == self.per, (self.n - self.n0, self.per)
        self.n = self.n0 + self.per * turns
        self.i = None


class Lots:

    def __init__(self, order, filled, drained):
        count = [0] * len(filled)
        self.filled_s, self.drained_s, self.use = filled, drained, {}
        for name, lot in order:
            self.use[name] = (lot, count[lot])
            count[lot] += 1

    def claim(self, pe, name, i=None, per=0):
        self.wait_before(pe, name, i, per)
        return self.use[name][0]

    def filled(self, name):
        return self.filled_s[self.use[name][0]]

    def drained(self, name):
        return self.drained_s[self.use[name][0]]

    def wait_filled(self, eng, name, i=None, per=0):
        lot, n = self.use[name]
        eng.wait_ge(self.filled_s[lot], later(n + 1, i, per))
        return lot

    def wait_before(self, eng, name, i=None, per=0):
        lot, n = self.use[name]
        if n:
            eng.wait_ge(self.drained_s[lot], later(n, i, per))

    def wait_drained(self, eng, name, i=None, per=0):
        lot, n = self.use[name]
        eng.wait_ge(self.drained_s[lot], later(n + 1, i, per))


class Stream:

    def __init__(self, K, L, names, widths, ends, loads):
        self.K, self.L, self.names, self.width, self.ends = K, L, names, widths, ends
        self.at = {n: j for j, n in enumerate(names) if n}
        self.loads = loads
        self.landed, self.ready, self.used, self.before = {}, {}, {}, {}
        slot, last, ready, used = [0] * RING, [None] * RING, 0, 0
        for j, n in enumerate(names):
            if n is None:
                continue
            r = j % RING
            slot[r] += 16 * loads.get(n, 1)
            ready += 1
            self.landed[n], self.ready[n], self.before[n] = slot[r], ready, last[r]
            if n not in ends:
                used += 1
                self.used[n] = used
            last[r] = n
        self.next_hi = self.next_lo = 0

    def slot(self, name):
        return self.at[name] % RING

    def columns(self, name):
        return self.width.get(name, CHUNK)

    def wait_used(self, eng, name, i=None):
        if name in self.ends:
            lot = self.L.use[self.ends[name]][0]
            self.L.wait_filled(eng, self.ends[name], i, PER_TURN[lot])
        else:
            eng.wait_ge(self.K.sig["chunk_used"], later(self.used[name], i, 2))

    def may_load(self, sp, name, i=None):
        if self.before[name]:
            sp.wait_ge(self.K.sig["lo_ready"], later(self.ready[self.before[name]], i, 6))

    def split_hi(self, act, name, i=None):
        K, r, n = self.K, self.slot(name), self.columns(name)
        act.wait_ge(K.landed[r], later(self.landed[name], i, 32))
        if self.before[name]:
            self.wait_used(act, self.before[name], i)
        act.activation(K.hi[:, r, 0:n], K.raw[:, r, 0:n], ACT.Copy).then_inc(K.sig["hi_ready"], 1)

    def split_lo(self, dve, name, i=None):
        K, r, n = self.K, self.slot(name), self.columns(name)
        dve.wait_ge(K.sig["hi_ready"], later(self.ready[name], i, 6))
        dve.tensor_tensor(K.lo[:, r, 0:n], K.raw[:, r, 0:n], K.hi[:, r, 0:n].bitcast(F32),
                          ALU.subtract).then_inc(K.sig["lo_ready"], 1)

    def hi_to(self, act, name, n=0):
        while self.next_hi <= min(self.at[name] + n, len(self.names) - 1):
            if self.names[self.next_hi]:
                self.split_hi(act, self.names[self.next_hi])
            self.next_hi += 1

    def lo_to(self, dve, name, n=0):
        while self.next_lo <= min(self.at[name] + n, len(self.names) - 1):
            if self.names[self.next_lo]:
                self.split_lo(dve, self.names[self.next_lo])
            self.next_lo += 1

    def parts(self, pe, name, i=None):
        K, r = self.K, self.slot(name)
        pe.wait_ge(K.sig["lo_ready"], later(self.ready[name], i, 6))
        return K.hi[:, r, :], K.lo[:, r, :]

    def done(self, last, name):
        if name not in self.ends:
            last.then_inc(self.K.sig["chunk_used"], 1)


def mm3(pe, out, a, b, start, stop):
    pe.matmul(out, a[0], b[0], start=start, stop=False)
    pe.matmul(out, a[0], b[1], start=False, stop=False)
    return pe.matmul(out, a[1], b[0], start=False, stop=stop)


class Core:

    def __init__(self, nc, ctx, A):
        self.nc, self.A = nc, A
        self.sig = Signals(nc, ctx)
        self.base = self.floor = (nc.sbuf_base + 63) // 64 * 64
        self.limit = nc.sbuf_top
        self.raw = self.tile("raw", [P, RING, CHUNK])
        self.hi = self.tile("w_hi", [P, RING, CHUNK], F32R)
        self.lo = self.tile("w_lo", [P, RING, CHUNK], F32R)
        self.x = self.tile("x", [P, T, D])
        self.ident = self.tile("ident", [P, P])
        self.rope = self.tile("rope", [P, T, 96])
        self.stat = self.tile("stat", [P, 256])
        self.floor = self.base
        self.ps = [ctx.enter_context(nc.psum_tensor(f"lot{n}", [P, 2, 512], F32)) for n in range(4)]
        self.landed = [self.sig[f"landed{r}"] for r in range(RING)]
        self.filled = [self.sig[f"filled{n}"] for n in range(4)]
        self.drained = [self.sig[f"drained{n}"] for n in range(4)]

    def tile(self, name, shape, dtype=F32):
        t = self.nc.alloc_sbuf_tensor_at(name, shape, dtype, offset=self.base)
        self.base += (4 * int(np.prod(shape[1:])) + 31) // 32 * 32
        assert self.base <= self.limit, (name, self.base, self.limit)
        return t

    def over(self, name, shape, offset, dtype=F32):
        return self.nc.alloc_sbuf_tensor_at(name, shape, dtype, offset=offset)


def token_product(K, ST, pe, out, xT, name, start, stop, k0, kn, n, tiles=range(T), c0=0, cn=None, i=None):
    w = [v[:, 0:kn * n].rearrange("p (k c) -> p k c", k=kn) for v in ST.parts(pe, name, i)]
    cn = n if cn is None else cn
    for t in tiles:
        for k in range(kn):
            last = mm3(pe, out(t), [v[:, k0 + k, t * P:(t + 1) * P] for v in xT],
                       [v[:, k, c0:c0 + cn] for v in w], start and k == 0, stop and k == kn - 1)
    return last


def project(K, L, ST, pe, name, chunks, n, xT, kn=4):
    lot = L.claim(pe, name)
    for c, chunk in enumerate(chunks):
        last = token_product(K, ST, pe, lambda t: K.ps[lot][:, t, 0:n], xT, chunk, c == 0, c == len(chunks) - 1,
                             c * kn, kn, n)
        ST.done(last, chunk)
    last.then_inc(L.filled(name), 1)


def transpose_x(K, L, pe, src, names):
    for half, name in enumerate(names):
        lot = L.claim(pe, name)
        dst = K.ps[lot][:, :, :].rearrange("p a b -> p (a b)").rearrange("p (k s) -> p k s", k=4)
        for kk in range(4):
            for t in range(T):
                last = pe.transpose(dst[:, kk, t * P:(t + 1) * P],
                                    src[:, t, (4 * half + kk) * P:(4 * half + kk + 1) * P], K.ident[:, :])
        last.then_inc(L.filled(name), 1)


def flat(ap):
    return ap.rearrange("p a b -> p (a b)")


def act_hi(K, L, act, name, dst, src=None):
    lot = L.wait_filled(act, name)
    act.activation(dst, flat(K.ps[lot][:, :, :]) if src is None else src(lot), ACT.Copy)\
       .then_inc(K.sig[f"hi_{name}"], 1)


def dve_lo(K, L, dve, name, dst, hi, src=None):
    lot = L.use[name][0]
    dve.wait_ge(K.sig[f"hi_{name}"], 1)
    dve.tensor_tensor(dst, flat(K.ps[lot][:, :, :]) if src is None else src(lot), hi.bitcast(F32),
                      ALU.subtract).then_inc(L.drained(name), 1)


class Attention:

    def __init__(self, K, L, tag, units, q, k, v, scale, p, pt, mask=None, out=None):
        self.K, self.L, self.tag, self.units = K, L, tag, units
        self.q, self.k, self.v, self.scale, self.mask = q, k, v, scale, mask
        self.p, self.pt, self.out = p, pt, out

    @staticmethod
    def lots(tag, units):
        order = [(f"{tag}S0", 0), (f"{tag}S1", 1)]
        for u in range(units):
            order.append((f"{tag}T{u}", 2))
            if u + 2 < units:
                order.append((f"{tag}S{u + 2}", u % 2))
            order.append((f"{tag}O{u}", 3))
        return order

    def pe(self, pe):
        K, L, tag = self.K, self.L, self.tag

        def scores(u):
            lot = L.claim(pe, f"{tag}S{u}")
            s = flat(K.ps[lot][:, :, :]).rearrange("p (h t k) -> p h t k", h=2, t=T)
            for h in range(2):
                for t in range(T):
                    last = pe.matmul(s[:, h, t, :], self.q(u, h)[:, t * P:(t + 1) * P], self.k(u, h),
                                     start=True, stop=True)
            last.then_inc(L.filled(f"{tag}S{u}"), 1)

        scores(0)
        scores(1)
        for u in range(self.units):
            pe.wait_ge(K.sig[f"{tag}_probs"], u + 1)
            L.claim(pe, f"{tag}T{u}")
            self.pe_turn(pe, u).then_inc(L.filled(f"{tag}T{u}"), 1)
            if u + 2 < self.units:
                scores(u + 2)
            L.wait_drained(pe, f"{tag}T{u}")
            L.claim(pe, f"{tag}O{u}")
            self.pe_out(pe, u).then_inc(L.filled(f"{tag}O{u}"), 1)

    def pe_turn(self, pe, u):
        p = self.p[:, u % 2, :].rearrange("p (h t k) -> p h t k", h=2, t=T)
        d = flat(self.K.ps[2][:, :, :]).rearrange("p (h c q) -> p h c q", h=2, c=T)
        for h in range(2):
            for t in range(T):
                for c in range(T):
                    last = pe.transpose(d[:, h, c, t * P:(t + 1) * P], p[:, h, t, c * P:(c + 1) * P],
                                        self.K.ident[:, :])
        return last

    def pe_out(self, pe, u):
        pt = self.pt[:, :].rearrange("p (h c q) -> p h c q", h=2, c=T)
        for h in range(2):
            for c in range(T):
                last = pe.matmul(self.K.ps[3][h * HD:(h + 1) * HD, 0, 0:S], self.v(u, h, c), pt[:, h, c, :],
                                 start=c == 0, stop=c == T - 1)
        return last

    def turned_size(self):
        return 2 * T * S

    def act_out(self, act, u):
        self.L.wait_filled(act, f"{self.tag}O{u}")
        act.activation(self.out[0][:, u, :], self.K.ps[3][:, 0, 0:S], ACT.Copy)\
           .then_inc(self.K.sig[f"{self.tag}_hi"], 1)

    def dve_out(self, dve, u):
        dve.wait_ge(self.K.sig[f"{self.tag}_hi"], u + 1)
        dve.tensor_tensor(self.out[1][:, u, :], self.K.ps[3][:, 0, 0:S], self.out[0][:, u, :].bitcast(F32),
                          ALU.subtract).then_inc(self.L.drained(f"{self.tag}O{u}"), 1)

    def weigh(self, dve, link, u, inv):
        p = self.p[:, u % 2, :].rearrange("p (n k) -> p n k", n=4)
        return dve.tensor_tensor(p, p, inv.unsqueeze(2).to_broadcast([P, 4, S]), ALU.mult)

    def act(self, act):
        K, L, tag = self.K, self.L, self.tag
        sums = K.stat[:, 200:208].rearrange("p (b n) -> p b n", b=2)
        neg = K.stat[:, 208:216].rearrange("p (b n) -> p b n", b=2)

        def exps(u):
            act.wait_ge(K.sig[f"{tag}_negmax"], u + 1)
            if u >= 2:
                L.wait_filled(act, f"{tag}T{u - 2}")
            lot = L.use[f"{tag}S{u}"][0]
            p = self.p[:, u % 2, :].rearrange("p (n k) -> p n k", n=4)
            s = p if self.mask is not None else flat(K.ps[lot][:, :, :]).rearrange("p (n k) -> p n k", n=4)
            for n in range(4):
                last = act.activation(p[:, n, :], s[:, n, :], ACT.Exp, bias=neg[:, u % 2, n:n + 1],
                                      scale=1.0 if self.mask is not None else self.scale,
                                      accum_out=sums[:, u % 2, n:n + 1])
            last.then_inc(K.sig[f"{tag}_exps"] if self.mask is not None else L.drained(f"{tag}S{u}"), 1)

        def turned(u):
            L.wait_filled(act, f"{tag}T{u}")
            if u:
                L.wait_filled(act, f"{tag}O{u - 1}")
            n = self.turned_size()
            act.activation(self.pt[:, 0:n], flat(K.ps[2][:, :, :])[:, 0:n], ACT.Copy)\
               .then_inc(L.drained(f"{tag}T{u}"), 1)

        exps(0)
        for u in range(self.units):
            if u + 1 < self.units:
                exps(u + 1)
            turned(u)
            if u:
                self.act_out(act, u - 1)
        self.act_out(act, self.units - 1)

    def dve(self, dve, link):
        K, L, tag = self.K, self.L, self.tag
        sums = K.stat[:, 200:208].rearrange("p (b n) -> p b n", b=2)
        neg = K.stat[:, 208:216].rearrange("p (b n) -> p b n", b=2)
        top = K.stat[:, 216:220]
        inv = K.stat[:, 220:224]

        def maxima(u):
            lot = L.wait_filled(dve, f"{tag}S{u}")
            s = flat(K.ps[lot][:, :, :])
            if self.mask is not None:
                if u >= 2:
                    L.wait_filled(dve, f"{tag}T{u - 2}")
                p = self.p[:, u % 2, :]
                dve.scalar_tensor_tensor(p.rearrange("p (h k) -> p h k", h=2), K.ps[lot][:, :, :], self.scale,
                                         self.mask, ALU.mult, ALU.add).then_inc(L.drained(f"{tag}S{u}"), 1)
                L.wait_drained(dve, f"{tag}S{u}")
                s = p
            if u:
                dve.wait_ge(K.sig[f"{tag}_negmax"], u)
            link(dve.tensor_reduce(top, s.rearrange("p (n k) -> p n k", n=4), AX_X, ALU.max))
            dve.tensor_scalar(neg[:, u % 2, :], top, -1.0 if self.mask is not None else -self.scale, None,
                              ALU.mult).then_inc(K.sig[f"{tag}_negmax"], 1)

        def normalise(u):
            if self.mask is not None:
                dve.wait_ge(K.sig[f"{tag}_exps"], u + 1)
            else:
                L.wait_drained(dve, f"{tag}S{u}")
            if u:
                dve.wait_ge(K.sig[f"{tag}_probs"], u)
            link(dve.reciprocal(inv, sums[:, u % 2, :]))
            self.weigh(dve, link, u, inv).then_inc(K.sig[f"{tag}_probs"], 1)

        maxima(0)
        for u in range(self.units):
            if u + 1 < self.units:
                maxima(u + 1)
            normalise(u)
            if u:
                self.dve_out(dve, u - 1)
        self.dve_out(dve, self.units - 1)



def ffn_chunks(steps):
    names = ["G0", "U0", None]
    for e in range(1, steps):
        names += [f"G{e}", f"U{e}", f"D{e - 1}"]
    return names + [f"D{steps - 1}"]


def ffn_ends(steps):
    return {f"U{e}": f"H{e}" for e in range(steps)} | {f"D{e}": f"Y{e}t1" for e in range(steps)}


def ffn_lots(steps):
    order = [("H0", 0)]
    for e in range(1, steps):
        order += [(f"H{e}", e % 2), (f"Y{e - 1}t0", 2), (f"Y{e - 1}t1", 3)]
    return order + [(f"Y{steps - 1}t0", 2), (f"Y{steps - 1}t1", 3)]


def ffn_walk(eng, steps, step, enter=None, leave=None):
    turns = (steps - 3) // 2
    step(0, None)
    with eng.Fori(0, turns) as i:
        if enter:
            enter(i)
        step(1, i)
        step(2, i)
    if leave:
        leave(turns)
    for e in range(1 + 2 * turns, steps - 1):
        step(e, None)


def true_step(e, i):
    return e if i is None else 2 * i + e


def ffn_load(K, ST, sp, steps, source):
    def load(name, i=None):
        ST.may_load(sp, name, i)
        e = true_step(int(name[1:]), i)
        sp.dma_start(K.raw[:, ST.slot(name), :].rearrange("p (k c) -> p k c", k=T if name[0] == "D" else KD),
                     source(name[0], e)).then_inc(K.landed[ST.slot(name)], 16)

    load("G0")
    load("U0")

    def step(e, i):
        load(f"G{e + 1}", i)
        load(f"U{e + 1}", i)
        load(f"D{e}", i)

    ffn_walk(sp, steps, step)
    load(f"D{steps - 1}")


def ffn_pe(K, L, ST, pe, steps, xT, h):
    def hidden(e, i=None):
        lot = L.claim(pe, f"H{e}", i, 1)
        for bank, name in enumerate((f"G{e}", f"U{e}")):
            w = [v[:, 0:CHUNK].rearrange("p (k c) -> p k c", k=KD) for v in ST.parts(pe, name, i)]
            for f in range(2):
                for k in range(KD):
                    last = mm3(pe, K.ps[lot][:, bank, f * S:(f + 1) * S], [v[:, k, f * P:(f + 1) * P] for v in w],
                               [v[:, k, :] for v in xT], k == 0, k == KD - 1)
            ST.done(last, name)
        last.then_inc(L.filled(f"H{e}"), 1)

    def down(e, i=None):
        pe.wait_ge(K.sig["h_lo"], later(e + 1, i, 2))
        for t in range(T):
            lot = L.claim(pe, f"Y{e}t{t}", i, 2)
            w = [v[:, 0:CHUNK].rearrange("p (k c) -> p k c", k=T) for v in ST.parts(pe, f"D{e}", i)]
            for n in range(2):
                for k in range(T):
                    last = mm3(pe, K.ps[lot][:, n, :], [v[:, e % 2, k, t * P:(t + 1) * P] for v in h],
                               [v[:, k, n * 512:(n + 1) * 512] for v in w], k == 0, k == T - 1)
            last.then_inc(L.filled(f"Y{e}t{t}"), 1)

    hidden(0)

    def step(e, i):
        hidden(e + 1, i)
        down(e, i)

    ffn_walk(pe, steps, step)
    down(steps - 1)


def ffn_act(K, L, ST, act, steps, first, second, wait_full, h_hi):
    def high(e, i):
        wait_full(e, i)
        act.activation(h_hi[:, e % 2, :, :], K.h[:, :, :], ACT.Copy).then_inc(K.sig["h_hi"], 1)

    def step(e, i):
        first(e, i)
        ST.split_hi(act, f"U{e + 1}", i)
        second(e, i)
        ST.split_hi(act, f"D{e}", i)
        high(e, i)
        if e + 2 < steps:
            ST.split_hi(act, f"G{e + 2}", i)

    ffn_walk(act, steps, step)
    e = steps - 1
    first(e, None)
    second(e, None)
    ST.split_hi(act, f"D{e}")
    high(e, None)


def ffn_dve(K, L, ST, dve, steps, first, second, add, h, enter, leave):
    def low(e, i):
        dve.wait_ge(K.sig["h_hi"], later(e + 1, i, 2))
        dve.tensor_tensor(h[1][:, e % 2, :, :], K.h[:, :, :], h[0][:, e % 2, :, :].bitcast(F32), ALU.subtract)\
           .then_inc(K.sig["h_lo"], 1)

    def sums(e, i):
        for t in range(T):
            L.wait_filled(dve, f"Y{e}t{t}", i, 2)
            L.wait_before(dve, f"Y{e}t{t}", i, 2)
            add(e, i, t).then_inc(L.drained(f"Y{e}t{t}"), 1)

    def step(e, i):
        first(e, i)
        ST.split_lo(dve, f"U{e + 1}", i)
        second(e, i)
        if e > 0:
            sums(e - 1, i)
        ST.split_lo(dve, f"D{e}", i)
        low(e, i)
        if e + 2 < steps:
            ST.split_lo(dve, f"G{e + 2}", i)

    ffn_walk(dve, steps, step, enter, leave)
    e = steps - 1
    first(e, None)
    second(e, None)
    sums(e - 1, None)
    ST.split_lo(dve, f"D{e}")
    low(e, None)
    sums(e, None)
    for t in range(T):
        L.wait_drained(dve, f"Y{e}t{t}")



ONE_CHUNKS = ["lat0", "lat1", "gkv", "gq0", "gq1", "pool0", "pool1", "g0a", "g0b", "g1a", "g1b", "uq", "ukv",
              "g2a", "g2b", "g3a", "g3b", "window", "g4a", "g4b", "pool_w", "g5a", "g5b",
              "bp0", "bp1", "bg0", "bg1", "bm0", "bm1", "wo00", "wo01", "wo10", "wo11"]
ONE_WIDTHS = {"lat0": 4 * LATENT, "lat1": 4 * LATENT, "uq": 2 * MLA_H * MLA_QK, "ukv": MLA_H * (NOPE + MLA_V),
              "pool_w": POOL_G * P}
ONE_ENDS = {"lat1": "lat", "gkv": "gkv", "gq1": "gq", "pool1": "pool", "uq": "q1", "ukv": "kv1", "window": "mix",
            "pool_w": "py", "wo01": "wo0", "wo11": "wo1"}
ONE_ENDS |= {f"g{g}b": f"g{g}" for g in range(6)} | {f"b{b}{c}": f"b{b}{c}" for b in "pgm" for c in range(2)}


def rms_act(K, act, tag, junk):
    for t in range(T):
        last = act.activation(junk[:, t, :], K.x[:, t, :], ACT.Square, accum_out=K.stat[:, t:t + 1])
    last.then_inc(K.sig[f"{tag}_squares"], 1)
    act.wait_ge(K.sig[f"{tag}_var"], 1)
    act.activation(K.stat[:, 2:4], K.stat[:, 2:4], ACT.Sqrt).then_inc(K.sig[f"{tag}_root"], 1)


def rms_dve(K, dve, link, tag, out, gain):
    st = K.stat
    dve.wait_ge(K.sig[f"{tag}_squares"], 1)
    dve.tensor_scalar(st[:, 2:4], st[:, 0:2], 1.0 / D, EPS, ALU.mult, ALU.add).then_inc(K.sig[f"{tag}_var"], 1)
    dve.wait_ge(K.sig[f"{tag}_root"], 1)
    link(dve.reciprocal(st[:, 0:2], st[:, 2:4]))
    dve.wait_ge(K.sig[f"{tag}_gain"], 16)
    for t in range(T):
        last = dve.scalar_tensor_tensor(out[:, t, :], K.x[:, t, :], st[:, t:t + 1], gain[:, :],
                                        ALU.mult, ALU.mult)
    last.then_inc(K.sig[f"{tag}_normed"], 1)


def heads(ap, h):
    return ap.rearrange("p t (h d) -> p t h d", h=h)


def over_heads(ap, h, d):
    if len(ap.shape) == 3:
        return ap.unsqueeze(3).to_broadcast([P, T, h, d])
    return ap.unsqueeze(1).unsqueeze(1).to_broadcast([P, T, h, d])


def rotate(dve, link, x, half, cos, sin, tmp, h):
    x1, x2 = x[:, :, :, 0:half], x[:, :, :, half:2 * half]
    c = cos.unsqueeze(2).to_broadcast([P, T, h, half])
    s = sin.unsqueeze(2).to_broadcast([P, T, h, half])
    n = T * h * half
    t = [tmp[:, i * n:(i + 1) * n].rearrange("p (t h d) -> p t h d", t=T, h=h) for i in range(2)]
    dve.tensor_tensor(t[0], x1, s, ALU.mult)
    link(dve.tensor_tensor(t[1], x2, s, ALU.mult))
    dve.tensor_tensor(x1, x1, c, ALU.mult)
    link(dve.tensor_tensor(x2, x2, c, ALU.mult))
    dve.tensor_tensor(x1, x1, t[1], ALU.subtract)
    return dve.tensor_tensor(x2, x2, t[0], ALU.add)


class OneTiles:

    def __init__(self, K):
        K.base = K.floor
        o = {}

        def tile(name, shape, dtype=F32):
            o[name] = K.base
            return K.tile("one_" + name, shape, dtype)

        def over(name, shape, at, dtype=F32, off=0):
            return K.over("one_" + name, shape, o[at] + off, dtype)

        KB = 1024
        self.hT_hi = tile("hT_hi", [P, KD, S], F32R)
        self.hT_lo = tile("hT_lo", [P, KD, S], F32R)
        self.gT_hi = over("gT_hi", [P, 4, S], "hT_hi", F32R)
        self.gT_lo = over("gT_lo", [P, 4, S], "hT_hi", F32R, 4 * KB)
        self.mT_hi = over("mT_hi", [P, 4, S], "hT_lo", F32R)
        self.mT_lo = over("mT_lo", [P, 4, S], "hT_lo", F32R, 4 * KB)
        self.gates = tile("gates", [P, T, 3 * D])
        self.gain = over("gain", [P, D], "gates")
        self.lat = tile("lat", [P, T, C_POOL])
        self.q = tile("q", [P, T, MLA_H * MLA_QK])
        self.kv = tile("kv", [P, T, MLA_H * (NOPE + MLA_V)])
        self.k = tile("k", [P, T, MLA_H * MLA_QK])
        self.mqT = tile("mqT", [P, MLA_H, S])
        self.mkT = tile("mkT", [P, MLA_H, S])
        self.gqT = tile("gqT", [P, GQA_H // 2, S])
        self.gkT = tile("gkT", [P, GQA_KV, S])
        self.mixT_hi = over("mixT_hi", [P, POOL_G, S], "mqT", F32R)
        self.mixT_lo = over("mixT_lo", [P, POOL_G, S], "mkT", F32R)
        self.tmp = tile("tmp", [P, T, D])
        self.scratch = over("scratch", [P, 1536], "tmp")
        self.k2 = over("k2", [P, T, 4 * HD], "tmp", off=6 * KB)
        self.oTp_hi = tile("oTp_hi", [P, 4, S], F32R)
        self.oTp_lo = tile("oTp_lo", [P, 4, S], F32R)
        self.cT_hi = over("cT_hi", [P, 3, S], "oTp_hi", F32R)
        self.cT_lo = over("cT_lo", [P, 3, S], "oTp_lo", F32R)
        self.p = tile("p", [P, 2, D])
        self.p_hi = over("p_hi", [P, T, 512], "p", F32R)
        self.p_lo = over("p_lo", [P, T, 512], "p", F32R, 4 * KB)
        self.h_hi = over("h_hi", [P, 2, 2, S], "p", F32R)
        self.h_lo = over("h_lo", [P, 2, 2, S], "p", F32R, 4 * KB)
        self.pt = tile("pt", [P, D])
        self.colrows = over("colrows", [P, 2, P], "pt")
        self.conv = over("conv", [P, 2, 2, S], "tmp")
        self.rows = tile("rows", [P, 704])
        self.cols = tile("cols", [P, 2, 92])


def block_one(K, M, layer):
    nc, A, sig, st = K.nc, K.A, K.sig, K.stat
    names = ONE_CHUNKS + ffn_chunks(FF_STEPS)
    order = [("xT0", 0), ("xT1", 1), ("lat", 2), ("gkv", 3), ("gq", 0), ("pool", 1), ("cols", 2), ("g0", 3),
             ("g1", 0), ("cT", 1), ("q0", 2), ("q1", 3), ("kv0", 0), ("kv1", 1), ("g2", 2), ("g3", 3), ("mix", 0),
             ("g4", 1), ("py", 2), ("g5", 3), ("gqT", 0), ("gkT", 1)]
    order += Attention.lots("ga", GQA_H // 2)
    order += [("bp0", 2), ("bp1", 0), ("mqT0", 1), ("mqT1", 2), ("mkT0", 3), ("mkT1", 0)]
    order += Attention.lots("ma", MLA_H // 2)
    order += [("bg0", 2), ("bg1", 0), ("bm0", 1), ("bm1", 2), ("mT0", 3), ("mT1", 0), ("wo0", 1), ("wo1", 2),
              ("fT0", 3), ("fT1", 0)]
    order += ffn_lots(FF_STEPS)
    L = Lots(order, K.filled, K.drained)
    ST = Stream(K, L, names, ONE_WIDTHS, ONE_ENDS | ffn_ends(FF_STEPS), {})
    K.h = M.conv[:, 1, :, :]
    hT = (M.hT_hi, M.hT_lo)
    group = GQA_H // GQA_KV
    ga = Attention(K, L, "ga", GQA_H // 2,
                   q=lambda u, h: M.gqT[h * HD:(h + 1) * HD, u, :],
                   k=lambda u, h: M.gkT[h * HD:(h + 1) * HD, (2 * u + h) // group, :],
                   v=lambda u, h, c: M.lat[:, c, C_GV + (2 * u + h) // group * HD:
                                           C_GV + ((2 * u + h) // group + 1) * HD],
                   scale=HD ** -0.5, p=M.p, pt=M.pt, out=(M.gT_hi, M.gT_lo))
    ma = Attention(K, L, "ma", MLA_H // 2,
                   q=lambda u, h: M.mqT[0:MLA_QK, 2 * u + h, :],
                   k=lambda u, h: M.mkT[0:MLA_QK, 2 * u + h, :],
                   v=lambda u, h, c: M.kv[:, c, (2 * u + h) * 2 * HD + NOPE:(2 * u + h + 1) * 2 * HD],
                   scale=MLA_QK ** -0.5, p=M.p, pt=M.pt, out=(M.mT_hi, M.mT_lo))
    merged = M.tmp

    def source(name):
        w = A["w_in"][layer]
        kpc = lambda a: a.rearrange("(k p) c -> p k c", p=P)
        half = lambda c0, c1, k: kpc(w[k * 512:(k + 1) * 512, c0:c1])
        if name in ("lat0", "lat1"):
            return half(0, LATENT, int(name[-1]))
        if name == "gkv":
            return kpc(w[:, C_GK:C_POOL])
        if name in ("gq0", "gq1"):
            return half(C_GQ, C_GK, int(name[-1]))
        if name in ("pool0", "pool1"):
            return half(C_POOL, C_GATE, int(name[-1]))
        if name == "uq":
            return kpc(A["mla_w_uq"][layer])
        if name == "ukv":
            return kpc(A["mla_w_ukv"][layer])
        if name == "window":
            return A["c_window"]
        if name == "pool_w":
            return A["pool_w"][layer].rearrange("g c d -> c g d")
        if name[:2] == "wo":
            c, k = int(name[2]), int(name[3])
            return kpc(A["w_out"][layer][k * 512:(k + 1) * 512, c * 512:(c + 1) * 512])
        if name[0] == "b":
            b = {"p": "w_branch_pool", "g": "w_branch_gqa", "m": "w_branch_mla"}[name[1]]
            c = int(name[2])
            return kpc(A[b][layer][:, c * 512:(c + 1) * 512])
        c = C_GATE + 512 * int(name[1])
        return half(c, c + 512, "ab".index(name[2]))

    def ff_source(kind, e):
        if kind == "D":
            return A["ffn_w_down"][layer][bass.ds(e * S, S), :].rearrange("(k p) c -> p k c", p=P)
        return A["ffn_w_up"][layer][:, bass.ds(e * S + (D_FF if kind == "U" else 0), S)]\
            .rearrange("(k p) c -> p k c", p=P)

    with nc.Block() as block:

        @block.sync
        def _(sp):
            sp.dma_start(M.gain[:, :], A["attn_norm_g"][layer].partition_broadcast(P)).then_inc(sig["n1_gain"], 16)
            for name in ONE_CHUNKS:
                ST.may_load(sp, name)
                src = source(name)
                sp.dma_start(K.raw[:, ST.slot(name), 0:ST.columns(name)].rearrange("p (k c) -> p k c", k=src.shape[1]),
                             src).then_inc(K.landed[ST.slot(name)], 16)
                if name == "gkv":
                    c = 0
                    for g, n in (("mla_q_norm_g", MLA_QL), ("mla_kv_norm_g", MLA_KVL), ("mla_q_head_g", MLA_QK),
                                 ("mla_k_head_g", MLA_QK), ("gqa_q_head_g", HD), ("gqa_k_head_g", HD)):
                        sp.dma_start(M.rows[:, c:c + n], A[g][layer].partition_broadcast(P))\
                          .then_inc(sig["rows"], 16)
                        c += n
                    for r0, r1, c, src in ((0, 44, 0, A["ffn_conv_w"][layer][0]), (44, 88, 0, A["ffn_conv_w"][layer][1]),
                                           (88, 92, 0, A["pool_scale"][layer]), (0, 44, 1, A["ffn_conv_w"][layer][2]),
                                           (44, 88, 1, A["ffn_conv_b"][layer])):
                        sp.dma_start(M.colrows[r0:r1, c, :], src.rearrange("(r p) -> r p", p=P))\
                          .then_inc(sig["colrows"], 16)
            sp.wait_ge(sig["merged"], 1)
            sp.dma_start(M.gain[:, :], A["ffn_norm_g"][layer].partition_broadcast(P)).then_inc(sig["n2_gain"], 16)
            ffn_load(K, ST, sp, FF_STEPS, ff_source)

        @block.tensor
        def _(pe):
            pe.wait_ge(sig["n1_normed"], 1)
            transpose_x(K, L, pe, M.tmp, ("xT0", "xT1"))
            for n in ("xT0", "xT1"):
                L.wait_drained(pe, n)
            project(K, L, ST, pe, "lat", ("lat0", "lat1"), LATENT, hT)
            project(K, L, ST, pe, "gkv", ("gkv",), 2 * GQA_KV * HD, hT, kn=KD)
            project(K, L, ST, pe, "gq", ("gq0", "gq1"), 512, hT)
            project(K, L, ST, pe, "pool", ("pool0", "pool1"), 512, hT)
            pe.wait_ge(sig["colrows"], 80)
            lot = L.claim(pe, "cols")
            pe.transpose(K.ps[lot][:, 0, 0:92], M.colrows[0:92, 0, :], K.ident[0:92, 0:92])
            pe.transpose(K.ps[lot][:, 1, 0:88], M.colrows[0:88, 1, :], K.ident[0:88, 0:88])\
              .then_inc(L.filled("cols"), 1)
            for g in range(2):
                project(K, L, ST, pe, f"g{g}", (f"g{g}a", f"g{g}b"), 512, hT)
            pe.wait_ge(sig["lat_normed"], 1)
            lot = L.claim(pe, "cT")
            d = flat(K.ps[lot][:, :, :]).rearrange("p (k s) -> p k s", k=4)
            for k in range(3):
                for t in range(T):
                    last = pe.transpose(d[:, k, t * P:(t + 1) * P], M.lat[:, t, k * P:(k + 1) * P], K.ident[:, :])
            last.then_inc(L.filled("cT"), 1)
            L.wait_drained(pe, "cT")
            cT = (M.cT_hi, M.cT_lo)
            for name, chunk, n, k0, kn in (("q", "uq", MLA_H * MLA_QK, 0, 2), ("kv", "ukv", MLA_H * 2 * HD, 2, 1)):
                for t in range(T):
                    lot = L.claim(pe, f"{name}{t}")
                    for bank in range(2):
                        c0, cn = bank * 512, min(512, n - bank * 512)
                        last = token_product(K, ST, pe, lambda t: K.ps[lot][:, bank, 0:cn], cT, chunk, True, True,
                                             k0, kn, n, tiles=(t,), c0=c0, cn=cn)
                    last.then_inc(L.filled(f"{name}{t}"), 1)
            for g in range(2, 4):
                project(K, L, ST, pe, f"g{g}", (f"g{g}a", f"g{g}b"), 512, hT)
            L.wait_drained(pe, "pool")
            lot = L.claim(pe, "mix")
            w = [v[:, :].rearrange("p (k g s) -> p k g s", k=T, g=POOL_G) for v in ST.parts(pe, "window")]
            d = flat(K.ps[lot][:, :, :]).rearrange("p (g s) -> p g s", g=POOL_G)
            for g in range(POOL_G):
                for k in range(T):
                    last = mm3(pe, d[:, g, :], [v[:, k, g * P:(g + 1) * P] for v in (M.p_hi, M.p_lo)],
                               [v[:, k, g, :] for v in w], k == 0, k == T - 1)
            last.then_inc(L.filled("mix"), 1)
            project(K, L, ST, pe, "g4", ("g4a", "g4b"), 512, hT)
            L.wait_drained(pe, "mix")
            lot = L.claim(pe, "py")
            w = [v[:, 0:POOL_G * P].rearrange("p (g c) -> p g c", g=POOL_G) for v in ST.parts(pe, "pool_w")]
            d = flat(K.ps[lot][:, :, :]).rearrange("p (g s) -> p g s", g=POOL_G)
            for g in range(POOL_G):
                last = mm3(pe, d[:, g, :], [v[:, g, :] for v in w], [v[:, g, :] for v in (M.mixT_hi, M.mixT_lo)],
                           True, True)
            last.then_inc(L.filled("py"), 1)
            project(K, L, ST, pe, "g5", ("g5a", "g5b"), 512, hT)
            pe.wait_ge(sig["gqa_ready"], 1)
            for name, src, pairs in (("gqT", M.lat[:, :, C_GQ:C_GK], 4), ("gkT", M.k2[:, :, :], 2)):
                lot = L.claim(pe, name)
                d = flat(K.ps[lot][:, :, :]).rearrange("p (k s) -> p k s", k=4)
                for k in range(pairs):
                    for t in range(T):
                        last = pe.transpose(d[:, k, t * P:(t + 1) * P], src[:, t, k * P:(k + 1) * P], K.ident[:, :])
                last.then_inc(L.filled(name), 1)
            L.wait_drained(pe, "gqT")
            L.wait_drained(pe, "gkT")
            ga.pe(pe)

            def branch(name, xT):
                for c in range(2):
                    lot = L.claim(pe, f"{name}{c}")
                    token_product(K, ST, pe, lambda t: K.ps[lot][:, t, :], xT, f"{name}{c}", True, True, 0, 4, 512)\
                        .then_inc(L.filled(f"{name}{c}"), 1)

            branch("bp", (M.oTp_hi, M.oTp_lo))
            pe.wait_ge(sig["mla_ready"], 1)
            for name, src in (("mqT", M.q), ("mkT", M.k)):
                for half in range(2):
                    lot = L.claim(pe, f"{name}{half}")
                    d = flat(K.ps[lot][:, :, :]).rearrange("p (k s) -> p k s", k=4)
                    for k in range(4):
                        for t in range(T):
                            h = 4 * half + k
                            last = pe.transpose(d[0:MLA_QK, k, t * P:(t + 1) * P],
                                                src[:, t, h * MLA_QK:(h + 1) * MLA_QK], K.ident[:, :])
                    last.then_inc(L.filled(f"{name}{half}"), 1)
            for n in ("mqT0", "mqT1", "mkT0", "mkT1"):
                L.wait_drained(pe, n)
            ma.pe(pe)
            L.wait_drained(pe, "gaO3")
            branch("bg", (M.gT_hi, M.gT_lo))
            L.wait_drained(pe, "maO3")
            branch("bm", (M.mT_hi, M.mT_lo))
            pe.wait_ge(sig["merged"], 1)
            transpose_x(K, L, pe, merged, ("mT0", "mT1"))
            for n in ("mT0", "mT1"):
                L.wait_drained(pe, n)
            for c in range(2):
                project(K, L, ST, pe, f"wo{c}", (f"wo{c}0", f"wo{c}1"), 512, hT)
            pe.wait_ge(sig["n2_normed"], 1)
            transpose_x(K, L, pe, M.tmp, ("fT0", "fT1"))
            for n in ("fT0", "fT1"):
                L.wait_drained(pe, n)
            ffn_pe(K, L, ST, pe, FF_STEPS, hT, (M.h_hi, M.h_lo))

        @block.scalar
        def _(act):
            def sigmoid(g):
                lot = L.wait_filled(act, f"g{g}")
                act.activation(M.gates[:, :, g * 512:(g + 1) * 512], K.ps[lot][:, :, :], ACT.Sigmoid)\
                   .then_inc(L.drained(f"g{g}"), 1)

            def root(name, cols):
                act.wait_ge(sig[f"{name}_var"], 1)
                act.activation(st[:, cols], st[:, cols], ACT.Sqrt).then_inc(sig[f"{name}_root"], 1)

            def take(name, dst, part=None, rows=P):
                lot = L.wait_filled(act, name)
                src = flat(K.ps[lot][:, :, :])[0:rows, :] if part is None else part(K.ps[lot])
                act.activation(dst, src, ACT.Copy).then_inc(L.drained(name), 1)

            rms_act(K, act, "n1", M.tmp)
            ST.hi_to(act, "lat0", 2)
            act_hi(K, L, act, "xT0", flat(M.hT_hi[:, 0:4, :]))
            act_hi(K, L, act, "xT1", flat(M.hT_hi[:, 4:8, :]))
            ST.hi_to(act, "gkv", 2)
            L.wait_drained(act, "lat")
            for t in range(T):
                act.activation(M.q[:, t, 0:MLA_QL], M.lat[:, t, 0:MLA_QL], ACT.Square,
                               accum_out=st[:, 4 + t:5 + t])
                last = act.activation(M.q[:, t, MLA_QL:MLA_QL + MLA_KVL], M.lat[:, t, MLA_QL:MLA_QL + MLA_KVL], ACT.Square,
                                      accum_out=st[:, 6 + t:7 + t])
            last.then_inc(sig["lat_squares"], 1)
            ST.hi_to(act, "gq1", 2)
            take("gq", M.lat[:, :, C_GQ:C_GK], lambda ps: ps[:, :, :])
            root("lat", slice(8, 12))
            ST.hi_to(act, "pool1", 2)
            act_hi(K, L, act, "pool", flat(M.p_hi[:, :, :]))
            ST.hi_to(act, "g0b", 1)
            root("gqa", slice(16, 36))
            ST.hi_to(act, "g0b", 2)
            sigmoid(0)
            ST.hi_to(act, "g1b", 2)
            sigmoid(1)
            act_hi(K, L, act, "cT", flat(M.cT_hi[:, :, :]), lambda lot: flat(K.ps[lot][:, :, :])[:, 0:3 * S])
            ST.hi_to(act, "uq", 2)
            n = MLA_H * MLA_QK
            for t in range(T):
                take(f"q{t}", M.q[:, t, :], lambda ps: flat(ps[:, :, :])[:, 0:n])
            ST.hi_to(act, "g2b", 2)
            sigmoid(2)
            ST.hi_to(act, "g3b", 2)
            sigmoid(3)
            ST.hi_to(act, "window", 2)
            act_hi(K, L, act, "mix", flat(M.mixT_hi[:, :, :]))
            root("mla", slice(80, 112))
            ST.hi_to(act, "g4b", 2)
            sigmoid(4)
            ST.hi_to(act, "pool_w", 2)
            L.wait_drained(act, "cols")
            lot = L.wait_filled(act, "py")
            for g in range(POOL_G):
                last = act.activation(M.oTp_hi[:, g, :], flat(K.ps[lot][:, :, :])[:, g * S:(g + 1) * S], ACT.Copy,
                                      scale=M.cols[:, 0, 88 + g:89 + g])
            last.then_inc(sig["hi_py"], 1)
            ST.hi_to(act, "g5b", 2)
            sigmoid(5)
            ST.hi_to(act, "g5b", 3)
            take("gqT", flat(M.gqT[:, :, :]))
            ga.act(act)
            ST.hi_to(act, "bp1", 2)
            for half in range(2):
                take(f"mqT{half}", flat(M.mqT[0:MLA_QK, 4 * half:4 * half + 4, :]), rows=MLA_QK)
            ma.act(act)
            ST.hi_to(act, "wo01")
            act_hi(K, L, act, "mT0", flat(M.hT_hi[:, 0:4, :]))
            act_hi(K, L, act, "mT1", flat(M.hT_hi[:, 4:8, :]))
            ST.hi_to(act, "wo11")
            ST.hi_to(act, "U0")
            L.wait_drained(act, "wo1")
            rms_act(K, act, "n2", M.tmp)
            act_hi(K, L, act, "fT0", flat(M.hT_hi[:, 0:4, :]))
            act_hi(K, L, act, "fT1", flat(M.hT_hi[:, 4:8, :]))
            ST.hi_to(act, "G1")

            def middle_tap(e, i):
                if e or i is not None:
                    act.wait_ge(sig["h_lo"], later(e, i, 2))
                lot = L.wait_filled(act, f"H{e}", i, 1)
                for b in range(2):
                    for f in range(2):
                        at = 22 * b + f + 2 * true_step(e, i)
                        last = act.activation(M.conv[:, b, f, :], K.ps[lot][:, b, f * S:(f + 1) * S], ACT.Identity,
                                              scale=M.cols[:, 0, bass.ds(44 + at, 1)],
                                              bias=M.cols[:, 1, bass.ds(44 + at, 1)])
                last.then_inc(sig["middle"], 1)

            def silu(e, i):
                L.wait_drained(act, f"H{e}", i, 1)
                act.activation(M.conv[:, 0, :, :], M.conv[:, 0, :, :], ACT.Silu).then_inc(sig["silu"], 1)

            ffn_act(K, L, ST, act, FF_STEPS, middle_tap, silu,
                    lambda e, i: act.wait_ge(sig["h_full"], later(e + 1, i, 2)), M.h_hi)

        @block.vector
        def _(dve):
            link = Chain(dve, sig["dve_chain"])

            def take(name, dst, part=None, rows=P):
                lot = L.wait_filled(dve, name)
                src = flat(K.ps[lot][:, :, :])[0:rows, :] if part is None else part(K.ps[lot])
                dve.tensor_copy(dst, src).then_inc(L.drained(name), 1)

            def mul(out, a, b):
                return dve.tensor_tensor(out, a, b, ALU.mult)

            rms_dve(K, dve, link, "n1", M.tmp, M.gain)
            ST.lo_to(dve, "lat0", 2)
            dve_lo(K, L, dve, "xT0", flat(M.hT_lo[:, 0:4, :]), flat(M.hT_hi[:, 0:4, :]))
            dve_lo(K, L, dve, "xT1", flat(M.hT_lo[:, 4:8, :]), flat(M.hT_hi[:, 4:8, :]))
            ST.lo_to(dve, "lat1", 2)
            take("lat", M.lat[:, :, 0:LATENT], lambda ps: ps[:, :, 0:LATENT])
            ST.lo_to(dve, "gkv", 2)
            take("gkv", M.lat[:, :, C_GK:C_POOL], lambda ps: ps[:, :, 0:C_POOL - C_GK])
            ST.lo_to(dve, "gq1", 2)
            dve.wait_ge(sig["lat_squares"], 1)
            dve.tensor_scalar(st[:, 8:10], st[:, 4:6], 1.0 / MLA_QL, EPS, ALU.mult, ALU.add)
            dve.tensor_scalar(st[:, 10:12], st[:, 6:8], 1.0 / MLA_KVL, EPS, ALU.mult, ALU.add)\
               .then_inc(sig["lat_var"], 1)
            ST.lo_to(dve, "pool1", 1)
            dve_lo(K, L, dve, "pool", flat(M.p_lo[:, :, :]), flat(M.p_hi[:, :, :]))
            dve.wait_ge(sig["lat_root"], 1)
            dve.wait_ge(sig["rows"], 96)
            link(dve.reciprocal(st[:, 4:8], st[:, 8:12]))
            for t in range(T):
                for c0, c1, s in ((0, MLA_QL, 4 + t), (MLA_QL, MLA_QL + MLA_KVL, 6 + t)):
                    last = dve.scalar_tensor_tensor(M.lat[:, t, c0:c1], M.lat[:, t, c0:c1], st[:, s:s + 1],
                                                    M.rows[:, c0:c1], ALU.mult, ALU.mult)
            last.then_inc(sig["lat_normed"], 1)
            ST.lo_to(dve, "g0b")
            qk = heads(M.lat[:, :, C_GQ:C_GV], 10)
            sq = M.scratch[:, 0:T * 10 * HD].rearrange("p (t h d) -> p t h d", t=T, h=10)
            n_qk = st[:, 16:36].rearrange("p (t h) -> p t h", t=T)
            L.wait_drained(dve, "gq")
            L.wait_drained(dve, "gkv")
            link(mul(sq, qk, qk))
            link(dve.tensor_reduce(st[:, 16:36], M.scratch[:, 0:T * 10 * HD].rearrange("p (n d) -> p n d", d=HD),
                                   AX_X, ALU.add))
            dve.tensor_scalar(st[:, 16:36], st[:, 16:36], 1.0 / HD, EPS, ALU.mult, ALU.add)\
               .then_inc(sig["gqa_var"], 1)
            lot = L.wait_filled(dve, "cols")
            dve.tensor_copy(M.cols[:, :, 0:88], K.ps[lot][:, :, 0:88])
            dve.tensor_copy(M.cols[:, 0, 88:92], K.ps[lot][:, 0, 88:92]).then_inc(L.drained("cols"), 1)
            ST.lo_to(dve, "g1a")
            dve.wait_ge(sig["gqa_root"], 1)
            link(dve.reciprocal(st[:, 16:36], st[:, 16:36]))
            link(mul(qk, qk, over_heads(n_qk, 10, HD)))
            mul(qk[:, :, 0:8, :], qk[:, :, 0:8, :], over_heads(M.rows[:, 576:640], 8, HD))
            link(mul(qk[:, :, 8:10, :], qk[:, :, 8:10, :], over_heads(M.rows[:, 640:704], 2, HD)))
            ST.lo_to(dve, "g1b")
            link(rotate(dve, link, qk, HD // 2, K.rope[:, :, 32:64], K.rope[:, :, 64:96], M.scratch, 10))
            k2 = M.k2[:, :, :].rearrange("p t (h two d) -> p t h two d", h=2, two=2)
            for two in range(2):
                last = dve.tensor_copy(k2[:, :, :, two, :], qk[:, :, 8:10, :])
            last.then_inc(sig["gqa_ready"], 1)
            dve_lo(K, L, dve, "cT", flat(M.cT_lo[:, :, :]), flat(M.cT_hi[:, :, :]),
                   lambda lot: flat(K.ps[lot][:, :, :])[:, 0:3 * S])
            ST.lo_to(dve, "uq", 2)
            for t in range(T):
                take(f"kv{t}", M.kv[:, t, :])
            ST.lo_to(dve, "g2b")
            q, k, kv = heads(M.q[:, :, :], 8), heads(M.k[:, :, :], 8), heads(M.kv[:, :, :], 8)
            kr = M.lat[:, :, MLA_QL + MLA_KVL:LATENT]
            n_q = st[:, 80:96].rearrange("p (t h) -> p t h", t=T)
            n_k = st[:, 96:112].rearrange("p (t h) -> p t h", t=T)
            L.wait_drained(dve, "q1")
            L.wait_drained(dve, "kv1")
            link(mul(M.scratch[:, :], flat(M.q[:, :, :]), flat(M.q[:, :, :])))
            link(dve.tensor_reduce(st[:, 80:96], M.scratch[:, :].rearrange("p (n d) -> p n d", d=MLA_QK),
                                   AX_X, ALU.add))
            ST.lo_to(dve, "g3a")
            link(mul(M.scratch[:, 0:1024].rearrange("p (t h d) -> p t h d", t=T, h=8), kv[:, :, :, 0:NOPE],
                     kv[:, :, :, 0:NOPE]))
            dve.tensor_reduce(st[:, 96:112], M.scratch[:, 0:1024].rearrange("p (n d) -> p n d", d=NOPE),
                              AX_X, ALU.add)
            link(mul(M.scratch[:, 1024:1088].rearrange("p (t d) -> p t d", t=T), kr, kr))
            link(dve.tensor_reduce(st[:, 72:74], M.scratch[:, 1024:1088].rearrange("p (t d) -> p t d", t=T),
                                   AX_X, ALU.add))
            link(dve.tensor_tensor(n_k, n_k, st[:, 72:74].unsqueeze(2).to_broadcast([P, T, 8]), ALU.add))
            dve.tensor_scalar(st[:, 80:112], st[:, 80:112], 1.0 / MLA_QK, EPS, ALU.mult, ALU.add)\
               .then_inc(sig["mla_var"], 1)
            ST.lo_to(dve, "g3b")
            ST.lo_to(dve, "window", 1)
            dve_lo(K, L, dve, "mix", flat(M.mixT_lo[:, :, :]), flat(M.mixT_hi[:, :, :]))
            dve.wait_ge(sig["mla_root"], 1)
            link(dve.reciprocal(st[:, 80:112], st[:, 80:112]))
            link(mul(q, q, over_heads(n_q, 8, MLA_QK)))
            mul(k[:, :, :, 0:NOPE], kv[:, :, :, 0:NOPE], over_heads(n_k, 8, NOPE))
            link(mul(k[:, :, :, NOPE:MLA_QK], kr.unsqueeze(2).to_broadcast([P, T, 8, ROPE]),
                     over_heads(n_k, 8, ROPE)))
            ST.lo_to(dve, "g4b")
            mul(q, q, over_heads(M.rows[:, 384:480], 8, MLA_QK))
            link(mul(k, k, over_heads(M.rows[:, 480:576], 8, MLA_QK)))
            ST.lo_to(dve, "pool_w")
            cos, sin = K.rope[:, :, 0:16], K.rope[:, :, 16:32]
            link(rotate(dve, link, q[:, :, :, NOPE:MLA_QK], ROPE // 2, cos, sin, M.scratch, 8))
            rotate(dve, link, k[:, :, :, NOPE:MLA_QK], ROPE // 2, cos, sin, M.scratch, 8)\
                .then_inc(sig["mla_ready"], 1)
            ST.lo_to(dve, "pool_w", 2)
            dve.wait_ge(sig["hi_py"], 1)
            lot = L.use["py"][0]
            for g in range(POOL_G):
                last = dve.scalar_tensor_tensor(M.oTp_lo[:, g, :], flat(K.ps[lot][:, :, :])[:, g * S:(g + 1) * S],
                                                M.cols[:, 0, 88 + g:89 + g], M.oTp_hi[:, g, :].bitcast(F32),
                                                ALU.mult, ALU.subtract)
            last.then_inc(L.drained("py"), 1)
            ST.lo_to(dve, "g5b", 3)
            take("gkT", flat(M.gkT[:, :, :]), lambda ps: ps[:, 0, :])
            ga.dve(dve, link)

            for g in range(6):
                L.wait_drained(dve, f"g{g}")
            for c in range(2):
                ST.lo_to(dve, f"bp{c}", 2)
                lot = L.wait_filled(dve, f"bp{c}")
                mul(merged[:, :, c * 512:(c + 1) * 512], K.ps[lot][:, :, :],
                    M.gates[:, :, 2 * D + c * 512:2 * D + (c + 1) * 512]).then_inc(L.drained(f"bp{c}"), 1)
            for half in range(2):
                take(f"mkT{half}", flat(M.mkT[0:MLA_QK, 4 * half:4 * half + 4, :]), rows=MLA_QK)
            ma.dve(dve, link)
            for c in range(2):
                L.wait_drained(dve, f"bp{c}")
            for name, b in (("bg", 1), ("bm", 0)):
                for c in range(2):
                    ST.lo_to(dve, f"{name}{c}", 2)
                    lot = L.wait_filled(dve, f"{name}{c}")
                    gate = M.gates[:, :, b * D + c * 512:b * D + (c + 1) * 512]
                    mul(gate, K.ps[lot][:, :, :], gate).then_inc(L.drained(f"{name}{c}"), 1)
                    L.wait_drained(dve, f"{name}{c}")
                    last = dve.tensor_tensor(merged[:, :, c * 512:(c + 1) * 512],
                                             merged[:, :, c * 512:(c + 1) * 512], gate, ALU.add)
                    if (name, c) == ("bm", 1):
                        last.then_inc(sig["merged"], 1)
                    else:
                        link(last)
            dve_lo(K, L, dve, "mT0", flat(M.hT_lo[:, 0:4, :]), flat(M.hT_hi[:, 0:4, :]))
            dve_lo(K, L, dve, "mT1", flat(M.hT_lo[:, 4:8, :]), flat(M.hT_hi[:, 4:8, :]))
            ST.lo_to(dve, "wo11")
            for c in range(2):
                lot = L.wait_filled(dve, f"wo{c}")
                x = K.x[:, :, c * 512:(c + 1) * 512]
                dve.tensor_tensor(x, x, K.ps[lot][:, :, :], ALU.add).then_inc(L.drained(f"wo{c}"), 1)
            L.wait_drained(dve, "wo1")
            ST.lo_to(dve, "U0")
            rms_dve(K, dve, link, "n2", M.tmp, M.gain)
            dve_lo(K, L, dve, "fT0", flat(M.hT_lo[:, 0:4, :]), flat(M.hT_hi[:, 0:4, :]))
            dve_lo(K, L, dve, "fT1", flat(M.hT_lo[:, 4:8, :]), flat(M.hT_hi[:, 4:8, :]))
            ST.lo_to(dve, "G1")

            def outer_taps(e, i):
                lot = L.use[f"H{e}"][0]
                dve.wait_ge(sig["middle"], later(e + 1, i, 2))
                for tap in (0, 2):
                    for b in range(2):
                        for f in range(2):
                            at = 22 * b + f + 2 * true_step(e, i)
                            u, c = K.ps[lot][:, b, f * S:(f + 1) * S], M.conv[:, b, f, :]
                            src, dst = (u[:, 0:S - 1], c[:, 1:S]) if tap == 0 else (u[:, 1:S], c[:, 0:S - 1])
                            w = M.cols[:, tap // 2, bass.ds(at, 1)]
                            last = dve.scalar_tensor_tensor(dst, src, w, dst, ALU.mult, ALU.add)
                    if tap == 0:
                        link(last)
                last.then_inc(L.drained(f"H{e}"), 1)

            def product(e, i):
                dve.wait_ge(sig["silu"], later(e + 1, i, 2))
                dve.tensor_tensor(K.h, M.conv[:, 0, :, :], K.h, ALU.mult).then_inc(sig["h_full"], 1)

            def add(e, i, t):
                return dve.tensor_tensor(K.x[:, t, :], K.x[:, t, :],
                                         flat(K.ps[L.use[f"Y{e}t{t}"][0]][:, :, :]), ALU.add)

            ffn_dve(K, L, ST, dve, FF_STEPS, outer_taps, product, add, (M.h_hi, M.h_lo),
                    lambda i: link.enter(i, 2), link.leave)



TWO_CHUNKS = ["iq0", "iq1", "ik", "dq0", "dq1", "dk0", "dk1", "sq0", "sq1", "sk0", "sk1", "dv0", "dv1", "sv0", "sv1",
              "g0a", "g0b", "g1a", "g1b", "g2a", "g2b", "g3a", "g3b", "bs0", "bs1", "bd0", "bd1",
              "wo00", "wo01", "wo10", "wo11", "route", "pg00", "pg01", "pg10", "pg11", "wple"]
N_ROUTE = N_G + N_E
TWO_WIDTHS = {"ik": KD * (HD + IDX_H), "route": KD * N_ROUTE}
TWO_ENDS = {"ik": "ik", "wo01": "wo0", "wo11": "wo1", "route": "rt", "pg01": "pg0", "pg11": "pg1", "wple": "pl1"}
TWO_ENDS |= {f"{n}1": n for n in ("iq", "dq", "dk", "sq", "sk", "dv", "sv")}
TWO_ENDS |= {f"g{g}b": f"g{g}" for g in range(4)} | {f"b{b}{c}": f"b{b}{c}" for b in "sd" for c in range(2)}
TWO_COLUMNS = {"dq": C_DQ, "dk": C_DK, "dv": C_DV, "sq": C_SQ, "sk": C_SK, "sv": C_SV, "iq": C_IQ}


class TwoTiles:

    def __init__(self, K):
        K.base = K.floor
        o = {}

        def tile(name, shape, dtype=F32):
            o[name] = K.base
            return K.tile("two_" + name, shape, dtype)

        def over(name, shape, at, dtype=F32, off=0):
            return K.over("two_" + name, shape, o[at] + off, dtype)

        KB = 1024
        self.rot = tile("rot", [P, T, ROT])
        self.causal = tile("causal", [P, T, S])
        self.hT_hi = tile("hT_hi", [P, KD, S], F32R)
        self.hT_lo = tile("hT_lo", [P, KD, S], F32R)
        self.sT_hi = over("sT_hi", [P, 4, S], "hT_hi", F32R)
        self.sT_lo = over("sT_lo", [P, 4, S], "hT_hi", F32R, 4 * KB)
        self.yT_hi = over("yT_hi", [P, 4, S], "hT_lo", F32R)
        self.yT_lo = over("yT_lo", [P, 4, S], "hT_lo", F32R, 4 * KB)
        self.gates = tile("gates", [P, T, 2 * D])
        self.pr = tile("pr", [P, T, C_ATT])
        self.ln_g = over("ln_g", [P, D], "pr")
        self.ln_b = over("ln_b", [P, D], "pr", off=4 * KB)
        self.ln2_g = over("ln2_g", [P, D], "pr", off=8 * KB)
        self.ln2_b = over("ln2_b", [P, D], "pr", off=12 * KB)
        self.ple = over("ple", [P, T, S], "pr", off=16 * KB)
        self.dqT, self.dkT, self.sqT, self.skT, self.iqT = (tile(n, [P, 4, S]) for n in ("dqT", "dkT", "sqT", "skT", "iqT"))
        self.ikT = tile("ikT", [P, S])
        self.pT_hi = over("pT_hi", [P, 2, S], "dqT", F32R)
        self.pT_lo = over("pT_lo", [P, 2, S], "dqT", F32R, 2 * KB)
        self.pgate = over("pgate", [P, 2, T, 512], "dkT")
        self.tmp = tile("tmp", [P, T, D])
        self.act = over("act", [P, 2, 2, S], "tmp")
        self.scratch = over("scratch", [P, 1024], "tmp")
        self.ik2 = over("ik2", [P, T, 2 * HD], "tmp", off=4 * KB)
        self.p = tile("p", [P, 2, D])
        self.h_hi = over("h_hi", [P, 2, 2, S], "p", F32R)
        self.h_lo = over("h_lo", [P, 2, 2, S], "p", F32R, 4 * KB)
        self.pt = tile("pt", [P, D])
        self.ya = tile("ya", [P, T, 512])
        self.score = tile("score", [P, T, S])
        self.work = tile("work", [P, T, S])
        self.bias = tile("bias", [P, T, S])
        self.top8 = tile("top8", [P, T, 8])
        self.wi = tile("wi", [P, T, 8])
        self.lam = tile("lam", [P, 4 * HD + 2])
        self.sub = tile("sub", [P, P])
        self.route_b = tile("route_b", [P, N_ROUTE])
        self.logit = tile("logit", [P, T, N_ROUTE])
        self.r32 = tile("r32", [P, T, N_E])
        self.r = tile("r", [P, 8, T, 8])
        self.iota = tile("iota", [P, 12])
        self.comb = tile("comb", [P, T, N_E])
        self.pos = tile("pos", [P, T], I32)
        self.inv = tile("inv", [P, ROT // 2])
        self.ang = tile("ang", [P, 4, T, ROT // 2])


def rotation_tables(K, M):
    nc, A, sig, st = K.nc, K.A, K.sig, K.stat
    turn, magic = 2 * np.pi, 1.5 * 2.0 ** 23
    c1 = 6.28125
    c2 = float(np.float32(np.frombuffer(np.uint32(np.float32(turn - c1).view(np.uint32) & 0xFFFFF000).tobytes(),
                                        np.float32)[0]))
    c3 = turn - c1 - c2
    with nc.Block() as block:

        @block.sync
        def _(sp):
            with nc.allow_non_contiguous_dma(reason="256 positions, one a partition and tile"):
                sp.dma_start(M.pos[:, :], A["positions_2"][0].rearrange("(t p) -> p t", p=P)).then_inc(sig["tables"], 16)
            sp.dma_start(M.inv[:, :], A["c_inv_freq"][0].partition_broadcast(P)).then_inc(sig["tables"], 16)
            sp.dma_start(M.causal[:, :, :], A["c_causal"]).then_inc(sig["tables"], 16)
            sp.dma_start(M.iota[:, 0:N_G], A["c_groups"][0].partition_broadcast(P)).then_inc(sig["tables"], 16)
            sp.dma_start(M.iota[:, 4:12], A["c_experts"][0].partition_broadcast(P)).then_inc(sig["tables"], 16)

        @block.scalar
        def _(act):
            act.wait_ge(sig["angles"], 1)
            act.activation(M.rot[:, :, 8:16], M.ang[:, 0, :, :], ACT.Sin).then_inc(sig["sines"], 1)
            act.activation(M.rot[:, :, 0:8], M.ang[:, 2, :, :], ACT.Sin).then_inc(sig["sines"], 1)

        @block.vector
        def _(dve):
            link = Chain(dve, sig["dve_chain"])
            dve.wait_ge(sig["tables"], 80)
            link(dve.tensor_copy(st[:, 0:T], M.pos[:, :]))
            for t in range(T):
                last = dve.tensor_scalar(M.ang[:, 0, t, :], M.inv[:, :], st[:, t:t + 1], None, ALU.mult)
            link(last)
            a, k, c = (M.ang[:, n, :, :] for n in range(3))
            link(dve.tensor_scalar(k, a, 1.0 / turn, magic, ALU.mult, ALU.add))
            link(dve.tensor_scalar(k, k, magic, None, ALU.subtract))
            for part in (c1, c2, c3):
                link(dve.scalar_tensor_tensor(a, k, -part, a, ALU.mult, ALU.add))
            link(dve.tensor_scalar(a, a, 3.1415925, -3.1415925, ALU.min, ALU.max))
            link(dve.scalar_tensor_tensor(c, a, -1.0, a, ALU.mult, ALU.max))
            dve.tensor_scalar(c, c, -1.0, np.pi / 2, ALU.mult, ALU.add).then_inc(sig["angles"], 1)


class DiffAttention(Attention):

    def pe_turn(self, pe, u):
        K, L = self.K, self.L
        p = self.p[:, u % 2, 0:T * S].rearrange("p (t k) -> p t k", t=T)
        d = K.ps[L.use[f"{self.tag}T{u}"][0]][:, 0, :].rearrange("p (c q) -> p c q", c=T)
        for t in range(T):
            for c in range(T):
                last = pe.transpose(d[:, c, t * P:(t + 1) * P], p[:, t, c * P:(c + 1) * P], K.ident[:, :])
        return last

    def pe_out(self, pe, u):
        K = self.K
        pt = self.pt[:, 0:T * S].rearrange("p (c q) -> p c q", c=T)
        for t in range(T):
            for c in range(T):
                last = pe.matmul(K.ps[3][:, t, 0:P], pt[:, c, t * P:(t + 1) * P], self.v(u, 0, c),
                                 start=c == 0, stop=c == T - 1)
        return last

    def turned_size(self):
        return T * S

    def act_out(self, act, u):
        self.L.wait_filled(act, f"{self.tag}O{u}")
        act.activation(self.out[:, :, u * P:(u + 1) * P], self.K.ps[3][:, :, 0:P], ACT.Copy)\
           .then_inc(self.L.drained(f"{self.tag}O{u}"), 1)

    def dve_out(self, dve, u):
        pass

    def weigh(self, dve, link, u, inv):
        p = self.p[:, u % 2, :].rearrange("p (n k) -> p n k", n=4)
        link(dve.tensor_scalar(inv[:, 2:4], inv[:, 2:4], self.K.stat[:, 120:121], None, ALU.mult))
        link(dve.tensor_tensor(p[:, 0:2, :], p[:, 0:2, :], inv[:, 0:2].unsqueeze(2).to_broadcast([P, 2, S]), ALU.mult))
        for t in range(T):
            last = dve.scalar_tensor_tensor(p[:, t, :], p[:, 2 + t, :], inv[:, 2 + t:3 + t], p[:, t, :],
                                            ALU.mult, ALU.add)
        return last


def norm_act(K, act, tag, junk):
    st = K.stat
    for t in range(T):
        last = act.activation(junk[:, t, :], K.x[:, t, :], ACT.Copy, accum_out=st[:, t:t + 1])
    last.then_inc(K.sig[f"{tag}_sums"], 1)
    act.wait_ge(K.sig[f"{tag}_centred"], 1)
    for t in range(T):
        last = act.activation(junk[:, t, :], K.x[:, t, :], ACT.Square, accum_out=st[:, 4 + t:5 + t])
    last.then_inc(K.sig[f"{tag}_squares"], 1)
    act.wait_ge(K.sig[f"{tag}_var"], 1)
    act.activation(st[:, 6:8], st[:, 6:8], ACT.Sqrt).then_inc(K.sig[f"{tag}_root"], 1)


def norm_dve(K, dve, link, tag, g, b):
    st = K.stat
    dve.wait_ge(K.sig[f"{tag}_sums"], 1)
    link(dve.tensor_scalar(st[:, 2:4], st[:, 0:2], 1.0 / D, None, ALU.mult))
    for t in range(T):
        last = dve.tensor_scalar(K.x[:, t, :], K.x[:, t, :], st[:, 2 + t:3 + t], None, ALU.subtract)
    last.then_inc(K.sig[f"{tag}_centred"], 1)
    dve.wait_ge(K.sig[f"{tag}_squares"], 1)
    dve.tensor_scalar(st[:, 6:8], st[:, 4:6], 1.0 / D, LN_EPS, ALU.mult, ALU.add).then_inc(K.sig[f"{tag}_var"], 1)
    dve.wait_ge(K.sig[f"{tag}_root"], 1)
    link(dve.reciprocal(st[:, 4:6], st[:, 6:8]))
    dve.wait_ge(K.sig[f"{tag}_gain"], 32)
    for t in range(T):
        last = dve.scalar_tensor_tensor(K.x[:, t, :], K.x[:, t, :], st[:, 4 + t:5 + t], g[:, :], ALU.mult, ALU.mult)
    link(last)
    dve.tensor_tensor(K.x[:, :, :], K.x[:, :, :], b[:, :].unsqueeze(1).to_broadcast([P, T, D]), ALU.add)\
       .then_inc(K.sig[f"{tag}_normed"], 1)


def block_two(K, M, layer):
    nc, A, sig, st = K.nc, K.A, K.sig, K.stat
    names = TWO_CHUNKS + ffn_chunks(N_E)
    order = [("xT0", 0), ("xT1", 1), ("iq", 2), ("ik", 3), ("dq", 0), ("dk", 1), ("sq", 2), ("iqT", 3), ("ikT", 0),
             ("sk", 1), ("I0", 2), ("I1", 3), ("I2", 2), ("I3", 3), ("dv", 0), ("sv", 1), ("g0", 2), ("g1", 3),
             ("dqT", 0), ("dkT", 1), ("sqT", 2), ("skT", 3), ("g2", 0), ("g3", 1)]
    order += Attention.lots("da", DIFF_H) + Attention.lots("sa", DSA_H // 2)
    order += [("bs0", 2), ("bs1", 0), ("yT", 1), ("bd0", 2), ("bd1", 3), ("mT0", 0), ("mT1", 1), ("wo0", 2),
              ("wo1", 3), ("pT", 0), ("nT0", 1), ("nT1", 2), ("rt", 3), ("pg0", 0), ("pg1", 1), ("pl0", 2), ("pl1", 3)]
    order += ffn_lots(N_E)
    L = Lots(order, K.filled, K.drained)
    ST = Stream(K, L, names, TWO_WIDTHS, TWO_ENDS | ffn_ends(N_E), {"route": 2})
    K.h = M.act[:, 1, :, :]
    hT = (M.hT_hi, M.hT_lo)
    merged = M.tmp
    pair = lambda tile: lambda u, h: tile[h * HD:(h + 1) * HD, u, :]
    over_two = lambda m: m[:, :, :].rearrange("p t k -> p (t k)").unsqueeze(1).to_broadcast([P, 2, T * S])
    da = DiffAttention(K, L, "da", DIFF_H, q=pair(M.dqT), k=pair(M.dkT),
                       v=lambda u, h, c: M.pr[:, c, C_DV + u * P:C_DV + (u + 1) * P],
                       scale=HD ** -0.5, p=M.p, pt=M.pt, mask=over_two(M.causal), out=M.ya)
    sa = Attention(K, L, "sa", DSA_H // 2, q=pair(M.sqT), k=pair(M.skT),
                   v=lambda u, h, c: M.pr[:, c, C_SV + (2 * u + h) * HD:C_SV + (2 * u + h + 1) * HD],
                   scale=HD ** -0.5, p=M.p, pt=M.pt, mask=over_two(M.bias), out=(M.sT_hi, M.sT_lo))

    def source(name):
        w = A["w_in_2"][layer]
        kpc = lambda a: a.rearrange("(k p) c -> p k c", p=P)
        square = lambda w, c, k: kpc(w[k * 512:(k + 1) * 512, c * 512:(c + 1) * 512])
        if name == "ik":
            return kpc(w[:, C_IK:C_GA])
        if name[:2] in TWO_COLUMNS:
            c, k = TWO_COLUMNS[name[:2]], int(name[2])
            return kpc(w[k * 512:(k + 1) * 512, c:c + 512])
        if name[:2] == "wo":
            return square(A["w_out_2"][layer], int(name[2]), int(name[3]))
        if name[:2] == "pg":
            return square(A["w_ple_gate_2"][layer], int(name[2]), int(name[3]))
        if name == "wple":
            return kpc(A["w_ple_2"][layer])
        if name[0] == "b":
            b, c = {"s": "w_branch_dsa_2", "d": "w_branch_diff_2"}[name[1]], int(name[2])
            return kpc(A[b][layer][:, c * 512:(c + 1) * 512])
        c, k = C_GA + 512 * int(name[1]), "ab".index(name[2])
        return kpc(w[k * 512:(k + 1) * 512, c:c + 512])

    def expert_source(kind, e):
        w = {"G": "w_exp_gate_2", "U": "w_exp_up_2", "D": "w_exp_down_2"}[kind]
        return A[w][layer].rearrange("g e d f -> (g e) d f")[e].rearrange("(k p) c -> p k c", p=P)

    with nc.Block() as block:

        @block.sync
        def _(sp):
            for name in TWO_CHUNKS:
                ST.may_load(sp, name)
                dst = K.raw[:, ST.slot(name), 0:ST.columns(name)]
                if name == "route":
                    dst = dst.rearrange("p (k c) -> p k c", k=KD)
                    for c0, c1, w in ((0, N_G, "w_route_group_2"), (N_G, N_ROUTE, "w_route_expert_2")):
                        sp.dma_start(dst[:, :, c0:c1], A[w][layer].rearrange("(k p) c -> p k c", p=P))\
                          .then_inc(K.landed[ST.slot(name)], 16)
                else:
                    src = source(name)
                    sp.dma_start(dst.rearrange("p (k c) -> p k c", k=src.shape[1]), src)\
                      .then_inc(K.landed[ST.slot(name)], 16)
                if name == "ik":
                    for dst, src in ((M.lam[:, 0:4 * HD], A["diff_lambda_2"][layer].rearrange("a d -> (a d)")),
                                     (M.lam[:, 4 * HD:4 * HD + 2], A["c_lam_init"][layer]),
                                     (M.sub[:, :], A["diff_subln_g_2"][layer]),
                                     (M.route_b[:, 0:N_G], A["b_route_group_2"][layer]),
                                     (M.route_b[:, N_G:N_ROUTE], A["b_route_expert_2"][layer])):
                        sp.dma_start(dst, src.partition_broadcast(P)).then_inc(sig["rows"], 16)
                if name == "bd1":
                    L.wait_filled(sp, "saO3")
                    for tile, src, s in ((M.ln_g, "ln1_g_2", "n1_gain"), (M.ln_b, "ln1_b_2", "n1_gain"),
                                         (M.ln2_g, "ln2_g_2", "n2_gain"), (M.ln2_b, "ln2_b_2", "n2_gain")):
                        sp.dma_start(tile[:, :], A[src][layer].partition_broadcast(P)).then_inc(sig[s], 16)
                    sp.dma_start(M.ple[:, :, :], A["p_2"][layer][0].rearrange("(t p) d -> p t d", p=P))\
                      .then_inc(sig["ple_rows"], 16)
            ffn_load(K, ST, sp, N_E, expert_source)

        @block.tensor
        def _(pe):
            def both(*names):
                for n in names:
                    L.wait_drained(pe, n)

            def group(name):
                project(K, L, ST, pe, name, (f"{name}0", f"{name}1"), 512, hT)

            def turn(name, src, pairs):
                lot = L.claim(pe, name)
                d = flat(K.ps[lot][:, :, :]).rearrange("p (k s) -> p k s", k=4)
                for k in range(pairs):
                    for t in range(T):
                        last = pe.transpose(d[:, k, t * P:(t + 1) * P], src[:, t, k * P:(k + 1) * P], K.ident[:, :])
                last.then_inc(L.filled(name), 1)

            transpose_x(K, L, pe, K.x, ("xT0", "xT1"))
            both("xT0", "xT1")
            group("iq")
            project(K, L, ST, pe, "ik", ("ik",), HD + IDX_H, hT, kn=KD)
            group("dq")
            group("dk")
            group("sq")
            pe.wait_ge(sig["index_ready"], 1)
            turn("iqT", M.pr[:, :, C_IQ:C_IK], 4)
            turn("ikT", M.ik2[:, :, :], 1)
            group("sk")
            both("iqT", "ikT")
            for u in range(4):
                lot = L.claim(pe, f"I{u}")
                s = flat(K.ps[lot][:, :, :]).rearrange("p (h t k) -> p h t k", h=2, t=T)
                for h in range(2):
                    for t in range(T):
                        last = pe.matmul(s[:, h, t, :], M.iqT[h * HD:(h + 1) * HD, u, t * P:(t + 1) * P],
                                         M.ikT[h * HD:(h + 1) * HD, :], start=True, stop=True)
                last.then_inc(L.filled(f"I{u}"), 1)
            group("dv")
            group("sv")
            project(K, L, ST, pe, "g0", ("g0a", "g0b"), 512, hT)
            project(K, L, ST, pe, "g1", ("g1a", "g1b"), 512, hT)
            pe.wait_ge(sig["diff_ready"], 1)
            turn("dqT", M.pr[:, :, C_DQ:C_DK], 4)
            turn("dkT", M.pr[:, :, C_DK:C_DV], 4)
            pe.wait_ge(sig["sparse_ready"], 1)
            turn("sqT", M.pr[:, :, C_SQ:C_SK], 4)
            turn("skT", M.pr[:, :, C_SK:C_SV], 4)
            project(K, L, ST, pe, "g2", ("g2a", "g2b"), 512, hT)
            project(K, L, ST, pe, "g3", ("g3a", "g3b"), 512, hT)
            both("dqT", "dkT", "dv")
            da.pe(pe)
            both("sqT", "skT", "sv")
            sa.pe(pe)

            def branch(name, xT):
                for c in range(2):
                    lot = L.claim(pe, f"{name}{c}")
                    token_product(K, ST, pe, lambda t: K.ps[lot][:, t, :], xT, f"{name}{c}", True, True, 0, 4, 512)\
                        .then_inc(L.filled(f"{name}{c}"), 1)

            both("saO3")
            branch("bs", (M.sT_hi, M.sT_lo))
            pe.wait_ge(sig["ya_normed"], 1)
            turn("yT", M.ya[:, :, :], 4)
            both("yT")
            branch("bd", (M.yT_hi, M.yT_lo))
            pe.wait_ge(sig["merged"], 1)
            transpose_x(K, L, pe, merged, ("mT0", "mT1"))
            both("mT0", "mT1")
            for c in range(2):
                project(K, L, ST, pe, f"wo{c}", (f"wo{c}0", f"wo{c}1"), 512, hT)
            pe.wait_ge(sig["ple_rows"], 16)
            turn("pT", M.ple[:, :, :], 2)
            pe.wait_ge(sig["n1_normed"], 1)
            transpose_x(K, L, pe, K.x, ("nT0", "nT1"))
            both("nT0", "nT1")
            project(K, L, ST, pe, "rt", ("route",), N_ROUTE, hT, kn=KD)
            for c in range(2):
                project(K, L, ST, pe, f"pg{c}", (f"pg{c}0", f"pg{c}1"), 512, hT)
            both("pT")
            for c in range(2):
                lot = L.claim(pe, f"pl{c}")
                token_product(K, ST, pe, lambda t: K.ps[lot][:, t, :], (M.pT_hi, M.pT_lo), "wple", True, True,
                              0, 2, D, c0=c * 512, cn=512).then_inc(L.filled(f"pl{c}"), 1)
            ffn_pe(K, L, ST, pe, N_E, hT, (M.h_hi, M.h_lo))

        @block.scalar
        def _(act):
            def take(name, dst, part=None, func=ACT.Copy):
                lot = L.wait_filled(act, name)
                src = flat(K.ps[lot][:, :, :]) if part is None else part(K.ps[lot])
                act.activation(dst, src, func).then_inc(L.drained(name), 1)

            def whole(ps):
                return ps[:, :, :]

            def columns(name):
                ST.hi_to(act, f"{name}1", 2)
                c = TWO_COLUMNS[name]
                take(name, M.pr[:, :, c:c + 512], whole)

            def sigmoid(g):
                take(f"g{g}", M.gates[:, :, g * 512:(g + 1) * 512], whole, ACT.Sigmoid)

            ST.hi_to(act, "iq0", 2)
            act_hi(K, L, act, "xT0", flat(M.hT_hi[:, 0:4, :]))
            act_hi(K, L, act, "xT1", flat(M.hT_hi[:, 4:8, :]))
            columns("iq")
            ST.hi_to(act, "ik", 2)
            act.wait_ge(sig["lam_dots"], 1)
            act.activation(st[:, 122:124], st[:, 122:124], ACT.Exp).then_inc(sig["lam_exps"], 1)
            columns("dq")
            columns("dk")
            columns("sq")
            take("iqT", flat(M.iqT[:, :, :]))
            columns("sk")
            for u in range(4):
                if u >= 2:
                    act.wait_ge(sig["index_sums"], u - 1)
                take(f"I{u}", M.p[:, u % 2, :], func=ACT.Relu)
            columns("dv")
            columns("sv")
            for g in range(2):
                ST.hi_to(act, f"g{g}b", 2)
                sigmoid(g)
            take("dqT", flat(M.dqT[:, :, :]))
            take("sqT", flat(M.sqT[:, :, :]))
            ST.hi_to(act, "g2b", 2)
            sigmoid(2)
            ST.hi_to(act, "g3b", 2)
            sigmoid(3)
            ST.hi_to(act, "g3b", 3)
            da.act(act)
            sa.act(act)
            act.wait_ge(sig["ya_var"], 1)
            act.activation(st[:, 130:138], st[:, 130:138], ACT.Sqrt).then_inc(sig["ya_root"], 1)
            ST.hi_to(act, "bs1", 1)
            act_hi(K, L, act, "yT", flat(M.yT_hi[:, :, :]))
            ST.hi_to(act, "wo01")
            act_hi(K, L, act, "mT0", flat(M.hT_hi[:, 0:4, :]))
            act_hi(K, L, act, "mT1", flat(M.hT_hi[:, 4:8, :]))
            ST.hi_to(act, "wo11", 1)
            act_hi(K, L, act, "pT", flat(M.pT_hi[:, :, :]), lambda lot: K.ps[lot][:, 0, :])
            L.wait_drained(act, "wo1")
            norm_act(K, act, "n1", M.tmp)
            ST.hi_to(act, "wo11", 3)
            act_hi(K, L, act, "nT0", flat(M.hT_hi[:, 0:4, :]))
            act_hi(K, L, act, "nT1", flat(M.hT_hi[:, 4:8, :]))
            ST.hi_to(act, "route", 3)
            act.wait_ge(sig["group_shift"], 1)
            act.activation(M.r[:, 0, :, 0:N_G], M.r[:, 0, :, 0:N_G], ACT.Exp).then_inc(sig["group_exps"], 1)
            act.wait_ge(sig["expert_shift"], 1)
            act.activation(M.r[:, 3, :, :], M.r[:, 3, :, :], ACT.Exp).then_inc(sig["expert_exps"], 1)
            ST.hi_to(act, "pg01", 2)
            take("pg0", M.pgate[:, 0, :, :], whole, ACT.Sigmoid)
            ST.hi_to(act, "pg11", 2)
            take("pg1", M.pgate[:, 1, :, :], whole, ACT.Sigmoid)
            ST.hi_to(act, "G1")

            def silu(e, i):
                lot = L.wait_filled(act, f"H{e}", i, 1)
                if e or i is not None:
                    L.wait_drained(act, f"H{e - 1}", i, 1)
                act.activation(flat(M.act[:, 0, :, :]), K.ps[lot][:, 0, :], ACT.Silu).then_inc(sig["silu"], 1)

            ffn_act(K, L, ST, act, N_E, silu, lambda e, i: None,
                    lambda e, i: L.wait_drained(act, f"H{e}", i, 1), M.h_hi)
            for t in range(T):
                L.wait_drained(act, f"Y{N_E - 1}t{t}")
            norm_act(K, act, "n2", M.tmp)

        @block.vector
        def _(dve):
            link = Chain(dve, sig["dve_chain"])

            def tt(out, a, b, op):
                return dve.tensor_tensor(out, a, b, op)

            def take(name, dst, part=None):
                lot = L.wait_filled(dve, name)
                dve.tensor_copy(dst, flat(K.ps[lot][:, :, :]) if part is None else part(K.ps[lot]))\
                   .then_inc(L.drained(name), 1)

            cos, sin = M.rot[:, :, 0:8], M.rot[:, :, 8:16]
            ST.lo_to(dve, "iq0", 2)
            dve_lo(K, L, dve, "xT0", flat(M.hT_lo[:, 0:4, :]), flat(M.hT_hi[:, 0:4, :]))
            dve_lo(K, L, dve, "xT1", flat(M.hT_lo[:, 4:8, :]), flat(M.hT_hi[:, 4:8, :]))
            ST.lo_to(dve, "iq1", 2)
            ST.lo_to(dve, "ik", 2)
            take("ik", M.pr[:, :, C_IK:C_GA], lambda ps: ps[:, :, 0:HD + IDX_H])
            dve.wait_ge(sig["rows"], 80)
            lam = M.lam[:, 0:4 * HD].rearrange("p (a b d) -> p a b d", a=2, b=2)
            prod = M.scratch[:, 0:2 * HD].rearrange("p (a d) -> p a d", a=2)
            link(tt(prod, lam[:, :, 0, :], lam[:, :, 1, :], ALU.mult))
            dve.tensor_reduce(st[:, 122:124], prod, AX_X, ALU.add).then_inc(sig["lam_dots"], 1)
            L.wait_drained(dve, "iq")
            L.wait_drained(dve, "ik")
            link(rotate(dve, link, heads(M.pr[:, :, C_IQ:C_IW], 9), ROT // 2, cos, sin, M.scratch[:, 128:], 9))
            for two in range(2):
                dve.tensor_copy(M.ik2[:, :, two * HD:(two + 1) * HD], M.pr[:, :, C_IK:C_IW])
            dve.tensor_scalar(M.wi[:, :, :], M.pr[:, :, C_IW:C_GA], IDX_H ** -0.5, None, ALU.mult)\
               .then_inc(sig["index_ready"], 1)
            ST.lo_to(dve, "dq1", 1)
            dve.wait_ge(sig["lam_exps"], 1)
            link(tt(st[:, 120:121], st[:, 123:124], st[:, 122:123], ALU.subtract))
            link(tt(st[:, 120:121], st[:, 120:121], M.lam[:, 4 * HD:4 * HD + 1], ALU.subtract))
            link(dve.tensor_scalar(M.sub[:, :], M.sub[:, :], M.lam[:, 4 * HD + 1:4 * HD + 2], None, ALU.mult))
            ST.lo_to(dve, "dk1", 2)
            L.wait_drained(dve, "dq")
            L.wait_drained(dve, "dk")
            rotate(dve, link, heads(M.pr[:, :, C_DQ:C_DV], 16), ROT // 2, cos, sin, M.scratch, 16)\
                .then_inc(sig["diff_ready"], 1)
            dve.wait_ge(sig["diff_ready"], 1)
            ST.lo_to(dve, "sq1", 2)
            take("ikT", M.ikT[:, :], lambda ps: ps[:, 0, 0:S])
            ST.lo_to(dve, "sk1", 2)
            L.wait_drained(dve, "sq")
            L.wait_drained(dve, "sk")
            rotate(dve, link, heads(M.pr[:, :, C_SQ:C_SV], 16), ROT // 2, cos, sin, M.scratch, 16)\
                .then_inc(sig["sparse_ready"], 1)
            dve.wait_ge(sig["index_ready"], 1)
            for u in range(4):
                L.wait_drained(dve, f"I{u}")
                p = M.p[:, u % 2, :].rearrange("p (h t k) -> p h t k", h=2, t=T)
                for h in range(2):
                    for t in range(T):
                        n = (t + 1) * P
                        w = M.wi[:, t, 2 * u + h:2 * u + h + 1]
                        if u == h == 0:
                            last = dve.tensor_scalar(M.score[:, t, 0:n], p[:, h, t, 0:n], w, None, ALU.mult)
                        else:
                            last = dve.scalar_tensor_tensor(M.score[:, t, 0:n], p[:, h, t, 0:n], w,
                                                            M.score[:, t, 0:n], ALU.mult, ALU.add)
                    if h == 0:
                        link(last)
                last.then_inc(sig["index_sums"], 1)
                dve.wait_ge(sig["index_sums"], u + 1)
            for t in range(T):
                n = (t + 1) * P
                last = dve.scalar_tensor_tensor(M.work[:, t, 0:n], M.score[:, t, 0:n], HD ** -0.5,
                                                M.causal[:, t, 0:n], ALU.mult, ALU.add)
            link(last)
            splits = {1: ("dv1", 2), 3: ("sv1", 1), 5: ("sv1", 2), 7: ("g0b", 2)}
            for r in range(TOPK // 8):
                for t in range(T):
                    last = dve.max(M.top8[:, t, :], M.work[:, t, 0:(t + 1) * P])
                link(last)
                for t in range(T):
                    w = M.work[:, t, 0:(t + 1) * P]
                    last = dve.match_replace(w, M.top8[:, t, :], w, PICKED)
                link(last)
                if r in splits:
                    ST.lo_to(dve, *splits[r])
            for t in range(T):
                n = (t + 1) * P
                last = dve.tensor_scalar(M.bias[:, t, 0:n], M.work[:, t, 0:n], -2e38, NEG, ALU.is_gt, ALU.mult)
            link(last)
            tt(M.bias[:, 0, 0:P], M.bias[:, 0, 0:P], M.causal[:, 0, 0:P], ALU.add)
            dve.tensor_copy(M.bias[:, 0, P:S], M.causal[:, 0, P:S])
            link(tt(M.bias[:, 1, :], M.bias[:, 1, :], M.causal[:, 1, :], ALU.add))
            ST.lo_to(dve, "g1b", 2)
            take("dkT", flat(M.dkT[:, :, :]))
            take("skT", flat(M.skT[:, :, :]))
            ST.lo_to(dve, "g2b", 2)
            ST.lo_to(dve, "g3b", 3)
            da.dve(dve, link)
            sa.dve(dve, link)
            for u in range(DIFF_H):
                L.wait_drained(dve, f"daO{u}")
            ya = heads(M.ya[:, :, :], DIFF_H)
            link(tt(M.scratch[:, :], flat(M.ya[:, :, :]), flat(M.ya[:, :, :]), ALU.mult))
            link(dve.tensor_reduce(st[:, 130:138], M.scratch[:, :].rearrange("p (n d) -> p n d", d=P), AX_X, ALU.add))
            dve.tensor_scalar(st[:, 130:138], st[:, 130:138], 1.0 / P, LN_EPS, ALU.mult, ALU.add)\
               .then_inc(sig["ya_var"], 1)
            dve.wait_ge(sig["ya_root"], 1)
            link(dve.reciprocal(st[:, 130:138], st[:, 130:138]))
            link(tt(ya, ya, over_heads(st[:, 130:138].rearrange("p (t h) -> p t h", t=T), DIFF_H, P), ALU.mult))
            tt(ya, ya, over_heads(M.sub[:, :], DIFF_H, P), ALU.mult).then_inc(sig["ya_normed"], 1)
            for g in range(4):
                L.wait_drained(dve, f"g{g}")
            for c in range(2):
                ST.lo_to(dve, f"bs{c}", 1)
                lot = L.wait_filled(dve, f"bs{c}")
                gate = M.gates[:, :, D + c * 512:D + (c + 1) * 512]
                ins = tt(merged[:, :, c * 512:(c + 1) * 512], K.ps[lot][:, :, :], gate, ALU.mult)
                ins.then_inc(L.drained(f"bs{c}"), 1)
            dve_lo(K, L, dve, "yT", flat(M.yT_lo[:, :, :]), flat(M.yT_hi[:, :, :]))
            for c in range(2):
                ST.lo_to(dve, f"bd{c}", 1)
                lot = L.wait_filled(dve, f"bd{c}")
                gate = M.gates[:, :, c * 512:(c + 1) * 512]
                tt(gate, K.ps[lot][:, :, :], gate, ALU.mult).then_inc(L.drained(f"bd{c}"), 1)
                L.wait_drained(dve, f"bd{c}")
                L.wait_drained(dve, f"bs{c}")
                last = tt(merged[:, :, c * 512:(c + 1) * 512], merged[:, :, c * 512:(c + 1) * 512], gate, ALU.add)
                if c == 0:
                    link(last)
            last.then_inc(sig["merged"], 1)
            ST.lo_to(dve, "wo01")
            dve_lo(K, L, dve, "mT0", flat(M.hT_lo[:, 0:4, :]), flat(M.hT_hi[:, 0:4, :]))
            dve_lo(K, L, dve, "mT1", flat(M.hT_lo[:, 4:8, :]), flat(M.hT_hi[:, 4:8, :]))
            ST.lo_to(dve, "wo11", 1)
            for c in range(2):
                lot = L.wait_filled(dve, f"wo{c}")
                x = K.x[:, :, c * 512:(c + 1) * 512]
                dve.scalar_tensor_tensor(x, x, ALPHA, K.ps[lot][:, :, :], ALU.mult, ALU.add)\
                   .then_inc(L.drained(f"wo{c}"), 1)
            dve_lo(K, L, dve, "pT", flat(M.pT_lo[:, :, :]), flat(M.pT_hi[:, :, :]), lambda lot: K.ps[lot][:, 0, :])
            for c in range(2):
                L.wait_drained(dve, f"wo{c}")
            norm_dve(K, dve, link, "n1", M.ln_g, M.ln_b)
            ST.lo_to(dve, "wo11", 3)
            dve_lo(K, L, dve, "nT0", flat(M.hT_lo[:, 0:4, :]), flat(M.hT_hi[:, 0:4, :]))
            dve_lo(K, L, dve, "nT1", flat(M.hT_lo[:, 4:8, :]), flat(M.hT_hi[:, 4:8, :]))
            ST.lo_to(dve, "route", 3)
            lot = L.wait_filled(dve, "rt")
            tt(M.logit[:, :, :], K.ps[lot][:, :, 0:N_ROUTE],
               M.route_b[:, :].unsqueeze(1).to_broadcast([P, T, N_ROUTE]), ALU.add).then_inc(L.drained("rt"), 1)
            L.wait_drained(dve, "rt")

            def first_of(out, v, top, index, n):
                small = M.r[:, 7, :, 0:n]
                link(tt(small, v, top.to_broadcast([P, T, n]), ALU.is_equal))
                link(dve.scalar_tensor_tensor(small, small, -100.0, index.unsqueeze(1).to_broadcast([P, T, n]),
                                              ALU.mult, ALU.add))
                link(dve.tensor_reduce(st[:, 146:148], small, AX_X, ALU.min))
                link(tt(out, small, st[:, 146:148].unsqueeze(2).to_broadcast([P, T, n]), ALU.is_equal))

            def top_of(cols, v):
                link(dve.tensor_reduce(st[:, cols], v, AX_X, ALU.max))
                return st[:, cols].unsqueeze(2)

            g = M.logit[:, :, 0:N_G]
            hot = M.r[:, 1, :, 0:N_G]
            top = top_of(slice(140, 142), g)
            tt(M.r[:, 0, :, 0:N_G], g, top.to_broadcast([P, T, N_G]), ALU.subtract).then_inc(sig["group_shift"], 1)
            first_of(hot, g, top, M.iota[:, 0:N_G], N_G)
            e = M.logit[:, :, N_G:N_ROUTE].rearrange("p t (g e) -> p t g e", g=N_G)
            r32 = M.r32[:, :, :].rearrange("p t (g e) -> p t g e", g=N_G)
            link(tt(r32, e, hot.unsqueeze(3).to_broadcast([P, T, N_G, E_G]), ALU.mult))
            el, one, two, pe_ = M.r[:, 2, :, :], M.r[:, 4, :, :], M.r[:, 5, :, :], M.r[:, 3, :, :]
            link(dve.tensor_reduce(el, M.r32[:, :, :].rearrange("p t (g e) -> p t e g", g=N_G), AX_X, ALU.add))
            top = top_of(slice(142, 144), el)
            tt(pe_, el, top.to_broadcast([P, T, E_G]), ALU.subtract).then_inc(sig["expert_shift"], 1)
            first_of(one, el, top, M.iota[:, 4:12], E_G)
            link(dve.scalar_tensor_tensor(el, one, NEG, el, ALU.mult, ALU.add))
            top = top_of(slice(144, 146), el)
            first_of(two, el, top, M.iota[:, 4:12], E_G)
            link(tt(one, one, two, ALU.add))
            dve.wait_ge(sig["group_exps"], 1)
            link(dve.tensor_reduce(st[:, 148:150], M.r[:, 0, :, 0:N_G], AX_X, ALU.add))
            dve.wait_ge(sig["expert_exps"], 1)
            link(tt(one, one, pe_, ALU.mult))
            link(dve.tensor_reduce(st[:, 150:152], one, AX_X, ALU.add))
            link(tt(st[:, 148:150], st[:, 148:150], st[:, 150:152], ALU.mult))
            link(dve.reciprocal(st[:, 148:150], st[:, 148:150]))
            link(tt(one, one, st[:, 148:150].unsqueeze(2).to_broadcast([P, T, E_G]), ALU.mult))
            comb = M.comb[:, :, :].rearrange("p t (g e) -> p t g e", g=N_G)
            link(tt(comb, hot.unsqueeze(3).to_broadcast([P, T, N_G, E_G]),
                    one.unsqueeze(2).to_broadcast([P, T, N_G, E_G]), ALU.mult))
            ST.lo_to(dve, "pg11", 2)
            for c in range(2):
                lot = L.wait_filled(dve, f"pl{c}")
                L.wait_drained(dve, f"pg{c}")
                gate = M.pgate[:, c, :, :]
                tt(gate, gate, K.ps[lot][:, :, :], ALU.mult).then_inc(L.drained(f"pl{c}"), 1)
                L.wait_drained(dve, f"pl{c}")
                x = K.x[:, :, c * 512:(c + 1) * 512]
                last = dve.scalar_tensor_tensor(x, x, ALPHA, gate, ALU.mult, ALU.add)
            link(last)
            ST.lo_to(dve, "G1")

            def product(e, i):
                lot = L.use[f"H{e}"][0]
                dve.wait_ge(sig["silu"], later(e + 1, i, 2))
                if e or i is not None:
                    dve.wait_ge(sig["h_lo"], later(e, i, 2))
                dve.tensor_tensor(flat(K.h), flat(M.act[:, 0, :, :]), K.ps[lot][:, 1, :], ALU.mult)\
                   .then_inc(L.drained(f"H{e}"), 1)
                L.wait_drained(dve, f"H{e}", i, 1)

            def add(e, i, t):
                w = M.comb[:, t, bass.ds(true_step(e, i), 1)]
                return dve.scalar_tensor_tensor(K.x[:, t, :], flat(K.ps[L.use[f"Y{e}t{t}"][0]][:, :, :]), w,
                                                K.x[:, t, :], ALU.mult, ALU.add)

            ffn_dve(K, L, ST, dve, N_E, lambda e, i: None, product, add, (M.h_hi, M.h_lo), None, None)
            norm_dve(K, dve, link, "n2", M.ln2_g, M.ln2_b)



INS = ["x", "attn_norm_g", "w_in", "mla_q_norm_g", "mla_w_uq", "mla_kv_norm_g", "mla_w_ukv", "mla_q_head_g",
       "mla_k_head_g", "gqa_q_head_g", "gqa_k_head_g", "pool_w", "pool_scale", "w_branch_mla", "w_branch_gqa",
       "w_branch_pool", "w_out", "ffn_norm_g", "ffn_w_up", "ffn_conv_w", "ffn_conv_b", "ffn_w_down", "p_2",
       "positions_2", "w_in_2", "diff_lambda_2", "diff_subln_g_2", "w_branch_diff_2", "w_branch_dsa_2", "w_out_2",
       "ln1_g_2", "ln1_b_2", "w_route_group_2", "b_route_group_2", "w_route_expert_2", "b_route_expert_2",
       "w_exp_gate_2", "w_exp_up_2", "w_exp_down_2", "w_ple_2", "w_ple_gate_2", "ln2_g_2", "ln2_b_2"]


def axial_tables(rot):
    row = np.repeat(np.arange(S // 64, dtype=np.float32), 64)
    col = np.tile(np.arange(64, dtype=np.float32), S // 64)
    n = rot // 4
    inv = (np.float32(10000.0) ** (-np.arange(n, dtype=np.float32) / np.float32(n))).astype(np.float32)
    ang = np.concatenate([row[:, None] * inv, col[:, None] * inv], axis=-1)
    return np.cos(ang).astype(np.float32), np.sin(ang).astype(np.float32)


def by_partition(a):
    return np.ascontiguousarray(a.reshape(T, P, -1).transpose(1, 0, 2))


def constants():
    rope = np.concatenate([*axial_tables(ROPE), *axial_tables(HD)], axis=-1)
    window = np.zeros((S, POOL_G, S), np.float32)
    for g, w in enumerate(POOL_WINDOWS):
        for t in range(S):
            lo, hi = max(t - w // 2, 0), min(t + w - w // 2, S)
            window[lo:hi, g, t] = np.float32(1) / np.float32(hi - lo)
            window[t, g, t] -= 1
    key, query = np.arange(S)[None, :], np.arange(S)[:, None]
    causal = np.where(key <= query, 0.0, NEG).astype(np.float32)
    inv = (1.0 / (np.float32(500000.0) ** (np.arange(0, ROT, 2, dtype=np.float32) / np.float32(ROT))))
    return {"c_rope": by_partition(rope), "c_window": by_partition(window.reshape(S, -1)).reshape(P, T, POOL_G * S),
            "c_ident": np.eye(P, dtype=np.float32), "c_causal": by_partition(causal),
            "c_inv_freq": inv.astype(np.float32)[None, :],
            "c_lam_init": np.array([[0.8 - 0.6 * np.exp(-0.3 * i), 0.2 + 0.6 * np.exp(-0.3 * i)]
                                    for i in range(DEPTH)], np.float32),
            "c_groups": np.arange(N_G, dtype=np.float32)[None, :], "c_experts": np.arange(E_G, dtype=np.float32)[None, :]}


def build(nc, A, out):
    with ExitStack() as ctx:
        K = Core(nc, ctx, A)
        one = OneTiles(K)
        two = TwoTiles(K)
        with nc.Block() as block:

            @block.sync
            def _(sp):
                sp.dma_start(K.x[:, :, :], A["x"][0].rearrange("(t p) d -> p t d", p=P)).then_inc(K.sig["start"], 16)
                sp.dma_start(K.ident[:, :], A["c_ident"]).then_inc(K.sig["start"], 16)
                sp.dma_start(K.rope[:, :, :], A["c_rope"]).then_inc(K.sig["start"], 16)
                sp.wait_ge(K.sig["start"], 48)

        with nc.Fori(0, DEPTH) as layer:
            block_one(K, one, layer)
            nc.all_engine_barrier(sems_to_clear=K.sig.span())
        rotation_tables(K, two)
        nc.all_engine_barrier(sems_to_clear=K.sig.span())
        with nc.Fori(0, DEPTH) as layer:
            block_two(K, two, layer)
            nc.all_engine_barrier(sems_to_clear=K.sig.span())
        with nc.Block() as block:

            @block.sync
            def _(sp):
                sp.dma_start(out[0].rearrange("(t p) d -> p t d", p=P), K.x[:, :, :]).then_inc(K.sig["stored"], 16)
                sp.wait_ge(K.sig["stored"], 16)


def kernel(**inputs):
    import concourse.bacc as bacc
    from concourse.bass_utils import run_bass_kernel_spmd

    nc = bacc.Bacc("TRN2", target_bir_lowering=False, num_devices=1)
    arrays = {name: np.ascontiguousarray(inputs[name]) for name in INS} | constants()
    A = {name: nc.dram_tensor(name, a.shape, mybir.dt.from_np(a.dtype), kind="ExternalInput").ap()
         for name, a in arrays.items()}
    out = nc.dram_tensor("out", (1, S, D), F32, kind="ExternalOutput").ap()
    build(nc, A, out)
    r = run_bass_kernel_spmd(nc, [arrays], core_ids=[0])
    return r.results[0]["out"]
```

```python
from contextlib import ExitStack

import numpy as np

import concourse.bass as bass
from concourse import mybir

F32 = mybir.dt.float32
F32R = mybir.dt.float32r
I32 = mybir.dt.int32
ACT = mybir.ActivationFunctionType
ALU = mybir.AluOpType
AX_X = mybir.AxisListType.X

P = 128
S = 256
T = S // P
D = 1024
KD = D // P
DEPTH = 2
EPS = 1e-6
LN_EPS = 1e-5

MLA_H, MLA_QL, MLA_KVL, NOPE, ROPE, MLA_V = 8, 256, 128, 64, 32, 64
MLA_QK = NOPE + ROPE
GQA_H, GQA_KV, HD = 8, 2, 64
POOL_WINDOWS = (2, 4, 8, 16)
POOL_G = 4
D_FF = 2816
FF_STEPS = D_FF // S
LATENT = MLA_QL + MLA_KVL + ROPE
C_GQ = LATENT
C_GK = C_GQ + GQA_H * HD
C_GV = C_GK + GQA_KV * HD
C_POOL = C_GV + GQA_KV * HD
C_GATE = C_POOL + POOL_G * P

DIFF_H, DSA_H, IDX_H = 4, 8, 8
TOPK = 64
ROT = HD // 4
N_G, E_G, D_E = 4, 8, 256
N_E = N_G * E_G
ALPHA = (2 * DEPTH) ** 0.25
NEG = -1e30
PICKED = -3e38
C_DQ, C_DK, C_DV, C_SQ, C_SK, C_SV, C_IQ, C_IK = 0, 512, 1024, 1536, 2048, 2560, 3072, 3584
C_IW = C_IK + HD
C_GA = C_IW + IDX_H
C_ATT = C_GA

RING = 3
CHUNK = 2048
FFN_TURN = (6, 2, (1, 1, 2, 2))
WINDOW_TURN = (24, 15, (4, 4, 1, 10))


def later(value, i, per):
    return value if i is None else i * per + value


class Signals:

    def __init__(self, nc, ctx):
        self.nc, self.ctx, self.made = nc, ctx, {}

    def __getitem__(self, name):
        if name not in self.made:
            self.made[name] = self.ctx.enter_context(self.nc.semaphore(name))
        return self.made[name]

    def span(self):
        nums = [s.num for s in self.made.values()]
        return range(min(nums), max(nums) + 1)


class Chain:

    def __init__(self, eng, done):
        self.eng, self.done, self.n, self.i, self.per = eng, done, 0, None, 0

    def __call__(self, ins):
        self.n += 1
        ins.then_inc(self.done, 1)
        self.eng.wait_ge(self.done, later(self.n, self.i, self.per))

    def enter(self, i, per):
        self.i, self.per, self.n0 = i, per, self.n

    def leave(self, turns):
        assert self.n - self.n0 == self.per, (self.n - self.n0, self.per)
        self.n = self.n0 + self.per * turns
        self.i = None


class Lots:

    def __init__(self, order, filled, drained):
        count = [0] * len(filled)
        self.filled_s, self.drained_s, self.use = filled, drained, {}
        for name, lot in order:
            self.use[name] = (lot, count[lot])
            count[lot] += 1

    def claim(self, pe, name, i=None, per=0):
        self.wait_before(pe, name, i, per)
        return self.use[name][0]

    def filled(self, name):
        return self.filled_s[self.use[name][0]]

    def drained(self, name):
        return self.drained_s[self.use[name][0]]

    def wait_filled(self, eng, name, i=None, per=0):
        lot, n = self.use[name]
        eng.wait_ge(self.filled_s[lot], later(n + 1, i, per))
        return lot

    def wait_before(self, eng, name, i=None, per=0):
        lot, n = self.use[name]
        if n:
            eng.wait_ge(self.drained_s[lot], later(n, i, per))

    def wait_drained(self, eng, name, i=None, per=0):
        lot, n = self.use[name]
        eng.wait_ge(self.drained_s[lot], later(n + 1, i, per))


class Stream:

    def __init__(self, K, L, names, widths, ends, loads, turn, free_after, wide_from=None, fourth=None,
                 by_pool=()):
        self.K, self.L, self.names, self.width, self.ends = K, L, names, widths, ends
        self.turn_chunks, self.turn_used, self.turn_lots = turn
        self.free_after, self.fourth = free_after, fourth
        self.at = {n: j for j, n in enumerate(names) if n}
        self.loads = loads
        self.landed, self.ready, self.used, self.before = {}, {}, {}, {}
        self.raw_slot, self.raw_free = {}, {}
        slot, last, ready, used = [0] * (RING + 1), [None] * RING, 0, 0
        wide = self.at[wide_from] if wide_from else len(names)
        for j, n in enumerate(names):
            if n is None:
                continue
            r = j % RING
            q = j - wide
            raw = r if q < 0 else ((wide + q % 4) % RING if q % 4 < RING else RING)
            slot[raw] += 16 * loads.get(n, 1)
            ready += 1
            self.landed[n], self.ready[n], self.before[n] = slot[raw], ready, last[r]
            self.raw_slot[n] = raw
            self.raw_free[n] = (self.ready[last[r]] if last[r] else 0) if q < RING else ready - 4
            if n not in ends:
                used += 1
                self.used[n] = used
            last[r] = n
        self.ring = RING if wide_from is None else RING + 1
        self.next_hi = self.next_lo = 0
        self.by_pool = by_pool

    def slot(self, name):
        return self.at[name] % RING

    def raw(self, name):
        r = self.raw_slot[name]
        return self.fourth[:, :] if r == RING else self.K.raw[:, r, :]

    def arrived(self, name):
        return self.K.landed[self.raw_slot[name]]

    def columns(self, name):
        return self.width.get(name, CHUNK)

    def wait_used(self, eng, name, i=None):
        if name in self.ends:
            lot = self.L.use[self.ends[name]][0]
            self.L.wait_filled(eng, self.ends[name], i, self.turn_lots[lot])
        else:
            eng.wait_ge(self.K.sig["chunk_used"], later(self.used[name], i, self.turn_used))

    def may_load(self, sp, name, i=None):
        if self.raw_free[name]:
            sp.wait_ge(self.K.sig["lo_ready"], later(self.raw_free[name], i, self.turn_chunks))

    def split_hi(self, act, name, i=None):
        K, r, n = self.K, self.slot(name), self.columns(name)
        act.wait_ge(self.arrived(name), later(self.landed[name], i, 16 * self.turn_chunks // self.ring))
        for other in self.free_after.get(name, [self.before[name]] if self.before[name] else []):
            if other in self.at:
                self.wait_used(act, other, i)
            else:
                self.L.wait_filled(act, other, i, self.turn_lots[self.L.use[other][0]])
        act.activation(K.hi[:, r, 0:n], self.raw(name)[:, 0:n], ACT.Copy).then_inc(K.sig["hi_ready"], 1)

    def split_lo(self, dve, name, i=None):
        K, r, n = self.K, self.slot(name), self.columns(name)
        dve.wait_ge(K.sig["hi_ready"], later(self.ready[name], i, self.turn_chunks))
        dve.tensor_tensor(K.lo[:, r, 0:n], self.raw(name)[:, 0:n], K.hi[:, r, 0:n].bitcast(F32),
                          ALU.subtract).then_inc(K.sig["lo_ready"], 1)

    def hi_to(self, act, name, n=0):
        while self.next_hi <= min(self.at[name] + n, len(self.names) - 1):
            if self.names[self.next_hi]:
                self.split_hi(act, self.names[self.next_hi])
            self.next_hi += 1

    def lo_to(self, dve, name, n=0):
        while self.next_lo <= min(self.at[name] + n, len(self.names) - 1):
            chunk = self.names[self.next_lo]
            if chunk and chunk not in self.by_pool:
                self.lo_in_order(dve, chunk, self.names[self.next_lo - 1] in self.by_pool)
            self.next_lo += 1

    def lo_by_pool(self, pool):
        for chunk in self.by_pool:
            self.lo_in_order(pool, chunk, self.names[self.at[chunk] - 1] not in self.by_pool)

    def lo_in_order(self, eng, chunk, after_other):
        if after_other and self.ready[chunk] > 1:
            eng.wait_ge(self.K.sig["lo_ready"], self.ready[chunk] - 1)
        self.split_lo(eng, chunk)

    def parts(self, pe, name, i=None):
        K, r = self.K, self.slot(name)
        pe.wait_ge(K.sig["lo_ready"], later(self.ready[name], i, self.turn_chunks))
        return K.hi[:, r, :], K.lo[:, r, :]

    def done(self, last, name):
        if name not in self.ends:
            last.then_inc(self.K.sig["chunk_used"], 1)


def mm3(pe, out, a, b, start, stop):
    pe.matmul(out, a[0], b[0], start=start, stop=False)
    pe.matmul(out, a[0], b[1], start=False, stop=False)
    return pe.matmul(out, a[1], b[0], start=False, stop=stop)


class Core:

    def __init__(self, nc, ctx, A):
        self.nc, self.A = nc, A
        self.sig = Signals(nc, ctx)
        self.base = self.floor = (nc.sbuf_base + 63) // 64 * 64
        self.limit = nc.sbuf_top
        self.raw = self.tile("raw", [P, RING, CHUNK])
        self.hi = self.tile("w_hi", [P, RING, CHUNK], F32R)
        self.lo = self.tile("w_lo", [P, RING, CHUNK], F32R)
        self.x = self.tile("x", [P, T, D])
        self.ident = self.tile("ident", [P, P])
        self.rope = self.tile("rope", [P, T, 96])
        self.stat = self.tile("stat", [P, 256])
        self.floor = self.base
        self.ps = [ctx.enter_context(nc.psum_tensor(f"lot{n}", [P, 2, 512], F32)) for n in range(4)]
        self.landed = [self.sig[f"landed{r}"] for r in range(RING + 1)]
        self.filled = [self.sig[f"filled{n}"] for n in range(4)]
        self.drained = [self.sig[f"drained{n}"] for n in range(4)]

    def tile(self, name, shape, dtype=F32):
        t = self.nc.alloc_sbuf_tensor_at(name, shape, dtype, offset=self.base)
        self.base += (4 * int(np.prod(shape[1:])) + 31) // 32 * 32
        assert self.base <= self.limit, (name, self.base, self.limit)
        return t

    def over(self, name, shape, offset, dtype=F32):
        return self.nc.alloc_sbuf_tensor_at(name, shape, dtype, offset=offset)


def token_product(K, ST, pe, out, xT, name, start, stop, k0, kn, n, tiles=range(T), c0=0, cn=None, i=None):
    w = [v[:, 0:kn * n].rearrange("p (k c) -> p k c", k=kn) for v in ST.parts(pe, name, i)]
    cn = n if cn is None else cn
    for t in tiles:
        for k in range(kn):
            last = mm3(pe, out(t), [v[:, k0 + k, t * P:(t + 1) * P] for v in xT],
                       [v[:, k, c0:c0 + cn] for v in w], start and k == 0, stop and k == kn - 1)
    return last


def project(K, L, ST, pe, name, chunks, n, xT, kn=4, turned=()):
    lot = L.claim(pe, name)
    for c, chunk in enumerate(chunks):
        for half in turned[c:c + 1] if len(chunks) > 1 else turned:
            L.wait_drained(pe, half)
        last = token_product(K, ST, pe, lambda t: K.ps[lot][:, t, 0:n], xT, chunk, c == 0, c == len(chunks) - 1,
                             c * kn, kn, n)
        ST.done(last, chunk)
    last.then_inc(L.filled(name), 1)


def transpose_x(K, L, pe, src, names, normed=None):
    for half, name in enumerate(names):
        if normed is not None:
            pe.wait_ge(normed, half + 1)
        lot = L.claim(pe, name)
        dst = K.ps[lot][:, :, :].rearrange("p a b -> p (a b)").rearrange("p (k s) -> p k s", k=4)
        for kk in range(4):
            for t in range(T):
                last = pe.transpose(dst[:, kk, t * P:(t + 1) * P],
                                    src[:, t, (4 * half + kk) * P:(4 * half + kk + 1) * P], K.ident[:, :])
        last.then_inc(L.filled(name), 1)


def flat(ap):
    return ap.rearrange("p a b -> p (a b)")


def act_hi(K, L, act, name, dst, src=None):
    lot = L.wait_filled(act, name)
    act.activation(dst, flat(K.ps[lot][:, :, :]) if src is None else src(lot), ACT.Copy)\
       .then_inc(K.sig[f"hi_{name}"], 1)


def dve_lo(K, L, dve, name, dst, hi, src=None):
    lot = L.use[name][0]
    dve.wait_ge(K.sig[f"hi_{name}"], 1)
    dve.tensor_tensor(dst, flat(K.ps[lot][:, :, :]) if src is None else src(lot), hi.bitcast(F32),
                      ALU.subtract).then_inc(L.drained(name), 1)


class Attention:

    def __init__(self, K, L, tag, units, q, k, v, scale, p, pt, mask=None, out=None):
        self.K, self.L, self.tag, self.units = K, L, tag, units
        self.q, self.k, self.v, self.scale, self.mask = q, k, v, scale, mask
        self.p, self.pt, self.out = p, pt, out
        self.keys = (P, S) if mask is not None else (S, S)

    @staticmethod
    def lots(tag, units, then=None, begun=False):
        order = [] if begun else [(f"{tag}S0", 0), (f"{tag}S1", 1)]
        for u in range(units):
            order.append((f"{tag}T{u}", 2))
            if u + 2 < units:
                order.append((f"{tag}S{u + 2}", u % 2))
            elif then:
                order.append((f"{then}S{u + 2 - units}", u % 2))
            order.append((f"{tag}O{u}", 3))
        return order

    def scores(self, pe, u):
        lot = self.L.claim(pe, f"{self.tag}S{u}")
        s = flat(self.K.ps[lot][:, :, :]).rearrange("p (h t k) -> p h t k", h=2, t=T)
        for h in range(2):
            for t in range(T):
                n = self.keys[t]
                last = pe.matmul(s[:, h, t, 0:n], self.q(u, h)[:, t * P:(t + 1) * P], self.k(u, h)[:, 0:n],
                                 start=True, stop=True)
        last.then_inc(self.L.filled(f"{self.tag}S{u}"), 1)

    def pe(self, pe, then=None, begun=False):
        K, L, tag = self.K, self.L, self.tag
        if not begun:
            self.scores(pe, 0)
            self.scores(pe, 1)
        for u in range(self.units):
            if u + 2 < self.units:
                self.scores(pe, u + 2)
            elif then:
                then.scores(pe, u + 2 - self.units)
            pe.wait_ge(K.sig[f"{tag}_probs"], u + 1)
            L.claim(pe, f"{tag}T{u}")
            self.pe_turn(pe, u).then_inc(L.filled(f"{tag}T{u}"), 1)
            L.wait_drained(pe, f"{tag}T{u}")
            L.claim(pe, f"{tag}O{u}")
            self.pe_out(pe, u).then_inc(L.filled(f"{tag}O{u}"), 1)

    def pe_turn(self, pe, u):
        p = self.p[:, u % 2, :].rearrange("p (h t k) -> p h t k", h=2, t=T)
        d = flat(self.K.ps[2][:, :, :]).rearrange("p (h c q) -> p h c q", h=2, c=T)
        for h in range(2):
            for t in range(T):
                for c in range(self.keys[t] // P):
                    last = pe.transpose(d[:, h, c, t * P:(t + 1) * P], p[:, h, t, c * P:(c + 1) * P],
                                        self.K.ident[:, :])
        return last

    def pe_out(self, pe, u):
        pt = self.pt[:, :].rearrange("p (h c q) -> p h c q", h=2, c=T)
        for h in range(2):
            for c in range(T):
                q0 = 0 if self.keys[0] > c * P else P
                last = pe.matmul(self.K.ps[3][h * HD:(h + 1) * HD, 0, q0:S], self.v(u, h, c), pt[:, h, c, q0:S],
                                 start=c == 0, stop=c == T - 1)
        return last

    def copy_turned(self, act):
        src, dst = (a.rearrange("p (h c q) -> p h c q", h=2, c=T)
                    for a in (flat(self.K.ps[2][:, :, :]), self.pt[:, 0:2 * T * S]))
        return self.copy_seen(act, src, dst)

    def copy_seen(self, act, src, dst):
        if self.mask is None:
            return act.activation(dst, src, ACT.Copy)
        act.activation(dst[:, :, 0, :], src[:, :, 0, :], ACT.Copy)
        return act.activation(dst[:, :, 1, P:S], src[:, :, 1, P:S], ACT.Copy)

    def seen(self, *tiles):
        if self.mask is None:
            return [[a for a in tiles]]
        return [[a[:, :, t, 0:n] for a in tiles] for t, n in enumerate(self.keys)]

    def act_out(self, act, u):
        self.L.wait_filled(act, f"{self.tag}O{u}")
        act.activation(self.out[0][:, u, :], self.K.ps[3][:, 0, 0:S], ACT.Copy)\
           .then_inc(self.K.sig[f"{self.tag}_hi"], 1)

    def dve_out(self, dve, u):
        dve.wait_ge(self.K.sig[f"{self.tag}_hi"], u + 1)
        dve.tensor_tensor(self.out[1][:, u, :], self.K.ps[3][:, 0, 0:S], self.out[0][:, u, :].bitcast(F32),
                          ALU.subtract).then_inc(self.L.drained(f"{self.tag}O{u}"), 1)

    def weigh(self, dve, link, u, inv):
        p = self.p[:, u % 2, :].rearrange("p (h t k) -> p h t k", h=2, t=T)
        inv = inv.rearrange("p (h t) -> p h t", h=2).unsqueeze(3).to_broadcast([P, 2, T, S])
        for a, b in self.seen(p, inv):
            last = dve.tensor_tensor(a, a, b, ALU.mult)
        return last

    def exps(self, act, u, last_turned=None):
        K, L, tag = self.K, self.L, self.tag
        sums = K.stat[:, 200:208].rearrange("p (b n) -> p b n", b=2)
        neg = K.stat[:, 208:216].rearrange("p (b n) -> p b n", b=2)
        act.wait_ge(K.sig[f"{tag}_negmax"], u + 1)
        if u >= 2 or last_turned:
            L.wait_filled(act, last_turned or f"{tag}T{u - 2}")
        lot = L.use[f"{tag}S{u}"][0]
        p = self.p[:, u % 2, :].rearrange("p (n k) -> p n k", n=4)
        s = p if self.mask is not None else flat(K.ps[lot][:, :, :]).rearrange("p (n k) -> p n k", n=4)
        for n in range(4):
            k = self.keys[n % T]
            last = act.activation(p[:, n, 0:k], s[:, n, 0:k], ACT.Exp, bias=neg[:, u % 2, n:n + 1],
                                  scale=1.0 if self.mask is not None else self.scale,
                                  accum_out=sums[:, u % 2, n:n + 1])
        last.then_inc(K.sig[f"{tag}_exps"] if self.mask is not None else L.drained(f"{tag}S{u}"), 1)

    def act(self, act, then=None, begun=False):
        K, L, tag = self.K, self.L, self.tag

        def turned(u):
            L.wait_filled(act, f"{tag}T{u}")
            if u:
                L.wait_filled(act, f"{tag}O{u - 1}")
            self.copy_turned(act).then_inc(L.drained(f"{tag}T{u}"), 1)

        if not begun:
            self.exps(act, 0)
        for u in range(self.units):
            if u + 1 < self.units:
                self.exps(act, u + 1, self.turned_before(u + 1, begun))
            elif then:
                then.exps(act, 0, f"{tag}T{u - 1}")
            turned(u)
            if u:
                self.act_out(act, u - 1)
        self.act_out(act, self.units - 1)

    def turned_before(self, u, begun):
        return f"{begun[0]}T{begun[1] - 1}" if u == 1 and begun else None

    def maxima(self, dve, link, u, last_turned=None):
        K, L, tag = self.K, self.L, self.tag
        neg = K.stat[:, 208:216].rearrange("p (b n) -> p b n", b=2)
        top = K.stat[:, 216:220]
        lot = L.wait_filled(dve, f"{tag}S{u}")
        s = flat(K.ps[lot][:, :, :])
        if self.mask is not None:
            if u >= 2 or last_turned:
                L.wait_filled(dve, last_turned or f"{tag}T{u - 2}")
            p = self.p[:, u % 2, :]
            for a, b, m in self.seen(*(v.rearrange("p (h t k) -> p h t k", h=2, t=T) for v in (p, s)), self.mask):
                last = dve.scalar_tensor_tensor(a, b, self.scale, m, ALU.mult, ALU.add)
            last.then_inc(L.drained(f"{tag}S{u}"), 1)
            L.wait_drained(dve, f"{tag}S{u}")
            s = p
        if u:
            dve.wait_ge(K.sig[f"{tag}_negmax"], u)
        if self.mask is None:
            last = dve.tensor_reduce(top, s.rearrange("p (n k) -> p n k", n=4), AX_X, ALU.max)
        else:
            for t, (a,) in enumerate(self.seen(s.rearrange("p (h t k) -> p h t k", h=2, t=T))):
                last = dve.tensor_reduce(top.rearrange("p (h t) -> p h t", h=2)[:, :, t], a, AX_X, ALU.max)
        link(last)
        dve.tensor_scalar(neg[:, u % 2, :], top, -1.0 if self.mask is not None else -self.scale, None,
                          ALU.mult).then_inc(K.sig[f"{tag}_negmax"], 1)

    def dve(self, dve, link, then=None, begun=False):
        K, L, tag = self.K, self.L, self.tag
        sums = K.stat[:, 200:208].rearrange("p (b n) -> p b n", b=2)
        inv = K.stat[:, 220:224]

        def normalise(u):
            if self.mask is not None:
                dve.wait_ge(K.sig[f"{tag}_exps"], u + 1)
            else:
                L.wait_drained(dve, f"{tag}S{u}")
            if u:
                dve.wait_ge(K.sig[f"{tag}_probs"], u)
            link(dve.reciprocal(inv, sums[:, u % 2, :]))
            self.weigh(dve, link, u, inv).then_inc(K.sig[f"{tag}_probs"], 1)

        if not begun:
            self.maxima(dve, link, 0)
        for u in range(self.units):
            if u + 1 < self.units:
                self.maxima(dve, link, u + 1, self.turned_before(u + 1, begun))
            elif then:
                dve.wait_ge(K.sig[f"{tag}_negmax"], u + 1)
                then.maxima(dve, link, 0, f"{tag}T{u - 1}")
            normalise(u)
            if u:
                self.dve_out(dve, u - 1)
        self.dve_out(dve, self.units - 1)



def ffn_chunks(steps):
    names = ["G0", "U0", None]
    for e in range(1, steps):
        names += [f"G{e}", f"U{e}", f"D{e - 1}"]
    return names + [f"D{steps - 1}"]


def ffn_ends(steps):
    return {f"U{e}": f"H{e}" for e in range(steps)} | {f"D{e}": f"Y{e}t1" for e in range(steps)}


def ffn_lots(steps):
    order = [("H0", 0)]
    for e in range(1, steps):
        order += [(f"H{e}", e % 2), (f"Y{e - 1}t0", 2), (f"Y{e - 1}t1", 3)]
    return order + [(f"Y{steps - 1}t0", 2), (f"Y{steps - 1}t1", 3)]


def ffn_walk(eng, steps, step, enter=None, leave=None):
    turns = (steps - 3) // 2
    step(0, None)
    with eng.Fori(0, turns) as i:
        if enter:
            enter(i)
        step(1, i)
        step(2, i)
    if leave:
        leave(turns)
    for e in range(1 + 2 * turns, steps - 1):
        step(e, None)


def true_step(e, i):
    return e if i is None else 2 * i + e


def ffn_load(K, ST, sp, steps, source):
    def load(name, i=None):
        ST.may_load(sp, name, i)
        e = true_step(int(name[1:]), i)
        sp.dma_start(ST.raw(name).rearrange("p (k c) -> p k c", k=T if name[0] == "D" else KD),
                     source(name[0], e)).then_inc(ST.arrived(name), 16)

    load("G0")
    load("U0")

    def step(e, i):
        load(f"G{e + 1}", i)
        load(f"U{e + 1}", i)
        load(f"D{e}", i)

    ffn_walk(sp, steps, step)
    load(f"D{steps - 1}")


def ffn_pe(K, L, ST, pe, steps, xT, h):
    def hidden(e, i=None):
        lot = L.claim(pe, f"H{e}", i, 1)
        for bank, name in enumerate((f"G{e}", f"U{e}")):
            w = [v[:, 0:CHUNK].rearrange("p (k c) -> p k c", k=KD) for v in ST.parts(pe, name, i)]
            for f in range(2):
                for k in range(KD):
                    last = mm3(pe, K.ps[lot][:, bank, f * S:(f + 1) * S], [v[:, k, f * P:(f + 1) * P] for v in w],
                               [v[:, k, :] for v in xT], k == 0, k == KD - 1)
            ST.done(last, name)
        last.then_inc(L.filled(f"H{e}"), 1)

    def down(e, i=None):
        pe.wait_ge(K.sig["h_lo"], later(e + 1, i, 2))
        for t in range(T):
            lot = L.claim(pe, f"Y{e}t{t}", i, 2)
            w = [v[:, 0:CHUNK].rearrange("p (k c) -> p k c", k=T) for v in ST.parts(pe, f"D{e}", i)]
            for n in range(2):
                for k in range(T):
                    last = mm3(pe, K.ps[lot][:, n, :], [v[:, e % 2, k, t * P:(t + 1) * P] for v in h],
                               [v[:, k, n * 512:(n + 1) * 512] for v in w], k == 0, k == T - 1)
            last.then_inc(L.filled(f"Y{e}t{t}"), 1)

    hidden(0)

    def step(e, i):
        hidden(e + 1, i)
        down(e, i)

    ffn_walk(pe, steps, step)
    down(steps - 1)


def ffn_act(K, L, ST, act, steps, first, second, wait_full, h_hi):
    def high(e, i):
        wait_full(e, i)
        act.activation(h_hi[:, e % 2, :, :], K.h[:, :, :], ACT.Copy).then_inc(K.sig["h_hi"], 1)

    def step(e, i):
        first(e, i)
        ST.split_hi(act, f"U{e + 1}", i)
        second(e, i)
        ST.split_hi(act, f"D{e}", i)
        high(e, i)
        if e + 2 < steps:
            ST.split_hi(act, f"G{e + 2}", i)

    ffn_walk(act, steps, step)
    e = steps - 1
    first(e, None)
    second(e, None)
    ST.split_hi(act, f"D{e}")
    high(e, None)


def ffn_dve(K, L, ST, dve, steps, first, second, add, h, enter, leave):
    def low(e, i):
        dve.wait_ge(K.sig["h_hi"], later(e + 1, i, 2))
        dve.tensor_tensor(h[1][:, e % 2, :, :], K.h[:, :, :], h[0][:, e % 2, :, :].bitcast(F32), ALU.subtract)\
           .then_inc(K.sig["h_lo"], 1)

    def sums(e, i):
        for t in range(T):
            L.wait_filled(dve, f"Y{e}t{t}", i, 2)
            L.wait_before(dve, f"Y{e}t{t}", i, 2)
            add(e, i, t).then_inc(L.drained(f"Y{e}t{t}"), 1)

    def step(e, i):
        first(e, i)
        ST.split_lo(dve, f"U{e + 1}", i)
        second(e, i)
        if e > 0:
            sums(e - 1, i)
        ST.split_lo(dve, f"D{e}", i)
        low(e, i)
        if e + 2 < steps:
            ST.split_lo(dve, f"G{e + 2}", i)

    ffn_walk(dve, steps, step, enter, leave)
    e = steps - 1
    first(e, None)
    second(e, None)
    sums(e - 1, None)
    ST.split_lo(dve, f"D{e}")
    low(e, None)
    sums(e, None)
    for t in range(T):
        L.wait_drained(dve, f"Y{e}t{t}")



ONE_CHUNKS = ["lat0", "lat1", "gkv", "gq0", "gq1", "pool0", "pool1", "g0a", "g0b", "g1a", "g1b", "uq", "ukv",
              "g2a", "g2b", "g3a", "g3b", "window", "g4a", "g4b", "pool_w", "g5a", "g5b",
              "bp0", "bp1", "bg0", "bg1", "bm0", "bm1", "wo00", "wo01", "wo10", "wo11"]
ONE_WIDTHS = {"lat0": 4 * LATENT, "lat1": 4 * LATENT, "uq": 2 * MLA_H * MLA_QK, "ukv": MLA_H * (NOPE + MLA_V),
              "pool_w": POOL_G * P}
ONE_ENDS = {"lat1": "lat", "gkv": "gkv", "gq1": "gq", "pool1": "pool", "uq": "q1", "ukv": "kv1", "window": "mix",
            "pool_w": "py", "wo01": "wo0", "wo11": "wo1"}
ONE_ENDS |= {f"g{g}b": f"g{g}" for g in range(6)} | {f"b{b}{c}": f"b{b}{c}" for b in "pgm" for c in range(2)}


def half_moments(K, dve, link, c):
    stats = K.stat[:, 176:200].rearrange("p (t c n) -> p t c n", t=T, c=2)
    for t in range(T):
        last = dve.bn_stats(stats[:, t, c, :], K.x[:, t, c * 512:(c + 1) * 512])
    link(last)


def moments(K, dve, link):
    stats = K.stat[:, 176:200].rearrange("p (t c n) -> p t c n", t=T, c=2)
    both = K.stat[:, 226:230].rearrange("p (t n) -> p t n", t=T)
    for t in range(T):
        last = dve.bn_aggr(both[:, t, :], stats[:, t, :, :])
    link(last)
    return both[:, :, 0:1], both[:, :, 1:2]


def root_act(K, act, tag):
    act.activation(K.stat[:, 232:233], K.ident[:, 0:1], ACT.Sqrt).then_inc(K.sig["table_in"], 1)
    act.wait_ge(K.sig[f"{tag}_var"], 1)
    act.activation(K.stat[:, 2:4], K.stat[:, 0:2], ACT.Sqrt).then_inc(K.sig[f"{tag}_root"], 1)


def rms_dve(K, dve, link, tag, out, gain):
    mean, var = moments(K, dve, link)
    inv = K.stat[:, 0:T].unsqueeze(2)
    link(dve.tensor_tensor(inv, mean, mean, ALU.mult))
    link(dve.tensor_tensor(inv, inv, var, ALU.add))
    dve.tensor_scalar(inv, inv, EPS, None, ALU.add).then_inc(K.sig[f"{tag}_var"], 1)
    dve.wait_ge(K.sig[f"{tag}_root"], 1)
    link(dve.reciprocal(K.stat[:, 0:T], K.stat[:, 2:4]))
    dve.wait_ge(K.sig[f"{tag}_gain"], 16)
    for h in range(2):
        for t in range(T):
            c = slice(h * 512, (h + 1) * 512)
            last = dve.scalar_tensor_tensor(out[:, t, c], K.x[:, t, c], K.stat[:, t:t + 1], gain[:, c],
                                            ALU.mult, ALU.mult)
        last.then_inc(K.sig[f"{tag}_normed"], 1)


def heads(ap, h):
    return ap.rearrange("p t (h d) -> p t h d", h=h)


def over_heads(ap, h, d):
    if len(ap.shape) == 3:
        return ap.unsqueeze(3).to_broadcast([P, T, h, d])
    return ap.unsqueeze(1).unsqueeze(1).to_broadcast([P, T, h, d])


def rotate(dve, link, x, half, cos, sin, tmp, h):
    x1, x2 = x[:, :, :, 0:half], x[:, :, :, half:2 * half]
    c = cos.unsqueeze(2).to_broadcast([P, T, h, half])
    s = sin.unsqueeze(2).to_broadcast([P, T, h, half])
    n = T * h * half
    t = [tmp[:, i * n:(i + 1) * n].rearrange("p (t h d) -> p t h d", t=T, h=h) for i in range(2)]
    dve.tensor_tensor(t[0], x1, s, ALU.mult)
    link(dve.tensor_tensor(t[1], x2, s, ALU.mult))
    dve.tensor_tensor(x1, x1, c, ALU.mult)
    link(dve.tensor_tensor(x2, x2, c, ALU.mult))
    dve.tensor_tensor(x1, x1, t[1], ALU.subtract)
    return dve.tensor_tensor(x2, x2, t[0], ALU.add)


class OneTiles:

    def __init__(self, K):
        K.base = K.floor
        o = {}

        def tile(name, shape, dtype=F32):
            o[name] = K.base
            return K.tile("one_" + name, shape, dtype)

        def over(name, shape, at, dtype=F32, off=0):
            return K.over("one_" + name, shape, o[at] + off, dtype)

        KB = 1024
        self.hT_hi = tile("hT_hi", [P, KD, S], F32R)
        self.hT_lo = tile("hT_lo", [P, KD, S], F32R)
        self.gT_hi = over("gT_hi", [P, 4, S], "hT_hi", F32R)
        self.gT_lo = over("gT_lo", [P, 4, S], "hT_hi", F32R, 4 * KB)
        self.mT_hi = over("mT_hi", [P, 4, S], "hT_lo", F32R)
        self.mT_lo = over("mT_lo", [P, 4, S], "hT_lo", F32R, 4 * KB)
        self.gates = tile("gates", [P, T, 3 * D])
        self.gain = over("gain", [P, D], "gates")
        self.lat = tile("lat", [P, T, C_POOL])
        self.q = tile("q", [P, T, MLA_H * MLA_QK])
        self.kv = tile("kv", [P, T, MLA_H * (NOPE + MLA_V)])
        self.k = tile("k", [P, T, MLA_H * MLA_QK])
        self.mqT = tile("mqT", [P, MLA_H, S])
        self.mkT = tile("mkT", [P, MLA_H, S])
        self.gqT = tile("gqT", [P, GQA_H // 2, S])
        self.gkT = tile("gkT", [P, GQA_KV, S])
        self.mixT_hi = over("mixT_hi", [P, POOL_G, S], "mqT", F32R)
        self.mixT_lo = over("mixT_lo", [P, POOL_G, S], "mkT", F32R)
        self.tmp = tile("tmp", [P, T, D])
        self.scratch = over("scratch", [P, 1536], "tmp")
        self.k2 = over("k2", [P, T, 4 * HD], "tmp", off=6 * KB)
        self.oTp_hi = tile("oTp_hi", [P, 4, S], F32R)
        self.oTp_lo = tile("oTp_lo", [P, 4, S], F32R)
        self.cT_hi = over("cT_hi", [P, 3, S], "oTp_hi", F32R)
        self.cT_lo = over("cT_lo", [P, 3, S], "oTp_lo", F32R)
        self.p = tile("p", [P, 2, D])
        self.p_hi = over("p_hi", [P, T, 512], "p", F32R)
        self.p_lo = over("p_lo", [P, T, 512], "p", F32R, 4 * KB)
        self.h_hi = over("h_hi", [P, 2, 2, S], "p", F32R)
        self.h_lo = over("h_lo", [P, 2, 2, S], "p", F32R, 4 * KB)
        self.pt = tile("pt", [P, D])
        self.colrows = over("colrows", [P, 2, P], "pt")
        self.conv = over("conv", [P, 2, 2, S], "tmp")
        self.rows = tile("rows", [P, 704])
        self.cols = tile("cols", [P, 2, 92])


def block_one(K, M, layer):
    nc, A, sig, st = K.nc, K.A, K.sig, K.stat
    names = ONE_CHUNKS + ffn_chunks(FF_STEPS)
    order = [("xT0", 0), ("xT1", 1), ("lat", 2), ("gkv", 3), ("gq", 0), ("pool", 1), ("cols", 2), ("g0", 3),
             ("g1", 0), ("cT", 1), ("q0", 2), ("q1", 3), ("kv0", 0), ("kv1", 1), ("g2", 2), ("g3", 3), ("mix", 0),
             ("g4", 1), ("py", 2), ("g5", 3), ("gqT", 0), ("gkT", 1)]
    order += Attention.lots("ga", GQA_H // 2)
    order += [("bp0", 2), ("bp1", 0), ("mqT0", 1), ("mqT1", 2), ("mkT0", 3), ("mkT1", 0)]
    order += Attention.lots("ma", MLA_H // 2)
    order += [("bg0", 2), ("bg1", 0), ("bm0", 1), ("bm1", 2), ("mT0", 3), ("mT1", 0), ("wo0", 1), ("wo1", 2),
              ("fT0", 3), ("fT1", 0)]
    order += ffn_lots(FF_STEPS)
    L = Lots(order, K.filled, K.drained)
    ST = Stream(K, L, names, ONE_WIDTHS, ONE_ENDS | ffn_ends(FF_STEPS), {}, FFN_TURN, {},
                by_pool=("window", "g4a", "g4b", "pool_w", "g5a", "bp0", "bp1", "bg0", "bg1", "bm0"))
    K.h = M.conv[:, 1, :, :]
    hT = (M.hT_hi, M.hT_lo)
    group = GQA_H // GQA_KV
    ga = Attention(K, L, "ga", GQA_H // 2,
                   q=lambda u, h: M.gqT[h * HD:(h + 1) * HD, u, :],
                   k=lambda u, h: M.gkT[h * HD:(h + 1) * HD, (2 * u + h) // group, :],
                   v=lambda u, h, c: M.lat[:, c, C_GV + (2 * u + h) // group * HD:
                                           C_GV + ((2 * u + h) // group + 1) * HD],
                   scale=HD ** -0.5, p=M.p, pt=M.pt, out=(M.gT_hi, M.gT_lo))
    ma = Attention(K, L, "ma", MLA_H // 2,
                   q=lambda u, h: M.mqT[0:MLA_QK, 2 * u + h, :],
                   k=lambda u, h: M.mkT[0:MLA_QK, 2 * u + h, :],
                   v=lambda u, h, c: M.kv[:, c, (2 * u + h) * 2 * HD + NOPE:(2 * u + h + 1) * 2 * HD],
                   scale=MLA_QK ** -0.5, p=M.p, pt=M.pt, out=(M.mT_hi, M.mT_lo))
    merged = M.tmp

    def source(name):
        w = A["w_in"][layer]
        kpc = lambda a: a.rearrange("(k p) c -> p k c", p=P)
        half = lambda c0, c1, k: kpc(w[k * 512:(k + 1) * 512, c0:c1])
        if name in ("lat0", "lat1"):
            return half(0, LATENT, int(name[-1]))
        if name == "gkv":
            return kpc(w[:, C_GK:C_POOL])
        if name in ("gq0", "gq1"):
            return half(C_GQ, C_GK, int(name[-1]))
        if name in ("pool0", "pool1"):
            return half(C_POOL, C_GATE, int(name[-1]))
        if name == "uq":
            return kpc(A["mla_w_uq"][layer])
        if name == "ukv":
            return kpc(A["mla_w_ukv"][layer])
        if name == "window":
            return A["c_window"]
        if name == "pool_w":
            return A["pool_w"][layer].rearrange("g c d -> c g d")
        if name[:2] == "wo":
            c, k = int(name[2]), int(name[3])
            return kpc(A["w_out"][layer][k * 512:(k + 1) * 512, c * 512:(c + 1) * 512])
        if name[0] == "b":
            b = {"p": "w_branch_pool", "g": "w_branch_gqa", "m": "w_branch_mla"}[name[1]]
            c = int(name[2])
            return kpc(A[b][layer][:, c * 512:(c + 1) * 512])
        c = C_GATE + 512 * int(name[1])
        return half(c, c + 512, "ab".index(name[2]))

    def ff_source(kind, e):
        if kind == "D":
            return A["ffn_w_down"][layer][bass.ds(e * S, S), :].rearrange("(k p) c -> p k c", p=P)
        return A["ffn_w_up"][layer][:, bass.ds(e * S + (D_FF if kind == "U" else 0), S)]\
            .rearrange("(k p) c -> p k c", p=P)

    with nc.Block() as block:

        @block.sync
        def _(sp):
            sp.dma_start(M.gain[:, :], A["attn_norm_g"][layer].partition_broadcast(P)).then_inc(sig["n1_gain"], 16)
            for name in ONE_CHUNKS:
                ST.may_load(sp, name)
                src = source(name)
                sp.dma_start(ST.raw(name)[:, 0:ST.columns(name)].rearrange("p (k c) -> p k c", k=src.shape[1]),
                             src).then_inc(ST.arrived(name), 16)
                if name == "gkv":
                    c = 0
                    for g, n in (("mla_q_norm_g", MLA_QL), ("mla_kv_norm_g", MLA_KVL), ("mla_q_head_g", MLA_QK),
                                 ("mla_k_head_g", MLA_QK), ("gqa_q_head_g", HD), ("gqa_k_head_g", HD)):
                        sp.dma_start(M.rows[:, c:c + n], A[g][layer].partition_broadcast(P))\
                          .then_inc(sig["rows"], 16)
                        c += n
                    for r0, r1, c, src in ((0, 44, 0, A["ffn_conv_w"][layer][0]), (44, 88, 0, A["ffn_conv_w"][layer][1]),
                                           (88, 92, 0, A["pool_scale"][layer]), (0, 44, 1, A["ffn_conv_w"][layer][2]),
                                           (44, 88, 1, A["ffn_conv_b"][layer])):
                        sp.dma_start(M.colrows[r0:r1, c, :], src.rearrange("(r p) -> r p", p=P))\
                          .then_inc(sig["colrows"], 16)
            sp.wait_ge(sig["merged"], 2)
            sp.dma_start(M.gain[:, :], A["ffn_norm_g"][layer].partition_broadcast(P)).then_inc(sig["n2_gain"], 16)
            ffn_load(K, ST, sp, FF_STEPS, ff_source)

        @block.tensor
        def _(pe):
            transpose_x(K, L, pe, M.tmp, ("xT0", "xT1"), sig["n1_normed"])
            project(K, L, ST, pe, "lat", ("lat0", "lat1"), LATENT, hT, turned=("xT0", "xT1"))
            project(K, L, ST, pe, "gkv", ("gkv",), 2 * GQA_KV * HD, hT, kn=KD)
            project(K, L, ST, pe, "gq", ("gq0", "gq1"), 512, hT)
            project(K, L, ST, pe, "pool", ("pool0", "pool1"), 512, hT)
            pe.wait_ge(sig["colrows"], 80)
            lot = L.claim(pe, "cols")
            pe.transpose(K.ps[lot][:, 0, 0:92], M.colrows[0:92, 0, :], K.ident[0:92, 0:92])
            pe.transpose(K.ps[lot][:, 1, 0:88], M.colrows[0:88, 1, :], K.ident[0:88, 0:88])\
              .then_inc(L.filled("cols"), 1)
            project(K, L, ST, pe, "g0", ("g0a", "g0b"), 512, hT)
            pe.wait_ge(sig["lat_normed"], 1)
            lot = L.claim(pe, "cT")
            d = flat(K.ps[lot][:, :, :]).rearrange("p (k s) -> p k s", k=4)
            for k in range(3):
                for t in range(T):
                    last = pe.transpose(d[:, k, t * P:(t + 1) * P], M.lat[:, t, k * P:(k + 1) * P], K.ident[:, :])
            last.then_inc(L.filled("cT"), 1)
            project(K, L, ST, pe, "g1", ("g1a", "g1b"), 512, hT)
            L.wait_drained(pe, "cT")
            cT = (M.cT_hi, M.cT_lo)
            for name, chunk, n, k0, kn in (("q", "uq", MLA_H * MLA_QK, 0, 2), ("kv", "ukv", MLA_H * 2 * HD, 2, 1)):
                for t in range(T):
                    lot = L.claim(pe, f"{name}{t}")
                    for bank in range(2):
                        c0, cn = bank * 512, min(512, n - bank * 512)
                        last = token_product(K, ST, pe, lambda t: K.ps[lot][:, bank, 0:cn], cT, chunk, True, True,
                                             k0, kn, n, tiles=(t,), c0=c0, cn=cn)
                    last.then_inc(L.filled(f"{name}{t}"), 1)
            for g in range(2, 4):
                project(K, L, ST, pe, f"g{g}", (f"g{g}a", f"g{g}b"), 512, hT)
            L.wait_drained(pe, "pool")
            lot = L.claim(pe, "mix")
            w = [v[:, :].rearrange("p (k g s) -> p k g s", k=T, g=POOL_G) for v in ST.parts(pe, "window")]
            d = flat(K.ps[lot][:, :, :]).rearrange("p (g s) -> p g s", g=POOL_G)
            for g in range(POOL_G):
                for k in range(T):
                    last = mm3(pe, d[:, g, :], [v[:, k, g * P:(g + 1) * P] for v in (M.p_hi, M.p_lo)],
                               [v[:, k, g, :] for v in w], k == 0, k == T - 1)
            last.then_inc(L.filled("mix"), 1)
            project(K, L, ST, pe, "g4", ("g4a", "g4b"), 512, hT)
            L.wait_drained(pe, "mix")
            lot = L.claim(pe, "py")
            w = [v[:, 0:POOL_G * P].rearrange("p (g c) -> p g c", g=POOL_G) for v in ST.parts(pe, "pool_w")]
            d = flat(K.ps[lot][:, :, :]).rearrange("p (g s) -> p g s", g=POOL_G)
            for g in range(POOL_G):
                last = mm3(pe, d[:, g, :], [v[:, g, :] for v in w], [v[:, g, :] for v in (M.mixT_hi, M.mixT_lo)],
                           True, True)
            last.then_inc(L.filled("py"), 1)
            project(K, L, ST, pe, "g5", ("g5a", "g5b"), 512, hT)
            pe.wait_ge(sig["gqa_ready"], 1)
            for name, src, pairs in (("gqT", M.lat[:, :, C_GQ:C_GK], 4), ("gkT", M.k2[:, :, :], 2)):
                lot = L.claim(pe, name)
                d = flat(K.ps[lot][:, :, :]).rearrange("p (k s) -> p k s", k=4)
                for k in range(pairs):
                    for t in range(T):
                        last = pe.transpose(d[:, k, t * P:(t + 1) * P], src[:, t, k * P:(k + 1) * P], K.ident[:, :])
                last.then_inc(L.filled(name), 1)
            L.wait_drained(pe, "gqT")
            L.wait_drained(pe, "gkT")
            ga.pe(pe)

            def branch(name, xT):
                for c in range(2):
                    lot = L.claim(pe, f"{name}{c}")
                    token_product(K, ST, pe, lambda t: K.ps[lot][:, t, :], xT, f"{name}{c}", True, True, 0, 4, 512)\
                        .then_inc(L.filled(f"{name}{c}"), 1)

            branch("bp", (M.oTp_hi, M.oTp_lo))
            pe.wait_ge(sig["mla_ready"], 1)
            for name, src in (("mqT", M.q), ("mkT", M.k)):
                for half in range(2):
                    lot = L.claim(pe, f"{name}{half}")
                    d = flat(K.ps[lot][:, :, :]).rearrange("p (k s) -> p k s", k=4)
                    for k in range(4):
                        for t in range(T):
                            h = 4 * half + k
                            last = pe.transpose(d[0:MLA_QK, k, t * P:(t + 1) * P],
                                                src[:, t, h * MLA_QK:(h + 1) * MLA_QK], K.ident[:, :])
                    last.then_inc(L.filled(f"{name}{half}"), 1)
            for n in ("mqT0", "mqT1", "mkT0", "mkT1"):
                L.wait_drained(pe, n)
            ma.pe(pe)
            L.wait_drained(pe, "gaO3")
            branch("bg", (M.gT_hi, M.gT_lo))
            L.wait_drained(pe, "maO3")
            branch("bm", (M.mT_hi, M.mT_lo))
            transpose_x(K, L, pe, merged, ("mT0", "mT1"), sig["merged"])
            for c in range(2):
                project(K, L, ST, pe, f"wo{c}", (f"wo{c}0", f"wo{c}1"), 512, hT,
                        turned=("mT0", "mT1") if c == 0 else ())
            transpose_x(K, L, pe, M.tmp, ("fT0", "fT1"), sig["n2_normed"])
            for n in ("fT0", "fT1"):
                L.wait_drained(pe, n)
            ffn_pe(K, L, ST, pe, FF_STEPS, hT, (M.h_hi, M.h_lo))

        @block.scalar
        def _(act):
            def sigmoid(g):
                lot = L.wait_filled(act, f"g{g}")
                act.activation(M.gates[:, :, g * 512:(g + 1) * 512], K.ps[lot][:, :, :], ACT.Sigmoid)\
                   .then_inc(L.drained(f"g{g}"), 1)

            def root(name, cols):
                act.wait_ge(sig[f"{name}_var"], 1)
                act.activation(st[:, cols], st[:, cols], ACT.Sqrt).then_inc(sig[f"{name}_root"], 1)

            def take(name, dst, part=None, rows=P):
                lot = L.wait_filled(act, name)
                src = flat(K.ps[lot][:, :, :])[0:rows, :] if part is None else part(K.ps[lot])
                act.activation(dst, src, ACT.Copy).then_inc(L.drained(name), 1)

            root_act(K, act, "n1")
            ST.hi_to(act, "lat0")
            act_hi(K, L, act, "xT0", flat(M.hT_hi[:, 0:4, :]))
            act_hi(K, L, act, "xT1", flat(M.hT_hi[:, 4:8, :]))
            ST.hi_to(act, "gkv", 2)
            L.wait_drained(act, "lat")
            for t in range(T):
                act.activation(M.q[:, t, 0:MLA_QL], M.lat[:, t, 0:MLA_QL], ACT.Square,
                               accum_out=st[:, 4 + t:5 + t])
                last = act.activation(M.q[:, t, MLA_QL:MLA_QL + MLA_KVL], M.lat[:, t, MLA_QL:MLA_QL + MLA_KVL], ACT.Square,
                                      accum_out=st[:, 6 + t:7 + t])
            last.then_inc(sig["lat_squares"], 1)
            ST.hi_to(act, "gq1", 2)
            take("gq", M.lat[:, :, C_GQ:C_GK], lambda ps: ps[:, :, :])
            root("lat", slice(8, 12))
            ST.hi_to(act, "pool1", 2)
            act_hi(K, L, act, "pool", flat(M.p_hi[:, :, :]))
            ST.hi_to(act, "g0b", 1)
            root("gqa", slice(16, 36))
            ST.hi_to(act, "g0b", 2)
            sigmoid(0)
            act_hi(K, L, act, "cT", flat(M.cT_hi[:, :, :]), lambda lot: flat(K.ps[lot][:, :, :])[:, 0:3 * S])
            ST.hi_to(act, "g1b", 2)
            sigmoid(1)
            ST.hi_to(act, "uq", 2)
            n = MLA_H * MLA_QK
            for t in range(T):
                take(f"q{t}", M.q[:, t, :], lambda ps: flat(ps[:, :, :])[:, 0:n])
            ST.hi_to(act, "g2b", 2)
            sigmoid(2)
            ST.hi_to(act, "g3b", 2)
            sigmoid(3)
            ST.hi_to(act, "window", 2)
            act_hi(K, L, act, "mix", flat(M.mixT_hi[:, :, :]))
            root("mla", slice(80, 112))
            ST.hi_to(act, "g4b", 2)
            sigmoid(4)
            ST.hi_to(act, "pool_w", 2)
            L.wait_drained(act, "cols")
            lot = L.wait_filled(act, "py")
            for g in range(POOL_G):
                last = act.activation(M.oTp_hi[:, g, :], flat(K.ps[lot][:, :, :])[:, g * S:(g + 1) * S], ACT.Copy,
                                      scale=M.cols[:, 0, 88 + g:89 + g])
            last.then_inc(sig["hi_py"], 1)
            ST.hi_to(act, "g5b", 2)
            sigmoid(5)
            ST.hi_to(act, "g5b", 3)
            take("gqT", flat(M.gqT[:, :, :]))
            ga.act(act)
            ST.hi_to(act, "bp1", 2)
            for half in range(2):
                take(f"mqT{half}", flat(M.mqT[0:MLA_QK, 4 * half:4 * half + 4, :]), rows=MLA_QK)
            ma.act(act)
            ST.hi_to(act, "wo01")
            act_hi(K, L, act, "mT0", flat(M.hT_hi[:, 0:4, :]))
            act_hi(K, L, act, "mT1", flat(M.hT_hi[:, 4:8, :]))
            ST.hi_to(act, "wo11")
            ST.hi_to(act, "U0")
            root_act(K, act, "n2")
            act_hi(K, L, act, "fT0", flat(M.hT_hi[:, 0:4, :]))
            act_hi(K, L, act, "fT1", flat(M.hT_hi[:, 4:8, :]))
            ST.hi_to(act, "G1")

            def middle_tap(e, i):
                if e or i is not None:
                    act.wait_ge(sig["h_lo"], later(e, i, 2))
                lot = L.wait_filled(act, f"H{e}", i, 1)
                for b in range(2):
                    for f in range(2):
                        at = 22 * b + f + 2 * true_step(e, i)
                        last = act.activation(M.conv[:, b, f, :], K.ps[lot][:, b, f * S:(f + 1) * S], ACT.Identity,
                                              scale=M.cols[:, 0, bass.ds(44 + at, 1)],
                                              bias=M.cols[:, 1, bass.ds(44 + at, 1)])
                last.then_inc(sig["middle"], 1)

            def silu(e, i):
                L.wait_drained(act, f"H{e}", i, 1)
                act.activation(M.conv[:, 0, :, :], M.conv[:, 0, :, :], ACT.Silu).then_inc(sig["silu"], 1)

            ffn_act(K, L, ST, act, FF_STEPS, middle_tap, silu,
                    lambda e, i: act.wait_ge(sig["h_full"], later(e + 1, i, 2)), M.h_hi)

        @block.vector
        def _(dve):
            link = Chain(dve, sig["dve_chain"])

            def take(name, dst, part=None, rows=P):
                lot = L.wait_filled(dve, name)
                src = flat(K.ps[lot][:, :, :])[0:rows, :] if part is None else part(K.ps[lot])
                dve.tensor_copy(dst, src).then_inc(L.drained(name), 1)

            def mul(out, a, b):
                return dve.tensor_tensor(out, a, b, ALU.mult)

            half_moments(K, dve, link, 0)
            half_moments(K, dve, link, 1)
            rms_dve(K, dve, link, "n1", M.tmp, M.gain)
            ST.lo_to(dve, "lat0")
            dve_lo(K, L, dve, "xT0", flat(M.hT_lo[:, 0:4, :]), flat(M.hT_hi[:, 0:4, :]))
            dve_lo(K, L, dve, "xT1", flat(M.hT_lo[:, 4:8, :]), flat(M.hT_hi[:, 4:8, :]))
            ST.lo_to(dve, "lat1", 2)
            take("lat", M.lat[:, :, 0:LATENT], lambda ps: ps[:, :, 0:LATENT])
            ST.lo_to(dve, "gkv", 2)
            take("gkv", M.lat[:, :, C_GK:C_POOL], lambda ps: ps[:, :, 0:C_POOL - C_GK])
            ST.lo_to(dve, "gq1", 2)
            dve.wait_ge(sig["lat_squares"], 1)
            dve.tensor_scalar(st[:, 8:10], st[:, 4:6], 1.0 / MLA_QL, EPS, ALU.mult, ALU.add)
            dve.tensor_scalar(st[:, 10:12], st[:, 6:8], 1.0 / MLA_KVL, EPS, ALU.mult, ALU.add)\
               .then_inc(sig["lat_var"], 1)
            ST.lo_to(dve, "pool1", 1)
            dve_lo(K, L, dve, "pool", flat(M.p_lo[:, :, :]), flat(M.p_hi[:, :, :]))
            dve.wait_ge(sig["lat_root"], 1)
            dve.wait_ge(sig["rows"], 96)
            link(dve.reciprocal(st[:, 4:8], st[:, 8:12]))
            for t in range(T):
                for c0, c1, s in ((0, MLA_QL, 4 + t), (MLA_QL, MLA_QL + MLA_KVL, 6 + t)):
                    last = dve.scalar_tensor_tensor(M.lat[:, t, c0:c1], M.lat[:, t, c0:c1], st[:, s:s + 1],
                                                    M.rows[:, c0:c1], ALU.mult, ALU.mult)
            last.then_inc(sig["lat_normed"], 1)
            ST.lo_to(dve, "g0b")
            qk = heads(M.lat[:, :, C_GQ:C_GV], 10)
            sq = M.scratch[:, 0:T * 10 * HD].rearrange("p (t h d) -> p t h d", t=T, h=10)
            n_qk = st[:, 16:36].rearrange("p (t h) -> p t h", t=T)
            L.wait_drained(dve, "gq")
            L.wait_drained(dve, "gkv")
            link(mul(sq, qk, qk))
            link(dve.tensor_reduce(st[:, 16:36], M.scratch[:, 0:T * 10 * HD].rearrange("p (n d) -> p n d", d=HD),
                                   AX_X, ALU.add))
            dve.tensor_scalar(st[:, 16:36], st[:, 16:36], 1.0 / HD, EPS, ALU.mult, ALU.add)\
               .then_inc(sig["gqa_var"], 1)
            lot = L.wait_filled(dve, "cols")
            dve.tensor_copy(M.cols[:, :, 0:88], K.ps[lot][:, :, 0:88])
            dve.tensor_copy(M.cols[:, 0, 88:92], K.ps[lot][:, 0, 88:92]).then_inc(L.drained("cols"), 1)
            ST.lo_to(dve, "g1a")
            dve_lo(K, L, dve, "cT", flat(M.cT_lo[:, :, :]), flat(M.cT_hi[:, :, :]),
                   lambda lot: flat(K.ps[lot][:, :, :])[:, 0:3 * S])
            dve.wait_ge(sig["gqa_root"], 1)
            link(dve.reciprocal(st[:, 16:36], st[:, 16:36]))
            link(mul(qk, qk, over_heads(n_qk, 10, HD)))
            mul(qk[:, :, 0:8, :], qk[:, :, 0:8, :], over_heads(M.rows[:, 576:640], 8, HD))
            link(mul(qk[:, :, 8:10, :], qk[:, :, 8:10, :], over_heads(M.rows[:, 640:704], 2, HD)))
            ST.lo_to(dve, "g1b")
            link(rotate(dve, link, qk, HD // 2, K.rope[:, :, 32:64], K.rope[:, :, 64:96], M.scratch, 10))
            k2 = M.k2[:, :, :].rearrange("p t (h two d) -> p t h two d", h=2, two=2)
            for two in range(2):
                last = dve.tensor_copy(k2[:, :, :, two, :], qk[:, :, 8:10, :])
            last.then_inc(sig["gqa_ready"], 1)
            ST.lo_to(dve, "uq", 2)
            for t in range(T):
                take(f"kv{t}", M.kv[:, t, :])
            ST.lo_to(dve, "g2b")
            q, k, kv = heads(M.q[:, :, :], 8), heads(M.k[:, :, :], 8), heads(M.kv[:, :, :], 8)
            kr = M.lat[:, :, MLA_QL + MLA_KVL:LATENT]
            n_q = st[:, 80:96].rearrange("p (t h) -> p t h", t=T)
            n_k = st[:, 96:112].rearrange("p (t h) -> p t h", t=T)
            L.wait_drained(dve, "q1")
            L.wait_drained(dve, "kv1")
            link(mul(M.scratch[:, :], flat(M.q[:, :, :]), flat(M.q[:, :, :])))
            link(dve.tensor_reduce(st[:, 80:96], M.scratch[:, :].rearrange("p (n d) -> p n d", d=MLA_QK),
                                   AX_X, ALU.add))
            ST.lo_to(dve, "g3a")
            link(mul(M.scratch[:, 0:1024].rearrange("p (t h d) -> p t h d", t=T, h=8), kv[:, :, :, 0:NOPE],
                     kv[:, :, :, 0:NOPE]))
            dve.tensor_reduce(st[:, 96:112], M.scratch[:, 0:1024].rearrange("p (n d) -> p n d", d=NOPE),
                              AX_X, ALU.add)
            link(mul(M.scratch[:, 1024:1088].rearrange("p (t d) -> p t d", t=T), kr, kr))
            link(dve.tensor_reduce(st[:, 72:74], M.scratch[:, 1024:1088].rearrange("p (t d) -> p t d", t=T),
                                   AX_X, ALU.add))
            link(dve.tensor_tensor(n_k, n_k, st[:, 72:74].unsqueeze(2).to_broadcast([P, T, 8]), ALU.add))
            dve.tensor_scalar(st[:, 80:112], st[:, 80:112], 1.0 / MLA_QK, EPS, ALU.mult, ALU.add)\
               .then_inc(sig["mla_var"], 1)
            ST.lo_to(dve, "g3b")
            ST.lo_to(dve, "window", 1)
            dve_lo(K, L, dve, "mix", flat(M.mixT_lo[:, :, :]), flat(M.mixT_hi[:, :, :]))
            dve.wait_ge(sig["mla_root"], 1)
            link(dve.reciprocal(st[:, 80:112], st[:, 80:112]))
            link(mul(q, q, over_heads(n_q, 8, MLA_QK)))
            mul(k[:, :, :, 0:NOPE], kv[:, :, :, 0:NOPE], over_heads(n_k, 8, NOPE))
            link(mul(k[:, :, :, NOPE:MLA_QK], kr.unsqueeze(2).to_broadcast([P, T, 8, ROPE]),
                     over_heads(n_k, 8, ROPE)))
            ST.lo_to(dve, "g4b")
            mul(q, q, over_heads(M.rows[:, 384:480], 8, MLA_QK))
            link(mul(k, k, over_heads(M.rows[:, 480:576], 8, MLA_QK)))
            ST.lo_to(dve, "pool_w")
            cos, sin = K.rope[:, :, 0:16], K.rope[:, :, 16:32]
            link(rotate(dve, link, q[:, :, :, NOPE:MLA_QK], ROPE // 2, cos, sin, M.scratch, 8))
            rotate(dve, link, k[:, :, :, NOPE:MLA_QK], ROPE // 2, cos, sin, M.scratch, 8)\
                .then_inc(sig["mla_ready"], 1)
            ST.lo_to(dve, "pool_w", 2)
            dve.wait_ge(sig["hi_py"], 1)
            lot = L.use["py"][0]
            for g in range(POOL_G):
                last = dve.scalar_tensor_tensor(M.oTp_lo[:, g, :], flat(K.ps[lot][:, :, :])[:, g * S:(g + 1) * S],
                                                M.cols[:, 0, 88 + g:89 + g], M.oTp_hi[:, g, :].bitcast(F32),
                                                ALU.mult, ALU.subtract)
            last.then_inc(L.drained("py"), 1)
            ST.lo_to(dve, "g5b", 3)
            take("gkT", flat(M.gkT[:, :, :]), lambda ps: ps[:, 0, :])
            ga.dve(dve, link)

            for g in range(6):
                L.wait_drained(dve, f"g{g}")
            for c in range(2):
                ST.lo_to(dve, f"bp{c}", 2)
                lot = L.wait_filled(dve, f"bp{c}")
                mul(merged[:, :, c * 512:(c + 1) * 512], K.ps[lot][:, :, :],
                    M.gates[:, :, 2 * D + c * 512:2 * D + (c + 1) * 512]).then_inc(L.drained(f"bp{c}"), 1)
            for half in range(2):
                take(f"mkT{half}", flat(M.mkT[0:MLA_QK, 4 * half:4 * half + 4, :]), rows=MLA_QK)
            ma.dve(dve, link)
            for c in range(2):
                L.wait_drained(dve, f"bp{c}")
            for name, b in (("bg", 1), ("bm", 0)):
                for c in range(2):
                    ST.lo_to(dve, f"{name}{c}", 2)
                    lot = L.wait_filled(dve, f"{name}{c}")
                    gate = M.gates[:, :, b * D + c * 512:b * D + (c + 1) * 512]
                    mul(gate, K.ps[lot][:, :, :], gate).then_inc(L.drained(f"{name}{c}"), 1)
                    L.wait_drained(dve, f"{name}{c}")
                    last = dve.tensor_tensor(merged[:, :, c * 512:(c + 1) * 512],
                                             merged[:, :, c * 512:(c + 1) * 512], gate, ALU.add)
                    if name == "bm":
                        last.then_inc(sig["merged"], 1)
                    else:
                        link(last)
            dve_lo(K, L, dve, "mT0", flat(M.hT_lo[:, 0:4, :]), flat(M.hT_hi[:, 0:4, :]))
            dve_lo(K, L, dve, "mT1", flat(M.hT_lo[:, 4:8, :]), flat(M.hT_hi[:, 4:8, :]))
            ST.lo_to(dve, "wo11")
            for c in range(2):
                lot = L.wait_filled(dve, f"wo{c}")
                x = K.x[:, :, c * 512:(c + 1) * 512]
                dve.tensor_tensor(x, x, K.ps[lot][:, :, :], ALU.add).then_inc(L.drained(f"wo{c}"), 1)
                L.wait_drained(dve, f"wo{c}")
                half_moments(K, dve, link, c)
                if c == 0:
                    ST.lo_to(dve, "G0")
            rms_dve(K, dve, link, "n2", M.tmp, M.gain)
            dve_lo(K, L, dve, "fT0", flat(M.hT_lo[:, 0:4, :]), flat(M.hT_hi[:, 0:4, :]))
            dve_lo(K, L, dve, "fT1", flat(M.hT_lo[:, 4:8, :]), flat(M.hT_hi[:, 4:8, :]))
            ST.lo_to(dve, "U0")
            ST.lo_to(dve, "G1")

            def outer_taps(e, i):
                lot = L.use[f"H{e}"][0]
                dve.wait_ge(sig["middle"], later(e + 1, i, 2))
                for tap in (0, 2):
                    for b in range(2):
                        for f in range(2):
                            at = 22 * b + f + 2 * true_step(e, i)
                            u, c = K.ps[lot][:, b, f * S:(f + 1) * S], M.conv[:, b, f, :]
                            src, dst = (u[:, 0:S - 1], c[:, 1:S]) if tap == 0 else (u[:, 1:S], c[:, 0:S - 1])
                            w = M.cols[:, tap // 2, bass.ds(at, 1)]
                            last = dve.scalar_tensor_tensor(dst, src, w, dst, ALU.mult, ALU.add)
                    if tap == 0:
                        link(last)
                last.then_inc(L.drained(f"H{e}"), 1)

            def product(e, i):
                dve.wait_ge(sig["silu"], later(e + 1, i, 2))
                dve.tensor_tensor(K.h, M.conv[:, 0, :, :], K.h, ALU.mult).then_inc(sig["h_full"], 1)

            def add(e, i, t):
                return dve.tensor_tensor(K.x[:, t, :], K.x[:, t, :],
                                         flat(K.ps[L.use[f"Y{e}t{t}"][0]][:, :, :]), ALU.add)

            ffn_dve(K, L, ST, dve, FF_STEPS, outer_taps, product, add, (M.h_hi, M.h_lo),
                    lambda i: link.enter(i, 2), link.leave)

        @block.gpsimd
        def _(pool):
            ST.lo_by_pool(pool)



TWO_CHUNKS = ["iq0", "iq1", "ik", "dq0", "dq1", "dk0", "dk1", "sq0", "sq1", "sk0", "sk1", "dv0", "dv1", "sv0", "sv1",
              "g0a", "g0b", "g1a", "g1b", "g2a", "g2b", "g3a", "g3b", "bs0", "bs1", "bd0", "bd1",
              "wo00", "wo01", "wo10", "wo11", "route", "pg00", "pg01", "pg10", "pg11", "wple"]
N_ROUTE = N_G + N_E
TWO_WIDTHS = {"ik": KD * (HD + IDX_H), "route": KD * N_ROUTE}
TWO_ENDS = {"ik": "ik", "wo01": "wo0", "wo11": "wo1", "route": "rt", "pg01": "pg0", "pg11": "pg1", "wple": "pl1"}
TWO_ENDS |= {f"{n}1": n for n in ("iq", "dq", "dk", "sq", "sk", "dv", "sv")}
TWO_ENDS |= {f"g{g}b": f"g{g}" for g in range(4)} | {f"b{b}{c}": f"b{b}{c}" for b in "sd" for c in range(2)}
TWO_COLUMNS = {"dq": C_DQ, "dk": C_DK, "dv": C_DV, "sq": C_SQ, "sk": C_SK, "sv": C_SV, "iq": C_IQ}


class TwoTiles:

    def __init__(self, K):
        K.base = K.floor
        o = {}

        def tile(name, shape, dtype=F32):
            o[name] = K.base
            return K.tile("two_" + name, shape, dtype)

        def over(name, shape, at, dtype=F32, off=0):
            return K.over("two_" + name, shape, o[at] + off, dtype)

        KB = 1024
        self.rot = tile("rot", [P, T, ROT])
        self.causal = tile("causal", [P, T, S])
        self.hT_hi = tile("hT_hi", [P, KD, S], F32R)
        self.hT_lo = tile("hT_lo", [P, KD, S], F32R)
        self.sT_hi = over("sT_hi", [P, 4, S], "hT_hi", F32R)
        self.sT_lo = over("sT_lo", [P, 4, S], "hT_hi", F32R, 4 * KB)
        self.yT_hi = over("yT_hi", [P, 4, S], "hT_lo", F32R)
        self.yT_lo = over("yT_lo", [P, 4, S], "hT_lo", F32R, 4 * KB)
        self.x_before = over("x_before", [P, T, D], "hT_hi")
        self.gates = tile("gates", [P, T, 2 * D])
        self.pr = tile("pr", [P, T, C_ATT])
        self.ln_g = over("ln_g", [P, D], "pr")
        self.ln_b = over("ln_b", [P, D], "pr", off=4 * KB)
        self.ln2_g = over("ln2_g", [P, D], "pr", off=8 * KB)
        self.ln2_b = over("ln2_b", [P, D], "pr", off=12 * KB)
        self.ple = over("ple", [P, T, S], "pr", off=16 * KB)
        self.dqT, self.dkT, self.sqT, self.skT, self.iqT = (tile(n, [P, 4, S]) for n in ("dqT", "dkT", "sqT", "skT", "iqT"))
        self.fourth = over("fourth", [P, CHUNK], "skT")
        self.ikT = tile("ikT", [P, S])
        self.pT_hi = over("pT_hi", [P, 2, S], "dqT", F32R)
        self.pT_lo = over("pT_lo", [P, 2, S], "dqT", F32R, 2 * KB)
        self.pgate = over("pgate", [P, 2, T, 512], "dkT")
        self.tmp = tile("tmp", [P, T, D])
        self.scratch = over("scratch", [P, 1024], "tmp")
        self.ik2 = over("ik2", [P, T, 2 * HD], "tmp", off=4 * KB)
        self.p = tile("p", [P, 2, D])
        self.pt = tile("pt", [P, D])
        self.ya = tile("ya", [P, T, 512])
        self.xg_hi = over("xg_hi", [P, KD, N_G * P], "gates", F32R)
        self.xg_lo = over("xg_lo", [P, KD, N_G * P], "p", F32R)
        self.slot_r = over("slot", [P, T, (N_G + 1) * P], "pr", F32R, 18 * KB)
        self.slot = self.slot_r[:, :, :].bitcast(F32)
        self.x_hi = over("x_hi", [P, T, D], "pr", F32R)
        self.x_lo = over("x_lo", [P, T, D], "tmp", F32R)
        self.slotT = over("slotT", [P, N_G * S], "pr", off=23 * KB)
        self.back = over("back", [P, S], "pr", off=27 * KB)
        self.y = over("y", [P, D], "tmp")
        self.score = tile("score", [P, T, S])
        self.work = tile("work", [P, T, S])
        self.bias = tile("bias", [P, T, S])
        self.act = over("act", [P, 2, D_E], "score")
        self.h_hi = over("h_hi", [P, 2, P], "work", F32R)
        self.h_lo = over("h_lo", [P, 2, P], "work", F32R, KB)
        self.top8 = tile("top8", [P, T, 8])
        self.wi = tile("wi", [P, T, 8])
        self.lam = tile("lam", [P, 4 * HD + 2])
        self.sub = tile("sub", [P, P])
        self.route_b = tile("route_b", [P, N_ROUTE])
        self.logit = tile("logit", [P, T, N_ROUTE])
        self.r32 = tile("r32", [P, T, N_E])
        self.r = tile("r", [P, 8, T, 8])
        self.iota = tile("iota", [P, 12])
        self.xw_hi = over("xw_hi", [P, KD, P], "tmp", F32R, 4 * KB)
        self.xw_lo = tile("xw_lo", [P, KD, P], F32R)
        self.tri = tile("tri", [P, 2 * P])
        self.slots = tile("slots", [P, P])
        self.weight = tile("weight", [P, N_E])
        self.over_f = tile("over_f", [P, 8])
        self.over = tile("over", [P, 2], I32)
        self.pos = tile("pos", [P, T], I32)
        self.inv = tile("inv", [P, ROT // 2])
        self.ang = tile("ang", [P, 4, T, ROT // 2])


def rotation_tables(K, M):
    nc, A, sig, st = K.nc, K.A, K.sig, K.stat
    turn, magic = 2 * np.pi, 1.5 * 2.0 ** 23
    c1 = 6.28125
    c2 = float(np.float32(np.frombuffer(np.uint32(np.float32(turn - c1).view(np.uint32) & 0xFFFFF000).tobytes(),
                                        np.float32)[0]))
    c3 = turn - c1 - c2
    with nc.Block() as block:

        @block.sync
        def _(sp):
            with nc.allow_non_contiguous_dma(reason="256 positions, one a partition and tile"):
                sp.dma_start(M.pos[:, :], A["positions_2"][0].rearrange("(t p) -> p t", p=P)).then_inc(sig["tables"], 16)
            sp.dma_start(M.inv[:, :], A["c_inv_freq"][0].partition_broadcast(P)).then_inc(sig["tables"], 16)
            sp.dma_start(M.causal[:, :, :], A["c_causal"]).then_inc(sig["tables"], 16)
            sp.dma_start(M.iota[:, 0:N_G], A["c_groups"][0].partition_broadcast(P)).then_inc(sig["tables"], 16)
            sp.dma_start(M.iota[:, 4:12], A["c_experts"][0].partition_broadcast(P)).then_inc(sig["tables"], 16)
            sp.dma_start(M.tri[:, :], A["c_tri"]).then_inc(sig["tables"], 16)
            sp.dma_start(M.slots[:, :], A["c_slots"][0].partition_broadcast(P)).then_inc(sig["tables"], 16)

        @block.scalar
        def _(act):
            act.wait_ge(sig["angles"], 1)
            act.activation(M.rot[:, :, 8:16], M.ang[:, 0, :, :], ACT.Sin).then_inc(sig["sines"], 1)
            act.activation(M.rot[:, :, 0:8], M.ang[:, 2, :, :], ACT.Sin).then_inc(sig["sines"], 1)

        @block.vector
        def _(dve):
            link = Chain(dve, sig["dve_chain"])
            dve.wait_ge(sig["tables"], 112)
            link(dve.tensor_copy(st[:, 0:T], M.pos[:, :]))
            for t in range(T):
                last = dve.tensor_scalar(M.ang[:, 0, t, :], M.inv[:, :], st[:, t:t + 1], None, ALU.mult)
            link(last)
            a, k, c = (M.ang[:, n, :, :] for n in range(3))
            link(dve.tensor_scalar(k, a, 1.0 / turn, magic, ALU.mult, ALU.add))
            link(dve.tensor_scalar(k, k, magic, None, ALU.subtract))
            for part in (c1, c2, c3):
                link(dve.scalar_tensor_tensor(a, k, -part, a, ALU.mult, ALU.add))
            link(dve.tensor_scalar(a, a, 3.1415925, -3.1415925, ALU.min, ALU.max))
            link(dve.scalar_tensor_tensor(c, a, -1.0, a, ALU.mult, ALU.max))
            dve.tensor_scalar(c, c, -1.0, np.pi / 2, ALU.mult, ALU.add).then_inc(sig["angles"], 1)


class DiffAttention(Attention):

    def pe_turn(self, pe, u):
        K, L = self.K, self.L
        p = self.p[:, u % 2, 0:T * S].rearrange("p (t k) -> p t k", t=T)
        d = K.ps[L.use[f"{self.tag}T{u}"][0]][:, 0, :].rearrange("p (c q) -> p c q", c=T)
        for t in range(T):
            for c in range(t + 1):
                last = pe.transpose(d[:, c, t * P:(t + 1) * P], p[:, t, c * P:(c + 1) * P], K.ident[:, :])
        return last

    def pe_out(self, pe, u):
        K = self.K
        pt = self.pt[:, 0:T * S].rearrange("p (c q) -> p c q", c=T)
        for t in range(T):
            for c in range(t + 1):
                last = pe.matmul(K.ps[3][:, t, 0:P], pt[:, c, t * P:(t + 1) * P], self.v(u, 0, c),
                                 start=c == 0, stop=c == t)
        return last

    def copy_turned(self, act):
        src, dst = (a.rearrange("p (h c q) -> p h c q", h=1, c=T) for a in (self.K.ps[2][:, 0, :], self.pt[:, 0:T * S]))
        return self.copy_seen(act, src, dst)

    def act_out(self, act, u):
        self.L.wait_filled(act, f"{self.tag}O{u}")
        act.activation(self.out[:, :, u * P:(u + 1) * P], self.K.ps[3][:, :, 0:P], ACT.Copy)\
           .then_inc(self.L.drained(f"{self.tag}O{u}"), 1)

    def dve_out(self, dve, u):
        pass

    def weigh(self, dve, link, u, inv):
        p = self.p[:, u % 2, :].rearrange("p (n k) -> p n k", n=4)
        link(dve.tensor_scalar(inv[:, 2:4], inv[:, 2:4], self.K.stat[:, 120:121], None, ALU.mult))
        for t, n in enumerate(self.keys):
            last = dve.tensor_scalar(p[:, t, 0:n], p[:, t, 0:n], inv[:, t:t + 1], None, ALU.mult)
        link(last)
        for t, n in enumerate(self.keys):
            last = dve.scalar_tensor_tensor(p[:, t, 0:n], p[:, 2 + t, 0:n], inv[:, 2 + t:3 + t], p[:, t, 0:n],
                                            ALU.mult, ALU.add)
        return last


def window_chunks(tag):
    names = []
    for e in range(E_G):
        if e + 1 < E_G or tag == "a":
            names += [f"G{e + 1}{tag}", f"U{e + 1}{tag}"]
        names.append(f"D{e}{tag}")
    return names


def window_ends(tag):
    return {f"U{e}{tag}": f"H{e}{tag}" for e in range(E_G + 1)} | {f"D{E_G - 1}{tag}": f"Y{tag}"}


def window_lots(tag):
    order = []
    for e in range(E_G):
        if e + 1 < E_G or tag == "a":
            order.append((f"H{e + 1}{tag}", (e + 1) % 2))
        order.append((f"T{e}{tag}", 3))
        if tag != "b" and 1 <= e <= T:
            order.append((f"S{e - 1}{tag}", 3))
    return order + [(f"Y{tag}", 2)]


class Windows:

    def __init__(self, K, M, L, ST, source):
        self.K, self.M, self.L, self.ST, self.source = K, M, L, ST, source

    def lot_of(self, tag, e):
        return "H8a" if tag == "z" and e == 0 else f"H{e}{tag}"

    def overflow(self, eng):
        eng.wait_ge(self.K.sig["overflow"], 1)
        return eng.value_load(self.M.over[0:1, 0:1], min_val=0, max_val=1)

    def load(self, sp, names, i, group):
        ST = self.ST
        for name in names:
            ST.may_load(sp, name, i)
            sp.dma_start(ST.raw(name).rearrange("p (k c) -> p k c", k=T if name[0] == "D" else KD),
                         self.source(name[0], group * E_G + int(name[1]))).then_inc(ST.arrived(name), 16)

    def hidden(self, pe, tag, e, bank, i):
        K, M, ST = self.K, self.M, self.ST
        name = f"{'GU'[bank]}{e}{tag}"
        w = [v[:, 0:CHUNK].rearrange("p (k c) -> p k c", k=KD) for v in ST.parts(pe, name, i)]
        for k in range(KD):
            last = mm3(pe, K.ps[e % 2][:, bank, 0:D_E], [v[:, k, :] for v in (M.xw_hi, M.xw_lo)],
                       [v[:, k, :] for v in w], k == 0, k == KD - 1)
        if bank:
            last.then_inc(self.L.filled(f"H{e}{tag}"), 1)
        else:
            ST.done(last, name)

    def hidden_all(self, pe, tag, e, i):
        self.L.claim(pe, f"H{e}{tag}", i, 4)
        self.hidden(pe, tag, e, 0, i)
        self.hidden(pe, tag, e, 1, i)

    def pe(self, pe, tag, i):
        K, M, L, ST = self.K, self.M, self.L, self.ST
        for e in range(E_G):
            more = e + 1 < E_G or tag == "a"
            if more:
                if e + 1 == E_G:
                    pe.wait_ge(K.sig["xw_hi"], later(2, i, 1))
                    pe.wait_ge(K.sig["xw_lo"], later(2, i, 1))
                L.claim(pe, f"H{e + 1}{tag}", i, 4)
                self.hidden(pe, tag, e + 1, 0, i)
            L.wait_drained(pe, self.lot_of(tag, e), i, 4)
            L.claim(pe, f"T{e}{tag}", i, 10)
            for f in range(2):
                last = pe.transpose(K.ps[3][:, 0, f * P:(f + 1) * P], M.act[:, 1, f * P:(f + 1) * P], K.ident[:, :])
            last.then_inc(L.filled(f"T{e}{tag}"), 1)
            if more:
                self.hidden(pe, tag, e + 1, 1, i)
            if e == 0:
                L.claim(pe, f"Y{tag}", i, 1)
            name = f"D{e}{tag}"
            w = [v[:, 0:CHUNK].rearrange("p (k c) -> p k c", k=T) for v in ST.parts(pe, name, i)]
            L.wait_drained(pe, f"T{e}{tag}", i, 10)
            for n in range(2):
                for f in range(2):
                    last = mm3(pe, K.ps[2][:, n, :], [v[:, f, :] for v in (M.h_hi, M.h_lo)],
                               [v[:, f, n * 512:(n + 1) * 512] for v in w], e == f == 0, e == E_G - 1 and f == 1)
            if e + 1 < E_G:
                ST.done(last, name)
            if tag != "b" and 1 <= e <= T:
                pe.wait_ge(K.sig["back"], later(1 + (tag == "z"), i, 1))
                self.give_back(pe, f"S{e - 1}{tag}", e - 1, i)
        last.then_inc(L.filled(f"Y{tag}"), 1)

    def give_back(self, pe, name, t, i):
        lot = self.L.claim(pe, name, i, WINDOW_TURN[2][self.L.use[name][0]])
        for n in range(2):
            last = pe.matmul(self.K.ps[lot][:, n, :], self.M.back[:, t * P:(t + 1) * P],
                             self.M.y[:, n * 512:(n + 1) * 512], start=True, stop=True)
        last.then_inc(self.L.filled(name), 1)

    def act(self, act, tag, i):
        K, M, L, ST = self.K, self.M, self.L, self.ST
        for e in range(E_G):
            ahead = e == 0 and tag != "b"
            more = (e + 1 < E_G or tag == "a") and not ahead
            if more:
                ST.split_hi(act, f"G{e + 1}{tag}", i)
            lot = L.wait_filled(act, self.lot_of(tag, e), i, 4)
            act.activation(M.act[:, 0, :], K.ps[lot][:, 0, 0:D_E], ACT.Silu).then_inc(K.sig["silu"], 1)
            if tag == "a" and e + 1 == E_G:
                act.activation(M.xw_hi[:, :, :], M.xg_hi[:, :, bass.ds(i * P + P, P)].bitcast(F32), ACT.Copy)\
                   .then_inc(K.sig["xw_hi"], 1)
            if more:
                ST.split_hi(act, f"U{e + 1}{tag}", i)
            ST.split_hi(act, f"D{e}{tag}", i)
            L.wait_filled(act, f"T{e}{tag}", i, 10)
            act.activation(flat(M.h_hi[:, :, :]), K.ps[3][:, 0, 0:D_E], ACT.Copy).then_inc(K.sig["h_hi"], 1)
        if tag == "a":
            ST.split_hi(act, "G1a", i + 1)
            ST.split_hi(act, "U1a", i + 1)
        L.wait_filled(act, f"Y{tag}", i, 1)
        act.activation(M.y[:, 0:512], K.ps[2][:, 0, :], ACT.Copy).then_inc(K.sig["y_half"], 1)

    def dve(self, dve, tag, i, first, n):
        K, M, L, ST = self.K, self.M, self.L, self.ST
        for e in range(E_G):
            ahead = e == 0 and tag != "b"
            more = (e + 1 < E_G or tag == "a") and not ahead
            if more:
                ST.split_lo(dve, f"G{e + 1}{tag}", i)
            dve.wait_ge(K.sig["silu"], later(n * E_G + e + 1, i, E_G))
            lot = L.use[self.lot_of(tag, e)][0]
            dve.scalar_tensor_tensor(M.act[:, 1, :], K.ps[lot][:, 1, 0:D_E], M.weight[:, bass.ds(first + e, 1)],
                                     M.act[:, 0, :], ALU.mult, ALU.mult).then_inc(K.drained[lot], 1)
            if tag == "a" and e + 1 == E_G:
                dve.tensor_copy(M.xw_lo[:, :, :], M.xg_lo[:, :, bass.ds(i * P + P, P)]).then_inc(K.sig["xw_lo"], 1)
            if tag != "b" and 2 <= e <= T + 1:
                dve.wait_ge(K.sig["pool_chain"], 4)
                self.add(dve, f"S{e - 2}{tag}", e - 2, i)
            if more:
                ST.split_lo(dve, f"U{e + 1}{tag}", i)
            ST.split_lo(dve, f"D{e}{tag}", i)
            dve.wait_ge(K.sig["h_hi"], later(n * E_G + e + 1, i, E_G))
            dve.tensor_tensor(flat(M.h_lo[:, :, :]), K.ps[3][:, 0, 0:D_E], flat(M.h_hi[:, :, :]).bitcast(F32),
                              ALU.subtract).then_inc(L.drained(f"T{e}{tag}"), 1)
        if tag == "a":
            ST.split_lo(dve, "G1a", i + 1)
            ST.split_lo(dve, "U1a", i + 1)
        dve.wait_ge(K.sig["y_half"], later(n + 1, i, 1))
        dve.tensor_copy(M.y[:, 512:D], K.ps[2][:, 1, :]).then_inc(L.drained(f"Y{tag}"), 1)

    def add(self, dve, name, t, i):
        lot = self.L.wait_filled(dve, name, i, WINDOW_TURN[2][self.L.use[name][0]])
        x = self.K.x[:, t, :]
        dve.tensor_tensor(x, flat(self.K.ps[lot][:, :, :]), x, ALU.add).then_inc(self.L.drained(name), 1)


def norm_dve(K, dve, link, tag, g, b):
    mean, var = moments(K, dve, link)
    inv = K.stat[:, 0:T].unsqueeze(2)
    dve.tensor_scalar(inv, var, LN_EPS, None, ALU.add).then_inc(K.sig[f"{tag}_var"], 1)
    dve.wait_ge(K.sig[f"{tag}_root"], 1)
    link(dve.reciprocal(K.stat[:, 0:T], K.stat[:, 2:4]))
    dve.wait_ge(K.sig[f"{tag}_gain"], 32)
    for h in range(2):
        c = slice(h * 512, (h + 1) * 512)
        for t in range(T):
            x = K.x[:, t, c]
            last = dve.scalar_tensor_tensor(x, x, mean[:, t, :], g[:, c], ALU.subtract, ALU.mult)
        link(last)
        for t in range(T):
            x = K.x[:, t, c]
            last = dve.scalar_tensor_tensor(x, x, K.stat[:, t:t + 1], b[:, c], ALU.mult, ALU.add)
        last.then_inc(K.sig[f"{tag}_normed"], 1)


def block_two(K, M, layer):
    nc, A, sig, st = K.nc, K.A, K.sig, K.stat
    names = TWO_CHUNKS + ["G0a", "U0a"] + window_chunks("a") + window_chunks("z") + \
        ["G0b", "U0b"] + window_chunks("b")
    order = [("xT0", 0), ("xT1", 1), ("iq", 2), ("ik", 3), ("dq", 0), ("dk", 1), ("sq", 2), ("iqT", 3), ("ikT", 0),
             ("sk", 1), ("I0", 2), ("I1", 3), ("I2", 2), ("I3", 3), ("dv", 0), ("sv", 1), ("g0", 2), ("g1", 3),
             ("dqT", 0), ("dkT", 1), ("sqT", 2), ("skT", 3), ("g2", 0), ("g3", 1)]
    order += Attention.lots("da", DIFF_H, then="sa") + Attention.lots("sa", DSA_H // 2, begun=True)
    order += [("bs0", 2), ("bs1", 0), ("yT", 1), ("bd0", 2), ("bd1", 3), ("mT0", 0), ("mT1", 1), ("wo0", 2),
              ("wo1", 3), ("pT", 0), ("nT0", 1), ("nT1", 2), ("rt", 3), ("pg0", 0), ("rank", 2), ("pg1", 1), ("pl0", 3), ("pl1", 2)]
    order += [("xg0", 0), ("xg1", 1), ("xg2", 2), ("xg3", 3), ("slotT", 3), ("weight", 0), ("H0a", 0)]
    order += window_lots("a") + window_lots("z") + [("S0f", 3), ("S1f", 2), ("more", 1), ("turned", 3), ("H0b", 0)]
    order += window_lots("b") + [("S0g", 3), ("S1g", 2)]
    L = Lots(order, K.filled, K.drained)
    ST = Stream(K, L, names, TWO_WIDTHS, TWO_ENDS | window_ends("a") | window_ends("z") | window_ends("b"),
                {"route": 2}, WINDOW_TURN, {"G1a": ["G0a"], "U1a": ["H0a"], "D0a": ["H0a", "xg2"]}, "G0a", M.fourth,
                by_pool=("bs0", "bs1", "bd0"))
    hT = (M.hT_hi, M.hT_lo)
    merged = M.tmp
    pair = lambda tile: lambda u, h: tile[h * HD:(h + 1) * HD, u, :]
    over_two = lambda m: m[:, :, :].unsqueeze(1).to_broadcast([P, 2, T, S])
    da = DiffAttention(K, L, "da", DIFF_H, q=pair(M.dqT), k=pair(M.dkT),
                       v=lambda u, h, c: M.pr[:, c, C_DV + u * P:C_DV + (u + 1) * P],
                       scale=HD ** -0.5, p=M.p, pt=M.pt, mask=over_two(M.causal), out=M.ya)
    sa = Attention(K, L, "sa", DSA_H // 2, q=pair(M.sqT), k=pair(M.skT),
                   v=lambda u, h, c: M.pr[:, c, C_SV + (2 * u + h) * HD:C_SV + (2 * u + h + 1) * HD],
                   scale=HD ** -0.5, p=M.p, pt=M.pt, mask=over_two(M.bias), out=(M.sT_hi, M.sT_lo))

    def source(name):
        w = A["w_in_2"][layer]
        kpc = lambda a: a.rearrange("(k p) c -> p k c", p=P)
        square = lambda w, c, k: kpc(w[k * 512:(k + 1) * 512, c * 512:(c + 1) * 512])
        if name == "ik":
            return kpc(w[:, C_IK:C_GA])
        if name[:2] in TWO_COLUMNS:
            c, k = TWO_COLUMNS[name[:2]], int(name[2])
            return kpc(w[k * 512:(k + 1) * 512, c:c + 512])
        if name[:2] == "wo":
            return square(A["w_out_2"][layer], int(name[2]), int(name[3]))
        if name[:2] == "pg":
            return square(A["w_ple_gate_2"][layer], int(name[2]), int(name[3]))
        if name == "wple":
            return kpc(A["w_ple_2"][layer])
        if name[0] == "b":
            b, c = {"s": "w_branch_dsa_2", "d": "w_branch_diff_2"}[name[1]], int(name[2])
            return kpc(A[b][layer][:, c * 512:(c + 1) * 512])
        c, k = C_GA + 512 * int(name[1]), "ab".index(name[2])
        return kpc(w[k * 512:(k + 1) * 512, c:c + 512])

    def expert_source(kind, e):
        w = {"G": "w_exp_gate_2", "U": "w_exp_up_2", "D": "w_exp_down_2"}[kind]
        return A[w][layer].rearrange("g e d f -> (g e) d f")[e].rearrange("(k p) c -> p k c", p=P)

    W = Windows(K, M, L, ST, expert_source)
    last_turn = N_G - 2

    with nc.Block() as block:

        @block.sync
        def _(sp):
            for name in TWO_CHUNKS:
                ST.may_load(sp, name)
                dst = ST.raw(name)[:, 0:ST.columns(name)]
                if name == "route":
                    dst = dst.rearrange("p (k c) -> p k c", k=KD)
                    for c0, c1, w in ((0, N_G, "w_route_group_2"), (N_G, N_ROUTE, "w_route_expert_2")):
                        sp.dma_start(dst[:, :, c0:c1], A[w][layer].rearrange("(k p) c -> p k c", p=P))\
                          .then_inc(ST.arrived(name), 16)
                else:
                    src = source(name)
                    sp.dma_start(dst.rearrange("p (k c) -> p k c", k=src.shape[1]), src)\
                      .then_inc(ST.arrived(name), 16)
                if name == "ik":
                    for dst, src in ((M.lam[:, 0:4 * HD], A["diff_lambda_2"][layer].rearrange("a d -> (a d)")),
                                     (M.lam[:, 4 * HD:4 * HD + 2], A["c_lam_init"][layer]),
                                     (M.sub[:, :], A["diff_subln_g_2"][layer]),
                                     (M.route_b[:, 0:N_G], A["b_route_group_2"][layer]),
                                     (M.route_b[:, N_G:N_ROUTE], A["b_route_expert_2"][layer])):
                        sp.dma_start(dst, src.partition_broadcast(P)).then_inc(sig["rows"], 16)
                if name == "bd1":
                    L.wait_filled(sp, "saO3")
                    for tile, src, s in ((M.ln_g, "ln1_g_2", "n1_gain"), (M.ln_b, "ln1_b_2", "n1_gain"),
                                         (M.ln2_g, "ln2_g_2", "n2_gain"), (M.ln2_b, "ln2_b_2", "n2_gain")):
                        sp.dma_start(tile[:, :], A[src][layer].partition_broadcast(P)).then_inc(sig[s], 16)
                    sp.dma_start(M.ple[:, :, :], A["p_2"][layer][0].rearrange("(t p) d -> p t d", p=P))\
                      .then_inc(sig["ple_rows"], 16)
            W.load(sp, ["G0a", "U0a"], None, 0)
            with sp.Fori(0, N_G - 1) as i:
                W.load(sp, window_chunks("a"), i, i)
            W.load(sp, window_chunks("z"), last_turn, N_G - 1)
            fifth = W.overflow(sp)
            group_of_fifth = sp.value_load(M.over[0:1, 1:2], min_val=0, max_val=N_G - 1)
            with sp.If(fifth > 0):
                W.load(sp, ["G0b", "U0b"] + window_chunks("b"), last_turn, group_of_fifth)

        @block.tensor
        def _(pe):
            def both(*names):
                for n in names:
                    L.wait_drained(pe, n)

            def group(name):
                project(K, L, ST, pe, name, (f"{name}0", f"{name}1"), 512, hT)

            def turn(name, src, pairs):
                lot = L.claim(pe, name)
                d = flat(K.ps[lot][:, :, :]).rearrange("p (k s) -> p k s", k=4)
                for k in range(pairs):
                    for t in range(T):
                        last = pe.transpose(d[:, k, t * P:(t + 1) * P], src[:, t, k * P:(k + 1) * P], K.ident[:, :])
                last.then_inc(L.filled(name), 1)

            transpose_x(K, L, pe, K.x, ("xT0", "xT1"))
            project(K, L, ST, pe, "iq", ("iq0", "iq1"), 512, hT, turned=("xT0", "xT1"))
            project(K, L, ST, pe, "ik", ("ik",), HD + IDX_H, hT, kn=KD)
            group("dq")
            group("dk")
            group("sq")
            pe.wait_ge(sig["index_ready"], 1)
            turn("iqT", M.pr[:, :, C_IQ:C_IK], 4)
            turn("ikT", M.ik2[:, :, :], 1)
            group("sk")
            both("iqT", "ikT")
            for u in range(4):
                lot = L.claim(pe, f"I{u}")
                s = flat(K.ps[lot][:, :, :]).rearrange("p (h t k) -> p h t k", h=2, t=T)
                for h in range(2):
                    for t in range(T):
                        n = (t + 1) * P
                        last = pe.matmul(s[:, h, t, 0:n], M.iqT[h * HD:(h + 1) * HD, u, t * P:(t + 1) * P],
                                         M.ikT[h * HD:(h + 1) * HD, 0:n], start=True, stop=True)
                last.then_inc(L.filled(f"I{u}"), 1)
            group("dv")
            group("sv")
            project(K, L, ST, pe, "g0", ("g0a", "g0b"), 512, hT)
            project(K, L, ST, pe, "g1", ("g1a", "g1b"), 512, hT)
            pe.wait_ge(sig["diff_ready"], 1)
            turn("dqT", M.pr[:, :, C_DQ:C_DK], 4)
            turn("dkT", M.pr[:, :, C_DK:C_DV], 4)
            pe.wait_ge(sig["sparse_ready"], 1)
            turn("sqT", M.pr[:, :, C_SQ:C_SK], 4)
            turn("skT", M.pr[:, :, C_SK:C_SV], 4)
            project(K, L, ST, pe, "g2", ("g2a", "g2b"), 512, hT)
            project(K, L, ST, pe, "g3", ("g3a", "g3b"), 512, hT)
            both("dqT", "dkT", "dv", "sqT", "skT", "sv")
            da.pe(pe, then=sa)
            sa.pe(pe, begun=("da", DIFF_H))

            def branch(name, xT):
                for c in range(2):
                    lot = L.claim(pe, f"{name}{c}")
                    token_product(K, ST, pe, lambda t: K.ps[lot][:, t, :], xT, f"{name}{c}", True, True, 0, 4, 512)\
                        .then_inc(L.filled(f"{name}{c}"), 1)

            both("saO3")
            branch("bs", (M.sT_hi, M.sT_lo))
            pe.wait_ge(sig["ya_normed"], 1)
            turn("yT", M.ya[:, :, :], 4)
            both("yT")
            branch("bd", (M.yT_hi, M.yT_lo))
            transpose_x(K, L, pe, merged, ("mT0", "mT1"), sig["merged"])
            for c in range(2):
                project(K, L, ST, pe, f"wo{c}", (f"wo{c}0", f"wo{c}1"), 512, hT,
                        turned=("mT0", "mT1") if c == 0 else ())
            pe.wait_ge(sig["ple_rows"], 16)
            turn("pT", M.ple[:, :, :], 2)
            transpose_x(K, L, pe, K.x, ("nT0", "nT1"), sig["n1_normed"])
            both("nT0", "nT1")
            project(K, L, ST, pe, "rt", ("route",), N_ROUTE, hT, kn=KD)
            project(K, L, ST, pe, "pg0", ("pg00", "pg01"), 512, hT)
            pe.wait_ge(sig["group_hot"], 1)
            lot = L.claim(pe, "rank")
            hot = M.r[:, 1, :, 0:N_G]
            tri, ones = M.tri[:, 0:P], M.tri[:, P:2 * P]
            out = K.ps[lot]
            pe.matmul(out[:, 0, 0:N_G], tri, hot[:, 0, :], start=True, stop=True)
            pe.matmul(out[:, 0, N_G:2 * N_G], ones, hot[:, 0, :], start=True, stop=False)
            pe.matmul(out[:, 0, N_G:2 * N_G], tri, hot[:, 1, :], start=False, stop=True)
            pe.matmul(out[:, 1, 0:N_G], ones, hot[:, 0, :], start=True, stop=False)
            pe.matmul(out[:, 1, 0:N_G], ones, hot[:, 1, :], start=False, stop=True).then_inc(L.filled("rank"), 1)
            project(K, L, ST, pe, "pg1", ("pg10", "pg11"), 512, hT)
            both("pT")
            for c in range(2):
                lot = L.claim(pe, f"pl{c}")
                token_product(K, ST, pe, lambda t: K.ps[lot][:, t, :], (M.pT_hi, M.pT_lo), "wple", True, True,
                              0, 2, D, c0=c * 512, cn=512).then_inc(L.filled(f"pl{c}"), 1)
            pe.wait_ge(sig["slots"], 1)
            pe.wait_ge(sig["x_lo"], 1)
            for j in range(KD // 2):
                lot = L.claim(pe, f"xg{j}")
                for kk in range(2):
                    k = 2 * j + kk
                    for t in range(T):
                        for x in (M.x_hi, M.x_lo):
                            last = pe.matmul(K.ps[lot][:, kk, :], x[:, t, k * P:(k + 1) * P],
                                             M.slot_r[:, t, 0:N_G * P], start=t == 0 and x is M.x_hi,
                                             stop=t == T - 1 and x is M.x_lo)
                last.then_inc(L.filled(f"xg{j}"), 1)
            lot = L.claim(pe, "slotT")
            for w in range(N_G):
                for t in range(T):
                    at = (w * T + t) * P
                    last = pe.transpose(flat(K.ps[lot][:, :, :])[:, at:at + P], M.slot[:, t, w * P:(w + 1) * P],
                                        K.ident[:, :])
            last.then_inc(L.filled("slotT"), 1)
            lot = L.claim(pe, "weight")
            for w in range(N_G):
                for t in range(T):
                    last = pe.matmul(K.ps[lot][:, 0, w * E_G:(w + 1) * E_G], M.slot[:, t, w * P:(w + 1) * P],
                                     M.r[:, 4, t, :], start=t == 0, stop=t == T - 1)
            last.then_inc(L.filled("weight"), 1)
            both("xg0", "xg1", "xg2", "xg3")
            pe.wait_ge(sig["y_start"], 1)
            pe.wait_ge(sig["xw_hi"], 1)
            pe.wait_ge(sig["xw_lo"], 1)
            W.hidden_all(pe, "a", 0, None)
            with pe.Fori(0, N_G - 1) as i:
                W.pe(pe, "a", i)
            W.pe(pe, "z", last_turn)
            L.wait_drained(pe, "Yz", last_turn, 1)
            pe.wait_ge(sig["back"], N_G + 1)
            for t in range(T):
                W.give_back(pe, f"S{t}f", t, last_turn)
            with pe.If(W.overflow(pe) > 0):
                lot = L.claim(pe, "more", last_turn, 4)
                for k in range(KD):
                    for t in range(T):
                        last = pe.matmul(flat(K.ps[lot][:, :, :])[:, k * P:(k + 1) * P],
                                         M.x_before[:, t, k * P:(k + 1) * P], M.slot[:, t, N_G * P:], start=t == 0,
                                         stop=t == T - 1)
                last.then_inc(L.filled("more"), 1)
                lot = L.claim(pe, "turned", last_turn, 10)
                for t in range(T):
                    pe.transpose(K.ps[lot][:, 0, t * P:(t + 1) * P], M.slot[:, t, N_G * P:], K.ident[:, :])
                for t in range(T):
                    last = pe.matmul(K.ps[lot][:, 1, 0:E_G], M.slot[:, t, N_G * P:], M.r[:, 4, t, :],
                                     start=t == 0, stop=t == T - 1)
                last.then_inc(L.filled("turned"), 1)
                L.wait_drained(pe, "turned", last_turn, 10)
                L.wait_drained(pe, "more", last_turn, 4)
                W.hidden_all(pe, "b", 0, last_turn)
                W.pe(pe, "b", last_turn)
                L.wait_drained(pe, "Yb", last_turn, 1)
                for t in range(T):
                    W.give_back(pe, f"S{t}g", t, last_turn)

        @block.scalar
        def _(act):
            def take(name, dst, part=None, func=ACT.Copy):
                lot = L.wait_filled(act, name)
                src = flat(K.ps[lot][:, :, :]) if part is None else part(K.ps[lot])
                act.activation(dst, src, func).then_inc(L.drained(name), 1)

            def whole(ps):
                return ps[:, :, :]

            def columns(name):
                ST.hi_to(act, f"{name}1", 2)
                c = TWO_COLUMNS[name]
                take(name, M.pr[:, :, c:c + 512], whole)

            def sigmoid(g):
                take(f"g{g}", M.gates[:, :, g * 512:(g + 1) * 512], whole, ACT.Sigmoid)

            act_hi(K, L, act, "xT0", flat(M.hT_hi[:, 0:4, :]))
            act_hi(K, L, act, "xT1", flat(M.hT_hi[:, 4:8, :]))
            ST.hi_to(act, "iq0", 2)
            columns("iq")
            ST.hi_to(act, "ik", 2)
            act.wait_ge(sig["lam_dots"], 1)
            act.activation(st[:, 122:124], st[:, 122:124], ACT.Exp).then_inc(sig["lam_exps"], 1)
            columns("dq")
            columns("dk")
            columns("sq")
            take("iqT", flat(M.iqT[:, :, :]))
            columns("sk")
            for u in range(4):
                if u >= 2:
                    act.wait_ge(sig["index_sums"], u - 1)
                lot = L.wait_filled(act, f"I{u}")
                s, p = (v.rearrange("p (h t k) -> p h t k", h=2, t=T) for v in (flat(K.ps[lot][:, :, :]), M.p[:, u % 2, :]))
                act.activation(p[:, :, 0, 0:P], s[:, :, 0, 0:P], ACT.Relu)
                act.activation(p[:, :, 1, :], s[:, :, 1, :], ACT.Relu).then_inc(L.drained(f"I{u}"), 1)
            columns("dv")
            columns("sv")
            for g in range(2):
                ST.hi_to(act, f"g{g}b", 2)
                sigmoid(g)
            take("dqT", flat(M.dqT[:, :, :]))
            take("sqT", flat(M.sqT[:, :, :]))
            ST.hi_to(act, "g2b", 2)
            sigmoid(2)
            ST.hi_to(act, "g3b", 2)
            sigmoid(3)
            da.act(act, then=sa)
            ST.hi_to(act, "g3b", 3)
            sa.act(act, begun=("da", DIFF_H))
            act.wait_ge(sig["ya_var"], 1)
            act.activation(st[:, 130:138], st[:, 130:138], ACT.Sqrt).then_inc(sig["ya_root"], 1)
            ST.hi_to(act, "bs1", 1)
            act_hi(K, L, act, "yT", flat(M.yT_hi[:, :, :]))
            ST.hi_to(act, "wo01")
            act_hi(K, L, act, "mT0", flat(M.hT_hi[:, 0:4, :]))
            act_hi(K, L, act, "mT1", flat(M.hT_hi[:, 4:8, :]))
            ST.hi_to(act, "wo11", 1)
            act_hi(K, L, act, "pT", flat(M.pT_hi[:, :, :]), lambda lot: K.ps[lot][:, 0, :])
            root_act(K, act, "n1")
            ST.hi_to(act, "wo11", 3)
            act_hi(K, L, act, "nT0", flat(M.hT_hi[:, 0:4, :]))
            act_hi(K, L, act, "nT1", flat(M.hT_hi[:, 4:8, :]))
            act.wait_ge(sig["n1_normed"], 2)
            act.activation(M.x_hi[:, :, :], K.x[:, :, :], ACT.Copy).then_inc(sig["x_hi"], 1)
            ST.hi_to(act, "route", 3)
            act.wait_ge(sig["group_shift"], 1)
            act.activation(M.r[:, 0, :, 0:N_G], M.r[:, 0, :, 0:N_G], ACT.Exp).then_inc(sig["group_exps"], 1)
            act.wait_ge(sig["expert_shift"], 1)
            act.activation(M.r[:, 3, :, :], M.r[:, 3, :, :], ACT.Exp).then_inc(sig["expert_exps"], 1)
            ST.hi_to(act, "pg01", 2)
            take("pg0", M.pgate[:, 0, :, :], whole, ACT.Sigmoid)
            ST.hi_to(act, "pg11", 1)
            take("pg1", M.pgate[:, 1, :, :], whole, ACT.Sigmoid)
            ST.hi_to(act, "G0a")
            for j in range(KD // 2):
                if j == 2:
                    ST.hi_to(act, "U0a")
                act_hi(K, L, act, f"xg{j}", flat(M.xg_hi[:, 2 * j:2 * j + 2, :]))
            take("slotT", M.slotT[:, :])
            act.activation(M.xw_hi[:, :, :], M.xg_hi[:, :, 0:P].bitcast(F32), ACT.Copy).then_inc(sig["xw_hi"], 1)
            ST.hi_to(act, "U1a")
            with act.Fori(0, N_G - 1) as i:
                W.act(act, "a", i)
            W.act(act, "z", last_turn)
            with act.If(W.overflow(act) > 0):
                lot = L.wait_filled(act, "more", last_turn, 4)
                act.activation(flat(M.xw_hi[:, :, :]), flat(K.ps[lot][:, :, :]), ACT.Copy).then_inc(sig["more_hi"], 1)
                lot = L.wait_filled(act, "turned", last_turn, 10)
                act.activation(M.back[:, :], K.ps[lot][:, 0, 0:S], ACT.Copy).then_inc(sig["turned_hi"], 1)
                ST.split_hi(act, "G0b", last_turn)
                ST.split_hi(act, "U0b", last_turn)
                W.act(act, "b", last_turn)
            root_act(K, act, "n2")

        @block.vector
        def _(dve):
            link = Chain(dve, sig["dve_chain"])

            def tt(out, a, b, op):
                return dve.tensor_tensor(out, a, b, op)

            def take(name, dst, part=None):
                lot = L.wait_filled(dve, name)
                dve.tensor_copy(dst, flat(K.ps[lot][:, :, :]) if part is None else part(K.ps[lot]))\
                   .then_inc(L.drained(name), 1)

            cos, sin = M.rot[:, :, 0:8], M.rot[:, :, 8:16]
            dve_lo(K, L, dve, "xT0", flat(M.hT_lo[:, 0:4, :]), flat(M.hT_hi[:, 0:4, :]))
            dve_lo(K, L, dve, "xT1", flat(M.hT_lo[:, 4:8, :]), flat(M.hT_hi[:, 4:8, :]))
            ST.lo_to(dve, "iq0", 2)
            ST.lo_to(dve, "iq1", 2)
            ST.lo_to(dve, "ik", 2)
            take("ik", M.pr[:, :, C_IK:C_GA], lambda ps: ps[:, :, 0:HD + IDX_H])
            dve.wait_ge(sig["rows"], 80)
            lam = M.lam[:, 0:4 * HD].rearrange("p (a b d) -> p a b d", a=2, b=2)
            prod = M.scratch[:, 0:2 * HD].rearrange("p (a d) -> p a d", a=2)
            link(tt(prod, lam[:, :, 0, :], lam[:, :, 1, :], ALU.mult))
            dve.tensor_reduce(st[:, 122:124], prod, AX_X, ALU.add).then_inc(sig["lam_dots"], 1)
            L.wait_drained(dve, "iq")
            L.wait_drained(dve, "ik")
            link(rotate(dve, link, heads(M.pr[:, :, C_IQ:C_IW], 9), ROT // 2, cos, sin, M.scratch[:, 128:], 9))
            for two in range(2):
                dve.tensor_copy(M.ik2[:, :, two * HD:(two + 1) * HD], M.pr[:, :, C_IK:C_IW])
            dve.tensor_scalar(M.wi[:, :, :], M.pr[:, :, C_IW:C_GA], IDX_H ** -0.5, None, ALU.mult)\
               .then_inc(sig["index_ready"], 1)
            ST.lo_to(dve, "dq1", 1)
            dve.wait_ge(sig["lam_exps"], 1)
            link(tt(st[:, 120:121], st[:, 123:124], st[:, 122:123], ALU.subtract))
            link(tt(st[:, 120:121], st[:, 120:121], M.lam[:, 4 * HD:4 * HD + 1], ALU.subtract))
            link(dve.tensor_scalar(M.sub[:, :], M.sub[:, :], M.lam[:, 4 * HD + 1:4 * HD + 2], None, ALU.mult))
            ST.lo_to(dve, "dk1", 2)
            L.wait_drained(dve, "dq")
            L.wait_drained(dve, "dk")
            rotate(dve, link, heads(M.pr[:, :, C_DQ:C_DV], 16), ROT // 2, cos, sin, M.scratch, 16)\
                .then_inc(sig["diff_ready"], 1)
            dve.wait_ge(sig["diff_ready"], 1)
            ST.lo_to(dve, "sq1", 2)
            take("ikT", M.ikT[:, :], lambda ps: ps[:, 0, 0:S])
            ST.lo_to(dve, "sk1", 2)
            L.wait_drained(dve, "sq")
            L.wait_drained(dve, "sk")
            rotate(dve, link, heads(M.pr[:, :, C_SQ:C_SV], 16), ROT // 2, cos, sin, M.scratch, 16)\
                .then_inc(sig["sparse_ready"], 1)
            dve.wait_ge(sig["index_ready"], 1)
            for u in range(4):
                L.wait_drained(dve, f"I{u}")
                p = M.p[:, u % 2, :].rearrange("p (h t k) -> p h t k", h=2, t=T)
                for h in range(2):
                    for t in range(T):
                        n = (t + 1) * P
                        w = M.wi[:, t, 2 * u + h:2 * u + h + 1]
                        if u == h == 0:
                            last = dve.tensor_scalar(M.score[:, t, 0:n], p[:, h, t, 0:n], w, None, ALU.mult)
                        else:
                            last = dve.scalar_tensor_tensor(M.score[:, t, 0:n], p[:, h, t, 0:n], w,
                                                            M.score[:, t, 0:n], ALU.mult, ALU.add)
                    if h == 0:
                        link(last)
                last.then_inc(sig["index_sums"], 1)
                dve.wait_ge(sig["index_sums"], u + 1)
            for t in range(T):
                n = (t + 1) * P
                last = dve.scalar_tensor_tensor(M.work[:, t, 0:n], M.score[:, t, 0:n], HD ** -0.5,
                                                M.causal[:, t, 0:n], ALU.mult, ALU.add)
            link(last)
            splits = {1: ("dv1", 2), 3: ("sv1", 1), 5: ("sv1", 2), 7: ("g0b", 2)}
            for r in range(TOPK // 8):
                for t in range(T):
                    last = dve.max(M.top8[:, t, :], M.work[:, t, 0:(t + 1) * P])
                link(last)
                for t in range(T):
                    w = M.work[:, t, 0:(t + 1) * P]
                    last = dve.match_replace(w, M.top8[:, t, :], w, PICKED)
                link(last)
                if r in splits:
                    ST.lo_to(dve, *splits[r])
            for t in range(T):
                n = (t + 1) * P
                last = dve.tensor_scalar(M.bias[:, t, 0:n], M.work[:, t, 0:n], -2e38, NEG, ALU.is_gt, ALU.mult)
            link(last)
            tt(M.bias[:, 0, 0:P], M.bias[:, 0, 0:P], M.causal[:, 0, 0:P], ALU.add)
            dve.tensor_copy(M.bias[:, 0, P:S], M.causal[:, 0, P:S])
            link(tt(M.bias[:, 1, :], M.bias[:, 1, :], M.causal[:, 1, :], ALU.add))
            ST.lo_to(dve, "g1b", 2)
            take("dkT", flat(M.dkT[:, :, :]))
            take("skT", flat(M.skT[:, :, :]))
            ST.lo_to(dve, "g2b", 2)
            ST.lo_to(dve, "g3b", 3)
            da.dve(dve, link, then=sa)
            sa.dve(dve, link, begun=("da", DIFF_H))
            for u in range(DIFF_H):
                L.wait_drained(dve, f"daO{u}")
            ya = heads(M.ya[:, :, :], DIFF_H)
            link(tt(M.scratch[:, :], flat(M.ya[:, :, :]), flat(M.ya[:, :, :]), ALU.mult))
            link(dve.tensor_reduce(st[:, 130:138], M.scratch[:, :].rearrange("p (n d) -> p n d", d=P), AX_X, ALU.add))
            dve.tensor_scalar(st[:, 130:138], st[:, 130:138], 1.0 / P, LN_EPS, ALU.mult, ALU.add)\
               .then_inc(sig["ya_var"], 1)
            dve.wait_ge(sig["ya_root"], 1)
            link(dve.reciprocal(st[:, 130:138], st[:, 130:138]))
            link(tt(ya, ya, over_heads(st[:, 130:138].rearrange("p (t h) -> p t h", t=T), DIFF_H, P), ALU.mult))
            tt(ya, ya, over_heads(M.sub[:, :], DIFF_H, P), ALU.mult).then_inc(sig["ya_normed"], 1)
            for g in range(4):
                L.wait_drained(dve, f"g{g}")
            for c in range(2):
                ST.lo_to(dve, f"bs{c}", 1)
                lot = L.wait_filled(dve, f"bs{c}")
                gate = M.gates[:, :, D + c * 512:D + (c + 1) * 512]
                ins = tt(merged[:, :, c * 512:(c + 1) * 512], K.ps[lot][:, :, :], gate, ALU.mult)
                ins.then_inc(L.drained(f"bs{c}"), 1)
            dve_lo(K, L, dve, "yT", flat(M.yT_lo[:, :, :]), flat(M.yT_hi[:, :, :]))
            for c in range(2):
                ST.lo_to(dve, f"bd{c}", 1)
                lot = L.wait_filled(dve, f"bd{c}")
                gate = M.gates[:, :, c * 512:(c + 1) * 512]
                tt(gate, K.ps[lot][:, :, :], gate, ALU.mult).then_inc(L.drained(f"bd{c}"), 1)
                L.wait_drained(dve, f"bd{c}")
                L.wait_drained(dve, f"bs{c}")
                tt(merged[:, :, c * 512:(c + 1) * 512], merged[:, :, c * 512:(c + 1) * 512], gate, ALU.add)\
                    .then_inc(sig["merged"], 1)
            ST.lo_to(dve, "wo01")
            dve_lo(K, L, dve, "mT0", flat(M.hT_lo[:, 0:4, :]), flat(M.hT_hi[:, 0:4, :]))
            dve_lo(K, L, dve, "mT1", flat(M.hT_lo[:, 4:8, :]), flat(M.hT_hi[:, 4:8, :]))
            ST.lo_to(dve, "wo11", 1)
            for c in range(2):
                lot = L.wait_filled(dve, f"wo{c}")
                x = K.x[:, :, c * 512:(c + 1) * 512]
                dve.scalar_tensor_tensor(x, x, ALPHA, K.ps[lot][:, :, :], ALU.mult, ALU.add)\
                   .then_inc(L.drained(f"wo{c}"), 1)
                L.wait_drained(dve, f"wo{c}")
                half_moments(K, dve, link, c)
            ST.lo_to(dve, "route")
            dve_lo(K, L, dve, "pT", flat(M.pT_lo[:, :, :]), flat(M.pT_hi[:, :, :]), lambda lot: K.ps[lot][:, 0, :])
            norm_dve(K, dve, link, "n1", M.ln_g, M.ln_b)
            dve_lo(K, L, dve, "nT0", flat(M.hT_lo[:, 0:4, :]), flat(M.hT_hi[:, 0:4, :]))
            dve_lo(K, L, dve, "nT1", flat(M.hT_lo[:, 4:8, :]), flat(M.hT_hi[:, 4:8, :]))
            ST.lo_to(dve, "pg01")
            lot = L.wait_filled(dve, "rt")
            tt(M.logit[:, :, :], K.ps[lot][:, :, 0:N_ROUTE],
               M.route_b[:, :].unsqueeze(1).to_broadcast([P, T, N_ROUTE]), ALU.add).then_inc(L.drained("rt"), 1)
            L.wait_drained(dve, "rt")

            def first_of(out, v, top, index, n, signal="dve_chain"):
                small = M.r[:, 7, :, 0:n]
                link(tt(small, v, top.to_broadcast([P, T, n]), ALU.is_equal))
                link(dve.scalar_tensor_tensor(small, small, -100.0, index.unsqueeze(1).to_broadcast([P, T, n]),
                                              ALU.mult, ALU.add))
                link(dve.tensor_reduce(st[:, 146:148], small, AX_X, ALU.min))
                last = tt(out, small, st[:, 146:148].unsqueeze(2).to_broadcast([P, T, n]), ALU.is_equal)
                if signal == "dve_chain":
                    link(last)
                else:
                    last.then_inc(sig[signal], 1)
                    dve.wait_ge(sig[signal], 1)

            def top_of(cols, v):
                link(dve.tensor_reduce(st[:, cols], v, AX_X, ALU.max))
                return st[:, cols].unsqueeze(2)

            small4 = M.r[:, 6, :, 0:N_G]
            g = M.logit[:, :, 0:N_G]
            hot = M.r[:, 1, :, 0:N_G]
            top = top_of(slice(140, 142), g)
            tt(M.r[:, 0, :, 0:N_G], g, top.to_broadcast([P, T, N_G]), ALU.subtract).then_inc(sig["group_shift"], 1)
            first_of(hot, g, top, M.iota[:, 0:N_G], N_G, "group_hot")
            e = M.logit[:, :, N_G:N_ROUTE].rearrange("p t (g e) -> p t g e", g=N_G)
            r32 = M.r32[:, :, :].rearrange("p t (g e) -> p t g e", g=N_G)
            link(tt(r32, e, hot.unsqueeze(3).to_broadcast([P, T, N_G, E_G]), ALU.mult))
            el, one, two, pe_ = M.r[:, 2, :, :], M.r[:, 4, :, :], M.r[:, 5, :, :], M.r[:, 3, :, :]
            link(dve.tensor_reduce(el, M.r32[:, :, :].rearrange("p t (g e) -> p t e g", g=N_G), AX_X, ALU.add))
            top = top_of(slice(142, 144), el)
            tt(pe_, el, top.to_broadcast([P, T, E_G]), ALU.subtract).then_inc(sig["expert_shift"], 1)
            first_of(one, el, top, M.iota[:, 4:12], E_G)
            link(dve.scalar_tensor_tensor(el, one, NEG, el, ALU.mult, ALU.add))
            top = top_of(slice(144, 146), el)
            first_of(two, el, top, M.iota[:, 4:12], E_G)
            link(tt(one, one, two, ALU.add))
            dve.wait_ge(sig["group_exps"], 1)
            link(dve.tensor_reduce(st[:, 148:150], M.r[:, 0, :, 0:N_G], AX_X, ALU.add))
            dve.wait_ge(sig["expert_exps"], 1)
            link(tt(one, one, pe_, ALU.mult))
            link(dve.tensor_reduce(st[:, 150:152], one, AX_X, ALU.add))
            link(tt(st[:, 148:150], st[:, 148:150], st[:, 150:152], ALU.mult))
            link(dve.reciprocal(st[:, 148:150], st[:, 148:150]))
            link(tt(one, one, st[:, 148:150].unsqueeze(2).to_broadcast([P, T, E_G]), ALU.mult))
            ST.lo_to(dve, "pg10")
            lot = L.wait_filled(dve, "rank")
            link(tt(small4, K.ps[lot][:, 0, 0:T * N_G].rearrange("p (t g) -> p t g", t=T), hot, ALU.mult))
            dve.tensor_scalar(M.over_f[:, 0:N_G], K.ps[lot][:, 1, 0:N_G], float(P), None, ALU.is_gt)\
                .then_inc(L.drained("rank"), 1)
            L.wait_drained(dve, "rank")
            link(dve.tensor_reduce(st[:, 160:162], small4, AX_X, ALU.add))
            link(dve.tensor_scalar(st[:, 162:164], st[:, 160:162], float(P), None, ALU.subtract))
            for t in range(T):
                for w in range(N_G):
                    dve.tensor_scalar(M.slot_r[:, t, w * P:(w + 1) * P], M.slots[:, :], st[:, 160 + t:161 + t],
                                      hot[:, t, w:w + 1], ALU.is_equal, ALU.mult)
                last = dve.tensor_scalar(M.slot_r[:, t, N_G * P:], M.slots[:, :], st[:, 162 + t:163 + t], None,
                                         ALU.is_equal)
            last.then_inc(sig["slots"], 1)
            ST.lo_to(dve, "pg11", 1)
            dve.wait_ge(sig["x_hi"], 1)
            tt(M.x_lo[:, :, :], K.x[:, :, :], M.x_hi[:, :, :].bitcast(F32), ALU.subtract).then_inc(sig["x_lo"], 1)
            link(tt(M.over_f[:, 4:8], M.over_f[:, 0:N_G], M.iota[:, 0:N_G], ALU.mult))
            link(dve.tensor_reduce(st[:, 164:166], M.over_f[:, :].rearrange("p (a g) -> p a g", a=2), AX_X, ALU.add))
            dve.tensor_copy(M.over[:, :], st[:, 164:166]).then_inc(sig["overflow"], 1)
            for c in range(2):
                lot = L.wait_filled(dve, f"pl{c}")
                L.wait_drained(dve, f"pg{c}")
                gate = M.pgate[:, c, :, :]
                tt(gate, gate, K.ps[lot][:, :, :], ALU.mult).then_inc(L.drained(f"pl{c}"), 1)
            ST.lo_to(dve, "G0a")
            for j in range(KD // 2):
                if j == 2:
                    ST.lo_to(dve, "U0a")
                dve_lo(K, L, dve, f"xg{j}", flat(M.xg_lo[:, 2 * j:2 * j + 2, :]), flat(M.xg_hi[:, 2 * j:2 * j + 2, :]))
            lot = L.wait_filled(dve, "weight")
            dve.tensor_copy(M.weight[:, :], K.ps[lot][:, 0, 0:N_E]).then_inc(L.drained("weight"), 1)
            L.wait_drained(dve, "weight")
            dve.tensor_copy(M.xw_lo[:, :, :], M.xg_lo[:, :, 0:P]).then_inc(sig["xw_lo"], 1)
            ST.lo_to(dve, "U1a")
            with dve.Fori(0, N_G - 1) as i:
                W.dve(dve, "a", i, i * E_G, 0)
            W.dve(dve, "z", last_turn, (N_G - 1) * E_G, 1)
            for t in range(T):
                W.add(dve, f"S{t}f", t, last_turn)
            with dve.If(W.overflow(dve) > 0):
                dve.wait_ge(sig["more_hi"], 1)
                lot = L.use["more"][0]
                dve.tensor_tensor(flat(M.xw_lo[:, :, :]), flat(K.ps[lot][:, :, :]),
                                  flat(M.xw_hi[:, :, :]).bitcast(F32), ALU.subtract).then_inc(L.drained("more"), 1)
                dve.wait_ge(sig["turned_hi"], 1)
                lot = L.use["turned"][0]
                dve.tensor_copy(M.weight[:, 0:E_G], K.ps[lot][:, 1, 0:E_G]).then_inc(L.drained("turned"), 1)
                L.wait_drained(dve, "turned", last_turn, 10)
                ST.split_lo(dve, "G0b", last_turn)
                ST.split_lo(dve, "U0b", last_turn)
                W.dve(dve, "b", last_turn, 0, 2)
                for t in range(T):
                    W.add(dve, f"S{t}g", t, last_turn)
                for t in range(T):
                    L.wait_drained(dve, f"S{t}g", last_turn, (10, 1)[t])
            for t in range(T):
                L.wait_drained(dve, f"S{t}f", last_turn, (10, 1)[t])
            half_moments(K, dve, link, 0)
            half_moments(K, dve, link, 1)
            norm_dve(K, dve, link, "n2", M.ln2_g, M.ln2_b)

        @block.gpsimd
        def _(pool):
            ST.lo_by_pool(pool)
            L.wait_filled(pool, "pg1")
            pool.tensor_copy(M.x_before[:, :, :], K.x[:, :, :]).then_inc(sig["pool_chain"], 1)
            pool.wait_ge(sig["pool_chain"], 1)
            for j in range(KD // 2):
                L.wait_filled(pool, f"xg{j}")
            pool.memset(M.y[:, :], 0.0).then_inc(sig["y_start"], 1)
            pool.memset(M.back[:, :], 0.0).then_inc(sig["back"], 1)
            for c in range(2):
                L.wait_drained(pool, f"pl{c}")
            pool.tensor_scalar(K.x[:, :, :], K.x[:, :, :], ALPHA, None, ALU.mult).then_inc(sig["pool_chain"], 1)
            pool.wait_ge(sig["pool_chain"], 2)
            for c in range(2):
                x = K.x[:, :, c * 512:(c + 1) * 512]
                pool.tensor_tensor(x, x, M.pgate[:, c, :, :], ALU.add).then_inc(sig["pool_chain"], 1)
            pool.wait_ge(sig["pool_chain"], 4)
            L.wait_drained(pool, "slotT")
            with pool.Fori(0, N_G - 1) as i:
                L.wait_filled(pool, "S1a", i, 10)
                pool.tensor_copy(M.back[:, :], M.slotT[:, bass.ds(i * S, S)]).then_inc(sig["back"], 1)
            L.wait_filled(pool, "S1z", last_turn, 10)
            pool.tensor_copy(M.back[:, :], M.slotT[:, (N_G - 1) * S:]).then_inc(sig["back"], 1)



INS = ["x", "attn_norm_g", "w_in", "mla_q_norm_g", "mla_w_uq", "mla_kv_norm_g", "mla_w_ukv", "mla_q_head_g",
       "mla_k_head_g", "gqa_q_head_g", "gqa_k_head_g", "pool_w", "pool_scale", "w_branch_mla", "w_branch_gqa",
       "w_branch_pool", "w_out", "ffn_norm_g", "ffn_w_up", "ffn_conv_w", "ffn_conv_b", "ffn_w_down", "p_2",
       "positions_2", "w_in_2", "diff_lambda_2", "diff_subln_g_2", "w_branch_diff_2", "w_branch_dsa_2", "w_out_2",
       "ln1_g_2", "ln1_b_2", "w_route_group_2", "b_route_group_2", "w_route_expert_2", "b_route_expert_2",
       "w_exp_gate_2", "w_exp_up_2", "w_exp_down_2", "w_ple_2", "w_ple_gate_2", "ln2_g_2", "ln2_b_2"]


def axial_tables(rot):
    row = np.repeat(np.arange(S // 64, dtype=np.float32), 64)
    col = np.tile(np.arange(64, dtype=np.float32), S // 64)
    n = rot // 4
    inv = (np.float32(10000.0) ** (-np.arange(n, dtype=np.float32) / np.float32(n))).astype(np.float32)
    ang = np.concatenate([row[:, None] * inv, col[:, None] * inv], axis=-1)
    return np.cos(ang).astype(np.float32), np.sin(ang).astype(np.float32)


def by_partition(a):
    return np.ascontiguousarray(a.reshape(T, P, -1).transpose(1, 0, 2))


def constants():
    rope = np.concatenate([*axial_tables(ROPE), *axial_tables(HD)], axis=-1)
    window = np.zeros((S, POOL_G, S), np.float32)
    for g, w in enumerate(POOL_WINDOWS):
        for t in range(S):
            lo, hi = max(t - w // 2, 0), min(t + w - w // 2, S)
            window[lo:hi, g, t] = np.float32(1) / np.float32(hi - lo)
            window[t, g, t] -= 1
    key, query = np.arange(S)[None, :], np.arange(S)[:, None]
    causal = np.where(key <= query, 0.0, NEG).astype(np.float32)
    inv = (1.0 / (np.float32(500000.0) ** (np.arange(0, ROT, 2, dtype=np.float32) / np.float32(ROT))))
    return {"c_rope": by_partition(rope), "c_window": by_partition(window.reshape(S, -1)).reshape(P, T, POOL_G * S),
            "c_ident": np.eye(P, dtype=np.float32), "c_causal": by_partition(causal),
            "c_inv_freq": inv.astype(np.float32)[None, :],
            "c_lam_init": np.array([[0.8 - 0.6 * np.exp(-0.3 * i), 0.2 + 0.6 * np.exp(-0.3 * i)]
                                    for i in range(DEPTH)], np.float32),
            "c_tri": np.concatenate([np.triu(np.ones((P, P), np.float32)), np.ones((P, P), np.float32)], axis=1),
            "c_slots": np.arange(1, P + 1, dtype=np.float32)[None, :],
            "c_groups": np.arange(N_G, dtype=np.float32)[None, :], "c_experts": np.arange(E_G, dtype=np.float32)[None, :]}


def build(nc, A, out):
    with ExitStack() as ctx:
        K = Core(nc, ctx, A)
        one = OneTiles(K)
        two = TwoTiles(K)
        with nc.Block() as block:

            @block.sync
            def _(sp):
                sp.dma_start(K.x[:, :, :], A["x"][0].rearrange("(t p) d -> p t d", p=P)).then_inc(K.sig["start"], 16)
                sp.dma_start(K.ident[:, :], A["c_ident"]).then_inc(K.sig["start"], 16)
                sp.dma_start(K.rope[:, :, :], A["c_rope"]).then_inc(K.sig["start"], 16)
                sp.wait_ge(K.sig["start"], 48)

        with nc.Fori(0, DEPTH) as layer:
            block_one(K, one, layer)
            nc.all_engine_barrier(sems_to_clear=K.sig.span())
        rotation_tables(K, two)
        nc.all_engine_barrier(sems_to_clear=K.sig.span())
        with nc.Fori(0, DEPTH) as layer:
            block_two(K, two, layer)
            nc.all_engine_barrier(sems_to_clear=K.sig.span())
        with nc.Block() as block:

            @block.sync
            def _(sp):
                sp.dma_start(out[0].rearrange("(t p) d -> p t d", p=P), K.x[:, :, :]).then_inc(K.sig["stored"], 16)
                sp.wait_ge(K.sig["stored"], 16)


def kernel(**inputs):
    import concourse.bacc as bacc
    from concourse.bass_utils import run_bass_kernel_spmd

    nc = bacc.Bacc("TRN2", target_bir_lowering=False, num_devices=1)
    arrays = {name: np.ascontiguousarray(inputs[name]) for name in INS} | constants()
    A = {name: nc.dram_tensor(name, a.shape, mybir.dt.from_np(a.dtype), kind="ExternalInput").ap()
         for name, a in arrays.items()}
    out = nc.dram_tensor("out", (1, S, D), F32, kind="ExternalOutput").ap()
    build(nc, A, out)
    r = run_bass_kernel_spmd(nc, [arrays], core_ids=[0])
    return r.results[0]["out"]
```
